# Optimizing a Trainium2 kernel written in Bass

```python
import math
import jax, jax.numpy as jnp
from jax import lax
import numpy as np

D_MODEL = 4096
BATCH = 1
SEQ = 256
DEPTH = 1

D_SSM = D_MODEL // 2
SSM_GROUP = 16
N_GROUPS = D_SSM // SSM_GROUP
STATE = 64
DT_MIN = 1e-3
DT_MAX = 1e-1
HEAD_DIM = 128
D_ATTN = D_MODEL // 2
N_HEADS = D_ATTN // (2 * HEAD_DIM)
Q_BLOCK = 128
SUBLN_EPS = 1e-5
N_BUCKETS = 32
MAX_DISTANCE = 128
EPS = 1e-6
N_IN = 2 * D_SSM + 4 * D_ATTN + 2 * D_MODEL
NEG_INF = -1e30

kernel_name = 'hybrid_s5_diffattn_adaln_block'

def rms_norm(x, g, eps):
    xf = x.astype(jnp.float32)
    return xf * lax.rsqrt(jnp.mean(xf * xf, axis=-1, keepdims=True) + eps) * g.astype(jnp.float32)

def _complex_affine_combine(e1, e2):
    a1r, a1i, b1r, b1i = e1
    a2r, a2i, b2r, b2i = e2
    ar = a2r * a1r - a2i * a1i
    ai = a2r * a1i + a2i * a1r
    br = a2r * b1r - a2i * b1i + b2r
    bi = a2r * b1i + a2i * b1r + b2i
    return (ar, ai, br, bi)

def s5_mixer(u, lam_re, lam_im, log_dt, b_re, b_im, c_re, c_im, d_skip, w_glu):
    bsz, seq, _ = u.shape
    uf = u.astype(jnp.float32).reshape(bsz, seq, N_GROUPS, SSM_GROUP)
    lr = lam_re.astype(jnp.float32)
    li = lam_im.astype(jnp.float32)
    dt = jnp.exp(log_dt.astype(jnp.float32))[:, None]
    mag = jnp.exp(lr * dt)
    ab_re = mag * jnp.cos(li * dt)
    ab_im = mag * jnp.sin(li * dt)
    den = lr * lr + li * li
    num_re = ab_re - 1.0
    coef_re = (num_re * lr + ab_im * li) / den
    coef_im = (ab_im * lr - num_re * li) / den
    br = b_re.astype(jnp.float32)
    bi = b_im.astype(jnp.float32)
    bb_re = coef_re[..., None] * br - coef_im[..., None] * bi
    bb_im = coef_re[..., None] * bi + coef_im[..., None] * br
    x_re = jnp.einsum('gpc,bsgc->bsgp', bb_re, uf)
    x_im = jnp.einsum('gpc,bsgc->bsgp', bb_im, uf)
    a_re = jnp.broadcast_to(ab_re, x_re.shape)
    a_im = jnp.broadcast_to(ab_im, x_im.shape)
    _, _, h_re, h_im = lax.associative_scan(_complex_affine_combine, (a_re, a_im, x_re, x_im), axis=1)
    y = (jnp.einsum('gcp,bsgp->bsgc', c_re.astype(jnp.float32), h_re)
         - jnp.einsum('gcp,bsgp->bsgc', c_im.astype(jnp.float32), h_im)
         + d_skip.astype(jnp.float32) * uf)
    y = y.reshape(bsz, seq, D_SSM)
    g = jax.nn.gelu(y)
    return g * jax.nn.sigmoid(g @ w_glu.astype(jnp.float32))

def t5_bucket(rel):
    n = jnp.maximum(rel, 0)
    max_exact = N_BUCKETS // 2
    nf = jnp.maximum(n, 1).astype(jnp.float32)
    large = max_exact + (jnp.log(nf / max_exact) / math.log(MAX_DISTANCE / max_exact)
                         * (N_BUCKETS - max_exact)).astype(jnp.int32)
    large = jnp.minimum(large, N_BUCKETS - 1)
    return jnp.where(n < max_exact, n, large)

def diff_attention(q, k, v, rel_bias, lam, lam_init, subln_g):
    bsz, seq = q.shape[0], q.shape[1]
    q = q.astype(jnp.float32) * (HEAD_DIM ** -0.5)
    k = k.astype(jnp.float32)
    v = v.astype(jnp.float32)
    table = rel_bias.astype(jnp.float32)
    k_pos = jnp.arange(seq)

    def block(i):
        start = i * Q_BLOCK
        qb = lax.dynamic_slice_in_dim(q, start, Q_BLOCK, axis=1)
        s = jnp.einsum('bqhmd,bkhmd->bhmqk', qb, k)
        rel = (start + jnp.arange(Q_BLOCK))[:, None] - k_pos[None, :]
        bias = jnp.transpose(table[t5_bucket(rel)], (2, 0, 1))
        s = jnp.where(rel[None, None, None] >= 0, s + bias[None, :, None], NEG_INF)
        p = jax.nn.softmax(s, axis=-1)
        attn = p[:, :, 0] - lam * p[:, :, 1]
        return jnp.einsum('bhqk,bkhd->bqhd', attn, v)

    o = lax.map(block, jnp.arange(seq // Q_BLOCK))
    o = jnp.moveaxis(o, 0, 1).reshape(bsz, seq, N_HEADS, 2 * HEAD_DIM)
    o = rms_norm(o, subln_g, SUBLN_EPS) * (1.0 - lam_init)
    return o.reshape(bsz, seq, D_ATTN)

def setup_inputs(seed: int = 0) -> dict:
    key = jax.random.key(seed)
    ks = jax.random.split(key, 32)
    f32 = jnp.float32

    def nrm(k, shape, scale):
        return jax.random.normal(k, shape, f32) * scale

    L = DEPTH
    lam_re = -0.5 + nrm(ks[6], (L, N_GROUPS, STATE), 0.01)
    lam_im = (math.pi * jnp.arange(STATE, dtype=f32))[None, None, :] + nrm(ks[7], (L, N_GROUPS, STATE), 0.01)
    log_dt = jax.random.uniform(ks[8], (L, N_GROUPS), f32, math.log(DT_MIN), math.log(DT_MAX))
    return {
        'x': nrm(ks[0], (BATCH, SEQ, D_MODEL), 1.0),
        'c': nrm(ks[1], (BATCH, D_MODEL), 1.0),
        'norm_g': 1.0 + nrm(ks[2], (L, D_MODEL), 0.02),
        'w_ada': nrm(ks[3], (L, D_MODEL, 3 * D_MODEL), 0.5 * D_MODEL ** -0.5),
        'b_ada': nrm(ks[4], (L, 3 * D_MODEL), 0.02),
        'w_in': nrm(ks[5], (L, D_MODEL, N_IN), D_MODEL ** -0.5),
        'ssm_lambda_re': lam_re,
        'ssm_lambda_im': lam_im,
        'ssm_log_dt': log_dt,
        'ssm_b_re': nrm(ks[9], (L, N_GROUPS, STATE, SSM_GROUP), (0.5 / SSM_GROUP) ** 0.5),
        'ssm_b_im': nrm(ks[10], (L, N_GROUPS, STATE, SSM_GROUP), (0.5 / SSM_GROUP) ** 0.5),
        'ssm_c_re': nrm(ks[11], (L, N_GROUPS, SSM_GROUP, STATE), (0.5 / STATE) ** 0.5),
        'ssm_c_im': nrm(ks[12], (L, N_GROUPS, SSM_GROUP, STATE), (0.5 / STATE) ** 0.5),
        'ssm_d': nrm(ks[13], (L, N_GROUPS, SSM_GROUP), 1.0),
        'w_glu': nrm(ks[14], (L, D_SSM, D_SSM), D_SSM ** -0.5),
        'lambda_q1': nrm(ks[15], (L, HEAD_DIM), 0.1),
        'lambda_k1': nrm(ks[16], (L, HEAD_DIM), 0.1),
        'lambda_q2': nrm(ks[17], (L, HEAD_DIM), 0.1),
        'lambda_k2': nrm(ks[18], (L, HEAD_DIM), 0.1),
        'subln_g': 1.0 + nrm(ks[19], (L, 2 * HEAD_DIM), 0.02),
        'w_out_ssm': nrm(ks[20], (L, D_SSM, D_MODEL), D_SSM ** -0.5),
        'w_out_attn': nrm(ks[21], (L, D_ATTN, D_MODEL), D_ATTN ** -0.5),
        'w_o': nrm(ks[22], (L, D_MODEL, D_MODEL), D_MODEL ** -0.5),
        'rel_bias': nrm(ks[23], (N_BUCKETS, N_HEADS), 0.5),
        'final_g': 1.0 + nrm(ks[24], (D_MODEL,), 0.02),
    }

def reference(x, c, norm_g, w_ada, b_ada, w_in, ssm_lambda_re, ssm_lambda_im, ssm_log_dt,
              ssm_b_re, ssm_b_im, ssm_c_re, ssm_c_im, ssm_d, w_glu,
              lambda_q1, lambda_k1, lambda_q2, lambda_k2, subln_g,
              w_out_ssm, w_out_attn, w_o, rel_bias, final_g):
    out_dtype = x.dtype
    bsz, seq, _ = x.shape
    widths = [D_SSM, D_SSM, D_ATTN, D_ATTN, D_ATTN, D_ATTN, D_MODEL, D_MODEL]
    offsets = [sum(widths[:i + 1]) for i in range(len(widths) - 1)]
    c_act = jax.nn.silu(c.astype(jnp.float32))
    h_res = x.astype(jnp.float32)
    for l in range(DEPTH):
        mod = c_act @ w_ada[l].astype(jnp.float32) + b_ada[l].astype(jnp.float32)
        shift, scale, gate = jnp.split(mod[:, None, :], 3, axis=-1)
        h = rms_norm(h_res, norm_g[l], EPS) * (1.0 + scale) + shift
        proj = h @ w_in[l].astype(jnp.float32)
        u_s, z_s, q, k, v, z_a, g_s, g_a = jnp.split(proj, offsets, axis=-1)
        y_s = s5_mixer(u_s, ssm_lambda_re[l], ssm_lambda_im[l], ssm_log_dt[l], ssm_b_re[l], ssm_b_im[l],
                       ssm_c_re[l], ssm_c_im[l], ssm_d[l], w_glu[l]) * jax.nn.silu(z_s)
        p_s = y_s @ w_out_ssm[l].astype(jnp.float32)
        lam_init = 0.8 - 0.6 * math.exp(-0.3 * l)
        lam = (jnp.exp(jnp.sum(lambda_q1[l].astype(jnp.float32) * lambda_k1[l].astype(jnp.float32)))
               - jnp.exp(jnp.sum(lambda_q2[l].astype(jnp.float32) * lambda_k2[l].astype(jnp.float32)))
               + lam_init)
        qh = q.reshape(bsz, seq, N_HEADS, 2, HEAD_DIM)
        kh = k.reshape(bsz, seq, N_HEADS, 2, HEAD_DIM)
        vh = v.reshape(bsz, seq, N_HEADS, 2 * HEAD_DIM)
        y_a = diff_attention(qh, kh, vh, rel_bias, lam, lam_init, subln_g[l]) * jax.nn.silu(z_a)
        p_a = y_a @ w_out_attn[l].astype(jnp.float32)
        merged = jax.nn.sigmoid(g_s) * p_s + jax.nn.sigmoid(g_a) * p_a
        h_res = h_res + gate * (merged @ w_o[l].astype(jnp.float32))
    return rms_norm(h_res, final_g, EPS).astype(out_dtype)


_drawn_inputs = setup_inputs


def setup_inputs(seed=0):
    import zlib

    import numpy as np

    out = dict(_drawn_inputs(seed))
    spreads = {}
    factors = {'norm_g': 8.0,
     'b_ada': 6.498,
     'ssm_lambda_re': 64.0,
     'ssm_lambda_im': 64.0,
     'ssm_log_dt': 64.0,
     'ssm_b_re': 64.0,
     'ssm_b_im': 64.0,
     'ssm_c_re': 64.0,
     'ssm_c_im': 64.0,
     'w_glu': 3.971,
     'lambda_q1': 8.0,
     'lambda_k1': 8.0,
     'lambda_q2': 64.0,
     'lambda_k2': 58.596,
     'subln_g': 27.837,
     'final_g': 8.23}
    for name, (base, spread) in spreads.items():
        noise = np.random.default_rng([zlib.crc32(name.encode()), seed]).standard_normal(out[name].shape)
        drawn = base * np.exp(spread * noise) if base else spread * noise
        out[name] = __import__('jax').numpy.asarray(drawn.astype(out[name].dtype))
    for name, factor in factors.items():
        out[name] = (out[name] * factor).astype(out[name].dtype)
    return out
```

```python
from contextlib import ExitStack
import math

import concourse.bass as bass
from concourse import mybir

F32 = mybir.dt.float32
F32R = mybir.dt.float32r
ALU = mybir.AluOpType
ACT = mybir.ActivationFunctionType
AX = mybir.AxisListType

P = 128
TOK = 256
NH = TOK // P
D = 4096
KT = D // P
CB = 512
UT = 4
UPB = KT // UT
RING = 4
NIN = 20480
G, ST, GC = 128, 64, 16
HEADS, HD = 8, 128
BLK_A, BLK_B, BLK_C = 4, 20, 16
SHIFT_SCALE = 2 * D
ADA_CB = 1024
ADA_UNITS = D // (2 * P)
NADA = SHIFT_SCALE // ADA_CB
R0 = NADA * ADA_UNITS
W_C = UPB * (BLK_A + BLK_B)
W_D = W_C + UPB * BLK_C
W_E = W_D + 4 * UT
W_F = W_E + 8 * UPB
ADA_C = (D // ADA_CB) * ADA_UNITS
ROUND = 1.5 * 2.0 ** 23
ROUND16 = 192.0
PI = math.pi
CW1 = 6.28125
CW2 = 0.0019340515136718750
CW3 = 2 * PI - CW1 - CW2
BELOW_PI = 3.1415925
NEG = -1e30
LAM_INIT = 0.8 - 0.6 * math.exp(-0.3 * 0)


def build(nc, x, c_col, g_col, w_ada, bada_col, bada_gate, w_in, lam_re, lam_im, log_dt,
          b_re, b_im, c_map, d_col, w_glu, lambdas, subln_g, w_oss, w_oat, w_o, rel_bias,
          final_g, onehot, ident_in, tvals, gmask_in, out):
    ctx = ExitStack()
    with ctx:
        def sb(name, shape, dt=F32):
            return ctx.enter_context(nc.sbuf_tensor(name, shape, dt))

        def sem(name):
            return ctx.enter_context(nc.semaphore(name))

        raw = sb("raw", [P, RING, UT, CB])
        w_hi = sb("w_hi", [P, 2, UT, CB], F32R)
        w_lo = sb("w_lo", [P, 2, UT, CB], F32R)
        a_hi = sb("a_hi", [P, KT, TOK], F32R)
        a_lo = sb("a_lo", [P, KT, TOK], F32R)
        feat = sb("feat", [P, KT, TOK])
        stage = sb("stage", [P, 2, NH, CB])
        work = sb("work", [P, 9216])
        ident = sb("ident", [P, P])
        ones = sb("ones", [P, 8])
        tv = sb("tv", [P, TOK])
        gmask = sb("gmask", [P, 8])
        rot = sb("rot", [P, 3, G])
        sgn = sb("sgn", [P, 2])
        dcol = sb("dcol", [P, 16])
        sc_col = sb("sc_col", [P, KT])
        sh_col = sb("sh_col", [P, KT])
        cact = sb("cact", [P, KT])
        small = sb("small", [P, 64])
        bank = [ctx.enter_context(nc.psum_tensor(f"bank{i}", [P, CB], F32)) for i in range(8)]

        def carve(base, off, shape):
            n = 1
            for s in shape:
                n *= s
            ap = base[:, off:off + n]
            if len(shape) == 1:
                return ap
            names = "abcd"[:len(shape)]
            return ap.rearrange(f"p ({' '.join(names)}) -> p {' '.join(names)}",
                                **{k: v for k, v in zip(names, shape)})

        def wk(off, *shape):
            return carve(work, off, shape)

        featf = feat[:, :, :].rearrange("p k t -> p (k t)")
        xs = carve(featf, 0, (NH, D))
        bb = wk(0, 2, 16, ST)
        adacc = wk(2048, 2, ADA_CB)
        hf = wk(4096, 2, UT, TOK)
        coef_l = wk(6144, 2, 16, ST)
        b_ld = carve(stage[:, :, :, :].rearrange("p b h c -> p (b h c)"), 0, (2, 16, ST))
        npar = wk(8192, 1024)
        PH, LO = wk(2048, 2, 2, TOK), wk(3072, 2, 2, TOK)
        FR = wk(4096, 2, 2, TOK)
        FA = wk(5120, 2, TOK)
        T1, T2, HH = wk(5632, 2, TOK), wk(6144, 2, TOK), wk(6656, 2, TOK)
        bd = wk(7168, 2, 2, 3, ST)
        cst = wk(7936, 4, 2, 2, 32)
        gl = wk(8448, 3, TOK)
        cosb = carve(featf, 4096, (2, 2, TOK))
        sinb = carve(featf, 5120, (2, 2, TOK))
        hcb = carve(featf, 6144, (2, 2, TOK))
        hsb = carve(featf, 7168, (2, 2, TOK))
        gacc = wk(0, ADA_CB)
        q_in, k_in, v_in, za_in, bias_in = (wk(1024 + 512 * i, NH, TOK) for i in range(5))
        qT, kT = wk(3584, 2, TOK), wk(4096, 2, TOK)
        sc = wk(4608, 2, 2, TOK)
        at = wk(5632, 2, TOK)
        aT = wk(6144, 2, TOK)
        ya = wk(6656, 2, TOK)
        szA = wk(7168, 2, TOK)
        subg = wk(7680, TOK)
        grow = wk(7936, ADA_CB)
        ysT = wk(0, 16, TOK)
        zs, sz, sig, ys = (wk(4096 + 1024 * i, NH, CB) for i in range(4))
        ga, gs, part, mrg = (wk(4096 + 1024 * i, NH, CB) for i in range(4))
        obuf = carve(featf, 0, (NH, D))
        xb = wk(0, 2, NH, CB)
        gate_b = wk(2048, 2, CB)
        fg = wk(3072, D)
        junk = wk(7168, NH, CB)

        proj_d = nc.dram_tensor("proj_scratch", (TOK, NIN), F32, kind="Internal").ap()
        coef_d = nc.dram_tensor("coef_scratch", (2, G, ST), F32, kind="Internal").ap()
        dist_d = nc.dram_tensor("dist_scratch", (HEADS, 512), F32, kind="Internal").ap()
        skew_d = nc.dram_tensor("skew_scratch", (HEADS, P * 513), F32, kind="Internal").ap()
        gate_d = nc.dram_tensor("gate_scratch", (1, D), F32, kind="Internal").ap()

        raw_full = [sem(f"raw_full{i}") for i in range(RING)]
        raw_used = sem("raw_used")
        h_done = sem("h_done")
        pe_used = sem("pe_used")
        stat_ready = sem("stat_ready")
        acc_free_a = sem("acc_free_a")
        acc_free_v = sem("acc_free_v")
        cons_in, x_in, misc_in = sem("cons_in"), sem("x_in"), sem("misc_in")
        act_misc = sem("act_misc")
        dve_misc = sem("dve_misc")
        pe_misc = sem("pe_misc")
        coef_io, dist_io, bias_io = sem("coef_io"), sem("dist_io"), sem("bias_io")
        bb_ready = sem("bb_ready")
        acc_ready = sem("acc_ready")
        ada_mm = sem("ada_mm")
        xt_pe = sem("xt_pe")
        hf_ready = sem("hf_ready")
        staged = sem("staged")
        stored = sem("stored")
        ut_pe, ut_done = sem("ut_pe"), sem("ut_done")
        frac_ready = sem("frac_ready")
        trig_ready = sem("trig_ready")
        prod_ready = sem("prod_ready")
        bd_ready = sem("bd_ready")
        c_in = sem("c_in")
        cst_ready = sem("cst_ready")
        x_pe = sem("x_pe")
        x_used = sem("x_used")
        hcs_ready = sem("hcs_ready")
        y_pe = sem("y_pe")
        y_used = sem("y_used")
        tanh_in, tanh_out = sem("tanh_in"), sem("tanh_out")
        gelu_done = sem("gelu_done")
        qk_in, va_in, ba_in, za_in_s = sem("qk_in"), sem("va_in"), sem("ba_in"), sem("za_in_s")
        qk_pe, qk_sb, s_pe, s_max, p_exp = (sem(n) for n in ("qk_pe", "qk_sb", "s_pe", "s_max", "p_exp"))
        at_sb, at_pe, at_t, o_pe, o_ssq, ya_sb, ya_pe, yaT_sb = (
            sem(n) for n in ("at_sb", "at_pe", "at_t", "o_pe", "o_ssq", "ya_sb", "ya_pe", "yaT_sb"))
        gacc_ready, gate_pe, gate_row, gate_st = (
            sem(n) for n in ("gacc_ready", "gate_pe", "gate_row", "gate_st"))
        bg_in = sem("bg_in")
        zs_in, gt_pe, sig_done, ys_sb, ys_pe, feat_sb = (
            sem(n) for n in ("zs_in", "gt_pe", "sig_done", "ys_sb", "ys_pe", "feat_sb"))
        ga_in, gs_in, ga_sig, gs_sig, ga_used, m_sb, m_pe = (
            sem(n) for n in ("ga_in", "gs_in", "ga_sig", "gs_sig", "ga_used", "m_sb", "m_pe"))
        xg_in = [sem("xg_in0"), sem("xg_in1")]
        fg_in, o_sb, o_sq, f_rms, f_rstd, f_out, out_st = (
            sem(n) for n in ("fg_in", "o_sb", "o_sq", "f_rms", "f_rstd", "f_out", "out_st"))

        w_in_v = w_in.rearrange("(u t p) (b c) -> b u p t c", t=UT, p=P, c=CB)
        w_glu_v = w_glu.rearrange("(u t p) (b c) -> b u p t c", t=UT, p=P, c=CB)
        w_oss_v = w_oss.rearrange("(u t p) (b c) -> b u p t c", t=UT, p=P, c=CB)
        w_oat_v = w_oat.rearrange("(u t p) (b c) -> b u p t c", t=UT, p=P, c=CB)
        w_o_v = w_o.rearrange("(u t p) (b c) -> b u p t c", t=UT, p=P, c=CB)
        ada_v = w_ada.rearrange("(u t p) (b c) -> b u p t c", t=2, p=P, c=ADA_CB)
        proj_v = proj_d.rearrange("(h p) (b c) -> b p h c", p=P, c=CB)
        proj_h = proj_d.rearrange("(h p) (b c) -> b p h c", p=P, c=TOK)
        x_v = x.rearrange("(h p) (b c) -> b p h c", p=P, c=CB)
        out_v = out.rearrange("(h p) (b c) -> b p h c", p=P, c=CB)

        def rows(v, n):
            return bass.AP(v.tensor, 0, [[0, P], [1, n]])

        def at_block(v, b):
            if isinstance(b, int):
                return v[b]
            return v[bass.ds(b, 1)].rearrange("o p h c -> (o p) h c")

        def at_unit(v, b, u):
            if isinstance(b, int) and isinstance(u, int):
                return v[b, u]
            if isinstance(u, int):
                return v[bass.ds(b, 1), u].rearrange("o p t c -> (o p) t c")
            return v[bass.ds(b, 1), bass.ds(u, 1)].rearrange("o q p t c -> (o q p) t c")

        raw_ada = raw[:, :, :, :].rearrange("p r t c -> p r (t c)").rearrange("p r (t c) -> p r t c", c=ADA_CB)

        def ring_of(w):
            return R0 + w if w < W_C else (R0 + w + ADA_C if w >= W_D else None)

        block = ctx.enter_context(nc.Block())

        @block.sync
        def _(sp):
            sp.dma_start(ident[:, :], ident_in).then_inc(cons_in, 16)
            sp.dma_start(cact[:, :], c_col).then_inc(cons_in, 16)
            sp.dma_start(npar[:, 0:64], lam_re).then_inc(cons_in, 16)
            sp.dma_start(npar[:, 64:128], lam_im).then_inc(cons_in, 16)
            sp.dma_start(small[:, 0:1], log_dt).then_inc(cons_in, 16)

            def load(r, slot, dst, src):
                if not (isinstance(r, int) and r < RING):
                    sp.wait_ge(raw_used, r - RING + 1)
                sp.dma_start(dst, src).then_inc(raw_full[slot], 16)

            def load_unit(r, slot, src):
                load(r, slot, raw[:, slot, :, :], src)

            def load_ada(r, slot, src):
                load(r, slot, raw_ada[:, slot, :, :], src)

            for u in range(ADA_UNITS):
                load_ada(u, u % RING, ada_v[0, u])
                if u == RING - 1:
                    for h in range(NH):
                        sp.dma_start(xs[:, h, :], x[h * P:(h + 1) * P, :]).then_inc(x_in, 16)
            with sp.Fori(1, NADA) as cb:
                for u in range(ADA_UNITS):
                    load_ada(cb * ADA_UNITS + u, u % RING, at_unit(ada_v, cb, u))
            with sp.Fori(0, BLK_A + BLK_B) as b:
                for u in range(UPB):
                    load_unit(b * UPB + (R0 + u), u % RING, at_unit(w_in_v, b, u))
            with sp.Fori(0, HEADS // 2) as cb:
                for rr in range(2):
                    for v in range(2 * UPB):
                        loc = 24 * rr + v + v // 2
                        load_unit(cb * 48 + (R0 + W_C + loc), loc % RING,
                                  at_unit(w_in_v, cb * 4 + (BLK_A + BLK_B + 2 * rr + v // UPB), v % UPB))
                        if v % 2:
                            load_ada(cb * 48 + (R0 + W_C + loc + 1), (loc + 1) % RING,
                                     at_unit(ada_v, cb + NADA, 8 * rr + v // 2))
            for w in range(W_D, W_E):
                r = ring_of(w)
                load_unit(r, r % RING, w_glu_v[(w - W_D) // UT, (w - W_D) % UT])
            with sp.Fori(0, 8) as j:
                for u in range(UPB):
                    v = w_oat_v if u < UT else w_oss_v
                    load_unit(j * UPB + (ring_of(W_E) + u), u % RING, at_unit(v, j, u % UT))
            with sp.Fori(0, 8) as j:
                for u in range(UPB):
                    load_unit(j * UPB + (ring_of(W_F) + u), u % RING, at_unit(w_o_v, j, u))
            sp.wait_ge(out_st, 16 * 8)

        @block.gpsimd
        def _(pool):
            pool.dma_start(tv[:, :], rows(tvals, TOK)).then_inc(misc_in, 16)
            pool.dma_start(gmask[:, :], gmask_in).then_inc(misc_in, 16)
            pool.dma_start(dcol[:, :], d_col).then_inc(misc_in, 16)
            pool.dma_start(sc_col[:, :], g_col).then_inc(misc_in, 16)
            pool.dma_start(small[:, 8:40], bada_col[:, 0:32]).then_inc(misc_in, 16)
            pool.dma_start(sh_col[:, :], bada_col[:, 32:64]).then_inc(misc_in, 16)
            pool.dma_start(npar[:, 512:1024].rearrange("p (a d) -> p a d", a=4),
                           rows(lambdas, 4 * HD).rearrange("p (a d) -> p a d", a=4)).then_inc(misc_in, 16)
            for k, src in enumerate((b_re, b_im)):
                pool.dma_start(b_ld[:, k, :, :], src).then_inc(misc_in, 16)
            pool.dma_start(hf[0:32, 0, 0:1, :].rearrange("p a t -> p (a t)"), onehot).then_inc(misc_in, 16)
            pool.dma_start(hf[0:32, 1, 0, 0:HEADS], rel_bias).then_inc(misc_in, 16)

            pool.wait_ge(dve_misc, 4)
            for k in range(2):
                pool.dma_start(coef_d[k], coef_l[:, 0, 6 + k, :]).then_inc(coef_io, 16)
            pool.wait_ge(coef_io, 32)
            pool.wait_ge(pe_misc, 1)
            for k in range(2):
                for e in range(8):
                    pool.dma_start(coef_l[e * GC:(e + 1) * GC, k, :, :],
                                   bass.AP(coef_d.tensor, k * G * ST + e * ST, [[0, GC], [8 * ST, 16], [1, ST]])
                                   ).then_inc(coef_io, 16)
            pool.wait_ge(dve_misc, 5)
            pool.dma_start(dist_d, hf[0:HEADS, 0, 1:3, :].rearrange("p a t -> p (a t)")).then_inc(dist_io, 16)
            pool.wait_ge(dist_io, 16)
            for h in range(HEADS):
                pool.dma_start(bass.AP(skew_d.tensor, h * P * 513, [[513, P], [1, 512]]),
                               bass.AP(dist_d.tensor, h * 512, [[0, P], [1, 512]])).then_inc(bias_io, 16)
            pool.wait_ge(coef_io, 32 + 16 * 16)
            pool.wait_ge(misc_in, 16 * 11)
            cre, cim = coef_l[:, 0, :, :], coef_l[:, 1, :, :]
            bre, bim = b_ld[:, 0, :, :], b_ld[:, 1, :, :]
            pool.wait_ge(ada_mm, NADA)
            p0, p1 = (adacc[:, k, :].rearrange("p (g s) -> p g s", s=ST) for k in range(2))
            nc.gpsimd.tensor_tensor(bb[:, 0, :, :], cre, bre, ALU.mult)
            nc.gpsimd.tensor_tensor(p0, cim, bim, ALU.mult)
            nc.gpsimd.tensor_tensor(bb[:, 1, :, :], cre, bim, ALU.mult)
            nc.gpsimd.tensor_tensor(p1, cim, bre, ALU.mult)
            pool.drain()
            nc.gpsimd.tensor_tensor(bb[:, 0, :, :], bb[:, 0, :, :], p0, ALU.subtract)
            nc.gpsimd.tensor_tensor(bb[:, 1, :, :], bb[:, 1, :, :], p1, ALU.add).then_inc(bb_ready, 1)
            pool.drain()
            pool.wait_ge(hf_ready, UPB)
            pool.wait_ge(stat_ready, UPB)

            def map_load(s, buf):
                pool.dma_start(cst[:, buf, :, :, :].rearrange("p a b c -> p (a b c)"),
                               c_map[bass.ds(s, 1)].rearrange("o p n -> (o p) n")).then_inc(c_in, 16)

            def tables(i, j, first, last):
                s = i * 8 + j
                buf = j % 2
                late = not (first and j < 2)
                pool.wait_ge(prod_ready, s + 1)
                if late:
                    pool.wait_ge(trig_ready, s - 1)
                SU = FR[:, buf, :, :]
                nc.gpsimd.tensor_tensor(SU, PH[:, buf, :, :], LO[:, buf, :, :], ALU.add)
                pool.drain()
                nc.gpsimd.tensor_scalar(SU, SU, 1.0, ROUND, ALU.mult, ALU.add)
                pool.drain()
                nc.gpsimd.tensor_scalar(SU, SU, 1.0, -ROUND, ALU.mult, ALU.add)
                pool.drain()
                nc.gpsimd.tensor_tensor(SU, PH[:, buf, :, :], SU, ALU.subtract)
                pool.drain()
                nc.gpsimd.tensor_tensor(SU, SU, LO[:, buf, :, :], ALU.add)
                pool.drain()
                nc.gpsimd.tensor_scalar(SU, SU, BELOW_PI / (2 * PI), -BELOW_PI / (2 * PI),
                                        ALU.min, ALU.max).then_inc(frac_ready, 1)
                pool.wait_ge(c_in, (s + 1) * 16)
                for k in range(2):
                    m_k = cst[:, j % 4, :, k, :]
                    ins = nc.gpsimd.tensor_tensor(m_k, m_k, sgn[:, k:k + 1].unsqueeze(2).to_broadcast([P, 2, 32]),
                                                  ALU.mult)
                ins.then_inc(cst_ready, 1)
                if late:
                    pool.wait_ge(x_pe, s - 1)
                    pool.wait_ge(y_pe, s - 1)
                if not (last and j >= 6):
                    map_load(s + 2, (j + 2) % 4)
                q = j % 4
                sup = i * 2 + j // 4
                m = gmask[:, 2 * q:2 * q + 2].unsqueeze(2).to_broadcast([P, 2, ST])
                for k in range(2):
                    src = bb[:, k, bass.ds(sup, 1), :].to_broadcast([P, 2, ST])
                    nc.gpsimd.tensor_tensor(bd[:, buf, :, k, :], src, m, ALU.mult)
                pool.drain()
                nc.gpsimd.tensor_scalar(bd[:, buf, :, 2, :], bd[:, buf, :, 0, :], -1.0, 0.0,
                                        ALU.mult, ALU.add).then_inc(bd_ready, 1)

            map_load(0, 0)
            map_load(1, 1)
            for j in range(8):
                tables(0, j, True, False)
            with pool.Fori(1, 7) as i:
                for j in range(8):
                    tables(i, j, False, False)
            for j in range(8):
                tables(7, j, False, True)

            pool.wait_ge(gelu_done, 16)
            pool.wait_ge(bias_io, 16 * HEADS)
            skew_v = skew_d[:, 0:P * 512].rearrange("h (p j) -> h p j", j=512)
            pool.dma_start(subg, rows(subln_g, TOK)).then_inc(ba_in, 16)

            def head_loads(h, first):
                if not first:
                    pool.wait_ge(qk_pe, h)
                pool.wait_ge(stored, h * 16 + 16 * 19)
                qk = [(q_in, 16), (k_in, 24)]
                for dst, b0 in qk:
                    pool.dma_start(dst, at_block(proj_h, h + b0)).then_inc(qk_in, 16)
                if not first:
                    pool.wait_ge(s_max, h)
                sk = skew_v[h] if first else skew_v[bass.ds(h, 1)].rearrange("o p j -> (o p) j")
                for qb in range(NH):
                    start = TOK - 1 - P * qb
                    pool.dma_start(bias_in[:, qb, :], sk[:, start:start + TOK]).then_inc(ba_in, 16)
                if not first:
                    pool.wait_ge(o_pe, h)
                pool.dma_start(v_in, at_block(proj_h, h + 32)).then_inc(va_in, 16)
                if not first:
                    pool.wait_ge(ya_sb, h)
                pool.dma_start(za_in, at_block(proj_h, h + 40)).then_inc(za_in_s, 16)

            bg_v = bada_gate.rearrange("o (b c) -> b o c", c=ADA_CB)
            gate_v = gate_d.rearrange("o (b c) -> b o c", c=ADA_CB)

            def block_row(v, b):
                return v[b] if isinstance(b, int) else v[bass.ds(b, 1)].rearrange("q o c -> (q o) c")

            def gate_out(cb):
                pool.wait_ge(gate_row, cb + 1)
                pool.dma_start(block_row(gate_v, cb), grow[0:1, :]).then_inc(gate_st, 16)
                pool.wait_ge(gate_st, cb * 16 + 16)

            pool.dma_start(grow[0:1, :], bg_v[0]).then_inc(bg_in, 16)
            head_loads(0, True)
            with pool.Fori(0, HEADS // 2 - 1) as cb:
                head_loads(cb * 2 + 1, False)
                head_loads(cb * 2 + 2, False)
                gate_out(cb)
                pool.dma_start(grow[0:1, :], block_row(bg_v, cb + 1)).then_inc(bg_in, 16)
            head_loads(HEADS - 1, False)
            gate_out(HEADS // 2 - 1)

            pool.wait_ge(yaT_sb, HEADS)
            for j in range(4):
                if j:
                    pool.wait_ge(ys_sb, j)
                pool.dma_start(zs, at_block(proj_v, 4 + j)).then_inc(zs_in, 16)
            pool.wait_ge(ys_sb, 4)
            pool.wait_ge(stored, 16 * 36)
            for j in range(8):
                if j:
                    pool.wait_ge(ga_used, j)
                pool.dma_start(ga, at_block(proj_v, 32 + j)).then_inc(ga_in, 16)
                if j:
                    pool.wait_ge(m_sb, j)
                pool.dma_start(gs, at_block(proj_v, 24 + j)).then_inc(gs_in, 16)
            pool.wait_ge(m_pe, 8)
            for j in range(8):
                if j >= 2:
                    pool.wait_ge(o_sb, j - 1)
                pool.dma_start(xb[:, j % 2, :, :], x_v[j]).then_inc(xg_in[j % 2], 16)
                pool.dma_start(gate_b[:, j % 2, :], bass.AP(gate_d.tensor, j * CB, [[0, P], [1, CB]])
                               ).then_inc(xg_in[j % 2], 16)
                if j == 1:
                    pool.dma_start(fg, rows(final_g, D)).then_inc(fg_in, 16)

        @block.scalar
        def _(act):
            act.wait_ge(cons_in, 16 * 5)
            nc.scalar.activation(small[:, 1:2], small[:, 0:1], ACT.Exp)
            act.drain()
            nc.scalar.activation(npar[:, 128:192], npar[:, 0:64], ACT.Exp,
                                 scale=small[:, 1:2]).then_inc(act_misc, 1)
            nc.scalar.activation(coef_l[:, 0, 0, 0:KT], cact[:, :], ACT.Sigmoid).then_inc(act_misc, 1)
            act.wait_ge(dve_misc, 2)
            nc.scalar.activation(npar[:, 256:320], npar[:, 192:256], ACT.Sin)
            nc.scalar.activation(npar[:, 320:384], npar[:, 192:256], ACT.Abs)
            act.drain()
            nc.scalar.activation(npar[:, 384:448], npar[:, 320:384], ACT.Sin,
                                 scale=-1.0, bias=small[:, 2:3]).then_inc(act_misc, 1)
            act.wait_ge(dve_misc, 3)
            nc.scalar.activation(small[:, 5:7], small[:, 3:5], ACT.Exp).then_inc(act_misc, 1)
            act.wait_ge(x_in, 32)
            for h in range(NH):
                nc.scalar.activation(a_hi[:, 16 * h:16 * h + 16, :].rearrange("p k t -> p (k t)"), xs[:, h, :], ACT.Square,
                                     accum_out=small[:, 40 + h:41 + h])
            act.drain()
            nc.scalar.activation(small[:, 42:44], small[:, 40:42], ACT.Sqrt, scale=1.0 / D,
                                 bias=small[:, 7:8]).then_inc(act_misc, 1)

            def high(w, slot, hb, full):
                act.wait_ge(raw_full[slot], full)
                if not (isinstance(w, int) and w < 2):
                    act.wait_ge(pe_used, w - 1)
                nc.scalar.activation(w_hi[:, hb, :, :], raw[:, slot, :, :], ACT.Copy).then_inc(h_done, 1)

            def turns(r):
                return (r // RING + 1) * 16

            def evac(b, par, pe_count):
                act.wait_ge(pe_used, pe_count)
                for hh in range(NH):
                    last = nc.scalar.activation(stage[:, par, hh, :], bank[2 * par + hh][:, :], ACT.Copy)
                last.then_inc(acc_free_a, 1)

            def store(b, par, n):
                act.wait_ge(acc_free_a, b + 1)
                if not (isinstance(n, int) and n == 0):
                    act.wait_ge(stored, n * 16)
                act.dma_start(at_block(proj_v, b), stage[:, par, :, :]).then_inc(stored, 16)

            def products(s, buf):
                for g in range(2):
                    col = s * 2 + g
                    for k, dst in enumerate((PH, LO)):
                        ph = rot[:, k, bass.ds(col, 1)] if not isinstance(col, int) else rot[:, k, col:col + 1]
                        ins = nc.scalar.activation(dst[:, buf, g, :], tv[:, :], ACT.Copy, scale=ph)
                ins.then_inc(prod_ready, 1)

            act.wait_ge(dist_io, 16)
            act.wait_ge(dve_misc, 7)
            for b in range(BLK_A):
                for u in range(UPB):
                    w = UPB * b + u
                    if b == 0:
                        act.wait_ge(xt_pe, u + 1)
                        if u >= 2:
                            act.wait_ge(stat_ready, u - 1)
                        for t in range(UT):
                            kt = UT * u + t
                            pb = bank[4 + 2 * (u % 2) + t // 2]
                            last = nc.scalar.activation(hf[:, u % 2, t, :], pb[:, TOK * (t % 2):TOK * (t % 2 + 1)],
                                                        ACT.Identity, scale=sc_col[:, kt:kt + 1],
                                                        bias=sh_col[:, kt:kt + 1])
                        last.then_inc(hf_ready, 1)
                    high(w, w % RING, w % 2, turns(R0 + w))
                    if b == BLK_A - 1 and u in (5, 6):
                        products(u - 5, u - 5)
                    if b and u == 1:
                        if b >= 3:
                            act.wait_ge(ut_pe, b - 2)
                        if b == 1:
                            act.wait_ge(bb_ready, 1)
                        evac(b - 1, (b - 1) % 2, UPB * b)

            def trig(i, j, first):
                s = i * 8 + j
                buf = j % 2
                act.wait_ge(frac_ready, s + 1)
                if not (first and j < 2):
                    act.wait_ge(hcs_ready, s - 1)
                nc.scalar.activation(FA, FR[:, buf, :, :], ACT.Abs)
                nc.scalar.activation(sinb[:, buf, :, :], FR[:, buf, :, :], ACT.Sin, scale=2 * PI)
                act.drain()
                nc.scalar.activation(cosb[:, buf, :, :], FA, ACT.Sin, scale=-2 * PI,
                                     bias=small[:, 2:3]).then_inc(trig_ready, 1)
                act.drain()

            def tanh(n):
                act.wait_ge(tanh_in, n)
                nc.scalar.activation(gl[:, 1, :], gl[:, 0, :], ACT.Tanh,
                                     scale=math.sqrt(2 / PI)).then_inc(tanh_out, 1)

            def act_b(i, first):
                for bl in range(2):
                    for u in range(UPB):
                        v = UPB * bl + u
                        w = i * 16 + (UPB * BLK_A + v)
                        high(w, v % RING, v % 2, i * 64 + turns(R0 + UPB * BLK_A + v))
                        if u == 1:
                            b = i * 2 + (BLK_A + bl - 1)
                            par = (bl + 1) % 2
                            if first and bl == 0:
                                act.wait_ge(ut_pe, 2)
                                evac(b, par, UPB * BLK_A)
                            else:
                                act.wait_ge(ut_pe, 3 if first else 4)
                                evac(b, par, i * 16 + UPB * (BLK_A + bl))
                                store(b, par, i * 2 + (bl - 1))
                        if v % 2:
                            act_pair(i, v // 2, first)

            def act_pair(i, j, first):
                trig(i, j, first)
                if not (isinstance(i, int) and i == 7 and j >= 6):
                    products(i * 8 + (j + 2), j % 2)
                if j == 2 and not first:
                    tanh(i * 2)
                if j == 6:
                    tanh(i * 2 + 1)

            act_b(0, True)
            with act.Fori(1, 7) as i:
                act_b(i, False)
            act_b(7, False)

            def plain_evac(b, par, nstored):
                evac(b, par, (b + 1) * UPB)
                store(b, par, nstored)

            for bl in range(4):
                for u in range(UPB):
                    w = UPB * (20 + bl) + u
                    high(w, u % RING, u % 2, turns(R0 + w))
                    if u == 1:
                        plain_evac(19 + bl, (19 + bl) % 2, 15 + bl)
                    if bl == 0 and u == 5:
                        tanh(16)

            def act_c(cb):
                for rr in range(2):
                    h1 = cb * 2 + (rr + 1)
                    for v in range(2 * UPB):
                        loc = 24 * rr + v + v // 2
                        w = cb * 32 + (W_C + 16 * rr + v)
                        high(w, loc % RING, v % 2, cb * (48 * 4) + turns(R0 + W_C + loc))
                        if v % UPB == 1:
                            b = cb * 4 + (23 + 2 * rr + v // UPB)
                            plain_evac(b, (1 + v // UPB) % 2, cb * 4 + (19 + 2 * rr + v // UPB))
                        if v == 2:
                            act.wait_ge(qk_pe, h1)
                            nc.scalar.activation(qT.rearrange("p m t -> p (m t)"), bank[4][:, :], ACT.Copy,
                                                 scale=HD ** -0.5)
                            nc.scalar.activation(kT.rearrange("p m t -> p (m t)"), bank[5][:, :],
                                                 ACT.Copy).then_inc(qk_sb, 1)
                        if v == 6:
                            act.wait_ge(s_max, h1)
                            for qb in range(2):
                                for m in range(2):
                                    k = 2 * qb + m
                                    nc.scalar.activation(sc[:, qb, m, :], sc[:, qb, m, :], ACT.Exp,
                                                         bias=small[:, 16 + k:17 + k],
                                                         accum_out=small[:, 20 + k:21 + k])
                            act.wait_ge(za_in_s, h1 * 16)
                            nc.scalar.activation(szA, za_in, ACT.Sigmoid).then_inc(p_exp, 1)
                        if v == 10:
                            act.wait_ge(at_pe, h1)
                            nc.scalar.activation(aT.rearrange("p m t -> p (m t)"), bank[4][:, :],
                                                 ACT.Copy).then_inc(at_t, 1)
                        if v == 12:
                            act.wait_ge(o_pe, h1)
                            for qb in range(2):
                                nc.scalar.activation(aT[:, qb, :], bank[6 + qb][:, 0:TOK], ACT.Square,
                                                     accum_out=small[:, 28 + qb:29 + qb])
                            act.drain()
                            nc.scalar.activation(small[:, 30:32], small[:, 28:30], ACT.Sqrt, scale=1.0 / TOK,
                                                 bias=small[:, 60:61]).then_inc(o_ssq, 1)
                        if v == 15:
                            act.wait_ge(ya_pe, h1)
                            nc.scalar.activation(feat[:, bass.ds(cb * 4 + (16 + 2 * rr), 2), :].rearrange("p k t -> p (k t)"),
                                                 bank[5][:, :], ACT.Copy).then_inc(yaT_sb, 1)

            with act.Fori(0, HEADS // 2) as cb:
                act_c(cb)

            def sig_prev(j):
                act.wait_ge(pe_used, W_D + UT * (j + 1))
                if j:
                    act.wait_ge(ys_sb, j)
                for hh in range(NH):
                    last = nc.scalar.activation(sig[:, hh, :], bank[2 * (j % 2) + hh][:, :], ACT.Sigmoid)
                last.then_inc(acc_free_a, 1)
                act.wait_ge(zs_in, 16 * (j + 1))
                nc.scalar.activation(sz, zs, ACT.Sigmoid).then_inc(sig_done, 1)

            def ysT_copy(j):
                act.wait_ge(ys_pe, j + 1)
                for k in range(2):
                    last = nc.scalar.activation(ysT[:, 4 * j + 2 * k:4 * j + 2 * k + 2, :].rearrange("p k t -> p (k t)"),
                                                bank[6 + k][:, :], ACT.Copy)
                last.then_inc(feat_sb, 1)

            for j in range(4):
                for u in range(UT):
                    w = W_D + UT * j + u
                    high(w, w % RING, w % 2, turns(ring_of(w)))
                    if u == 1:
                        if j == 0:
                            plain_evac(39, 1, 35)
                        else:
                            sig_prev(j - 1)
                    if u == 3 and j:
                        ysT_copy(j - 1)

            def mT_copy(j):
                act.wait_ge(m_pe, j + 1)
                for k in range(2):
                    last = nc.scalar.activation(feat[:, 4 * j + 2 * k:4 * j + 2 * k + 2, :].rearrange("p k t -> p (k t)"),
                                                bank[4 + k][:, :], ACT.Copy)
                last.then_inc(feat_sb, 1)

            def gs_sigmoid(j):
                act.wait_ge(gs_in, 16 * (j + 1))
                nc.scalar.activation(gs, gs, ACT.Sigmoid).then_inc(gs_sig, 1)

            for j in range(8):
                for u in range(UPB):
                    w = W_E + UPB * j + u
                    high(w, w % RING, w % 2, turns(ring_of(w)))
                    if u == 1:
                        if j == 0:
                            sig_prev(3)
                        else:
                            gs_sigmoid(j - 1)
                    if u == 3:
                        if j == 0:
                            ysT_copy(3)
                        act.wait_ge(ga_in, 16 * (j + 1))
                        nc.scalar.activation(ga, ga, ACT.Sigmoid).then_inc(ga_sig, 1)
                    if u == 4 and j:
                        mT_copy(j - 1)

            def squares(j):
                act.wait_ge(o_sb, j + 1)
                for hh in range(NH):
                    last = nc.scalar.activation(junk[:, hh, :], obuf[:, hh, CB * j:CB * (j + 1)], ACT.Square,
                                                accum_out=small[:, 40 + 8 * hh + j:41 + 8 * hh + j])
                last.then_inc(o_sq, 1)
                act.drain()

            for j in range(8):
                for u in range(UPB):
                    w = W_F + UPB * j + u
                    high(w, w % RING, w % 2, turns(ring_of(w)))
                    if u == 1 and j == 0:
                        gs_sigmoid(7)
                    if u == 4:
                        if j == 0:
                            mT_copy(7)
                        else:
                            squares(j - 1)
            squares(7)
            act.wait_ge(f_rms, 1)
            nc.scalar.activation(small[:, 34:36], small[:, 32:34], ACT.Sqrt, scale=1.0 / D,
                                 bias=small[:, 7:8]).then_inc(f_rstd, 1)
            for j in range(8):
                act.wait_ge(f_out, j + 1)
                act.dma_start(out_v[j], obuf[:, :, CB * j:CB * (j + 1)]).then_inc(out_st, 16)

        @block.vector
        def _(dve):
            V = nc.vector

            V.memset(ones[:, :], 1.0)
            V.memset(sgn[:, :], -1.0)
            dve.drain()
            V.memset(sgn[0:ST, 0:1], 1.0)
            V.memset(small[:, 2:3], PI / 2)
            V.memset(small[:, 7:8], 1e-6)
            V.memset(small[:, 60:61], 1e-5).then_inc(dve_misc, 1)
            dve.wait_ge(act_misc, 2)
            n = lambda k: npar[:, 64 * k:64 * (k + 1)]
            lr, li, mag, red, sn, ab, cs = n(0), n(1), n(2), n(3), n(4), n(5), n(6)
            V.tensor_tensor(cact[:, :], cact[:, :], coef_l[:, 0, 0, 0:KT], ALU.mult)
            V.tensor_scalar(red, li, small[:, 1:2], None, ALU.mult)
            dve.drain()
            V.tensor_scalar(ab, red, 1 / (2 * PI), ROUND, ALU.mult, ALU.add)
            dve.drain()
            V.tensor_scalar(ab, ab, ROUND, None, ALU.subtract)
            dve.drain()
            for cw in (CW1, CW2, CW3):
                V.scalar_tensor_tensor(red, ab, -cw, red, ALU.mult, ALU.add)
                dve.drain()
            V.tensor_scalar(red, red, BELOW_PI, -BELOW_PI, ALU.min, ALU.max).then_inc(dve_misc, 1)
            dve.wait_ge(misc_in, 16 * 11)
            lam = npar[:, 512:1024].rearrange("p (a d) -> p a d", a=4)
            for k in range(2):
                V.tensor_tensor(lam[:, 2 * k, :], lam[:, 2 * k, :], lam[:, 2 * k + 1, :], ALU.mult)
            dve.drain()
            V.tensor_reduce(small[:, 3:5], lam[:, 0::2, :], AX.X, ALU.add).then_inc(dve_misc, 1)
            dve.wait_ge(act_misc, 3)
            abre, abim, den, num, t0, t1 = cs, sn, coef_l[:, 0, 2, :], coef_l[:, 0, 3, :], coef_l[:, 0, 4, :], coef_l[:, 0, 5, :]
            cre, cim, ph = coef_l[:, 0, 6, :], coef_l[:, 0, 7, :], coef_l[:, 1, 0:6, :].rearrange("p (a b) s -> p a (b s)", a=3)
            V.tensor_tensor(abre, mag, cs, ALU.mult)
            V.tensor_tensor(abim, mag, sn, ALU.mult)
            V.tensor_tensor(den, lr, lr, ALU.mult)
            V.tensor_tensor(t0, li, li, ALU.mult)
            dve.drain()
            V.tensor_tensor(den, den, t0, ALU.add)
            V.tensor_scalar(num, abre, 1.0, None, ALU.subtract)
            dve.drain()
            V.reciprocal(den, den)
            V.tensor_tensor(cre, num, lr, ALU.mult)
            V.tensor_tensor(t0, abim, li, ALU.mult)
            V.tensor_tensor(cim, abim, lr, ALU.mult)
            V.tensor_tensor(t1, num, li, ALU.mult)
            dve.drain()
            V.tensor_tensor(cre, cre, t0, ALU.add)
            V.tensor_tensor(cim, cim, t1, ALU.subtract)
            dve.drain()
            V.tensor_tensor(cre, cre, den, ALU.mult)
            V.tensor_tensor(cim, cim, den, ALU.mult)
            V.tensor_scalar(red, red, 1 / (2 * PI), None, ALU.mult)
            dve.drain()
            V.tensor_scalar(ab, red, ROUND16, None, ALU.add)
            dve.drain()
            for half in range(2):
                V.tensor_scalar(ph[:, 0, ST * half:ST * (half + 1)], ab, ROUND16, None, ALU.subtract)
                V.tensor_copy(ph[:, 2, ST * half:ST * (half + 1)], mag)
            dve.drain()
            for half in range(2):
                last = V.tensor_tensor(ph[:, 1, ST * half:ST * (half + 1)], red, ph[:, 0, 0:ST], ALU.subtract)
            last.then_inc(dve_misc, 1)
            dve.wait_ge(pe_misc, 1)
            V.tensor_copy(rot[:, :, :].rearrange("p a g -> p (a g)"), bank[1][:, 0:3 * G])
            V.tensor_copy(hf[0:HEADS, 0, 1, :], bank[2][0:HEADS, 0:TOK])
            V.memset(hf[0:HEADS, 0, 2, :], NEG)
            dve.wait_ge(act_misc, 4)
            dve.drain()
            V.tensor_tensor(small[:, 5:6], small[:, 6:7], small[:, 5:6], ALU.subtract)
            dve.drain()
            V.tensor_scalar(small[:, 6:7], small[:, 5:6], LAM_INIT, None, ALU.subtract).then_inc(dve_misc, 1)

            def ada_unit(r, slot, full, acc, kt, first, last):
                dve.wait_ge(raw_full[slot], full)
                for t in range(2):
                    src, col = raw_ada[:, slot, t, :], kt + t
                    cc = cact[:, col:col + 1] if isinstance(col, int) else cact[:, bass.ds(col, 1)]
                    if first and t == 0:
                        ins = V.tensor_scalar(acc, src, cc, None, ALU.mult)
                    else:
                        ins = V.scalar_tensor_tensor(acc, src, cc, acc, ALU.mult, ALU.add)
                    if t == 0 or not last:
                        if t:
                            ins.then_inc(raw_used, 1)
                        dve.drain()
                    else:
                        ins.then_inc(raw_used, 1)
                        dve.drain()

            def ada_block(cb, par, first):
                if not first:
                    dve.wait_ge(ada_mm, cb - 1)
                for u in range(ADA_UNITS):
                    ada_unit(None, u % RING, cb * (16 * ADA_UNITS // RING) + 16 * (u // RING + 1),
                             adacc[:, par, :], 2 * u, u == 0, u == ADA_UNITS - 1)
                dve.drain().then_inc(acc_ready, 1)

            ada_block(0, 0, True)
            dve.wait_ge(act_misc, 5)
            V.reciprocal(small[:, 44:46], small[:, 42:44])
            dve.drain()
            for h in range(NH):
                last = V.tensor_scalar(xs[:, h, :], xs[:, h, :], small[:, 44 + h:45 + h], None, ALU.mult)
            last.then_inc(dve_misc, 1)
            ada_block(1, 1, True)
            with dve.Fori(1, NADA // 2) as i:
                for par in range(2):
                    ada_block(i * 2 + par, par, False)
            dve.wait_ge(ada_mm, NADA)
            V.tensor_tensor(small[:, 8:40], bank[0][:, 0:KT], small[:, 8:40], ALU.add)
            V.tensor_tensor(sh_col[:, :], bank[0][:, KT:2 * KT], sh_col[:, :], ALU.add)
            dve.drain()
            V.tensor_scalar(sh_col[:, :], sh_col[:, :], 1.0, None, ALU.add)
            dve.drain()
            V.tensor_tensor(sc_col[:, :], sh_col[:, :], sc_col[:, :], ALU.mult)
            dve.drain()
            V.tensor_copy(sh_col[:, :], small[:, 8:40]).then_inc(dve_misc, 1)

            def low(w, slot, hb):
                dve.wait_ge(h_done, w + 1)
                V.tensor_tensor(w_lo[:, hb, :, :], raw[:, slot, :, :], w_hi[:, hb, :, :].bitcast(F32),
                                ALU.subtract).then_inc(raw_used, 1)

            def split(src, k0, pe_count):
                if pe_count:
                    dve.wait_ge(pe_used, pe_count)
                V.tensor_copy(a_hi[:, k0:k0 + UT, :], src)
                dve.drain()
                V.tensor_tensor(a_lo[:, k0:k0 + UT, :], src, a_hi[:, k0:k0 + UT, :].bitcast(F32),
                                ALU.subtract).then_inc(stat_ready, 1)

            def ut_copy(b):
                dve.wait_ge(ut_pe, b + 1)
                for k in range(2):
                    last = V.tensor_copy(feat[:, 4 * b + 2 * k:4 * b + 2 * k + 2, :].rearrange("p k t -> p (k t)"),
                                         bank[6 + k][:, :])
                last.then_inc(ut_done, 1)

            for b in range(BLK_A):
                for u in range(UPB):
                    w = UPB * b + u
                    if b == 0:
                        dve.wait_ge(hf_ready, u + 1)
                        split(hf[:, u % 2, :, :], UT * u, 0)
                    low(w, w % RING, w % 2)
                    if b and u == 3:
                        ut_copy(b - 1)

            def scan_pair(s, buf, first):
                dve.wait_ge(trig_ready, s + 1)
                dve.wait_ge(x_pe, s + 1)
                bx = [bank[4 + k][:, :].rearrange("p (a t) -> p a t", a=2) for k in range(2)]
                V.tensor_tensor(T1, bx[0], cosb[:, buf, :, :], ALU.mult)
                V.tensor_tensor(T2, bx[1], sinb[:, buf, :, :], ALU.mult).then_inc(x_used, 1)
                dve.drain()
                V.tensor_tensor(T1, T1, T2, ALU.add)
                dve.drain()
                for g in range(2):
                    col = s * 2 + g
                    r = rot[:, 2, bass.ds(col, 1)] if not isinstance(col, int) else rot[:, 2, col:col + 1]
                    V.tensor_tensor_scan(HH[:, g, :], r.to_broadcast([P, TOK]), T1[:, g, :], 0.0,
                                         ALU.mult, ALU.add)
                dve.drain()
                if not first:
                    dve.wait_ge(y_pe, s - 1)
                V.tensor_tensor(hcb[:, buf, :, :], HH, cosb[:, buf, :, :], ALU.mult)
                V.tensor_tensor(hsb[:, buf, :, :], HH, sinb[:, buf, :, :], ALU.mult).then_inc(hcs_ready, 1)

            def y_evac(sup):
                dve.wait_ge(y_pe, sup * 4 + 4)
                if isinstance(sup, int):
                    f, dd = feat[:, sup:sup + 1, :].rearrange("p k t -> p (k t)"), dcol[:, sup:sup + 1]
                else:
                    f, dd = feat[:, bass.ds(sup, 1), :].rearrange("p k t -> p (k t)"), dcol[:, bass.ds(sup, 1)]
                V.scalar_tensor_tensor(gl[:, 2, :], f, dd, bank[6][:, 0:TOK], ALU.mult, ALU.add).then_inc(y_used, 1)
                dve.drain()
                V.tensor_tensor(gl[:, 0, :], gl[:, 2, :], gl[:, 2, :], ALU.mult)
                dve.drain()
                V.tensor_scalar(gl[:, 0, :], gl[:, 0, :], 0.044715, 1.0, ALU.mult, ALU.add)
                dve.drain()
                V.tensor_tensor(gl[:, 0, :], gl[:, 0, :], gl[:, 2, :], ALU.mult).then_inc(tanh_in, 1)

            def y_gelu(sup):
                dve.wait_ge(tanh_out, sup + 1)
                f = (feat[:, sup:sup + 1, :] if isinstance(sup, int) else feat[:, bass.ds(sup, 1), :]
                     ).rearrange("p k t -> p (k t)")
                V.scalar_tensor_tensor(gl[:, 0, :], gl[:, 1, :], 1.0, gl[:, 2, :], ALU.add, ALU.mult)
                dve.drain()
                V.tensor_scalar(f, gl[:, 0, :], 0.5, None, ALU.mult).then_inc(gelu_done, 1)
                dve.drain()

            def dve_b(i, first):
                for v in range(2 * UPB):
                    low(i * 16 + (UPB * BLK_A + v), v % RING, v % 2)
                    if first and v == 3:
                        ut_copy(3)
                    if v % 2:
                        j = v // 2
                        if not (first and j == 0):
                            scan_pair(i * 8 + (j - 1), (j - 1) % 2, first and j <= 2)
                        if j == 5:
                            y_evac(i * 2)
                        if j == 6:
                            y_gelu(i * 2)
                        if j == 1 and not first:
                            y_evac(i * 2 - 1)
                        if j == 2 and not first:
                            y_gelu(i * 2 - 1)

            dve_b(0, True)
            with dve.Fori(1, 8) as i:
                dve_b(i, False)
            for bl in range(4):
                for u in range(UPB):
                    w = UPB * (20 + bl) + u
                    low(w, u % RING, u % 2)
                    if bl == 0:
                        if u == 1:
                            scan_pair(63, 1, False)
                        if u == 3:
                            y_evac(15)
                        if u == 6:
                            y_gelu(15)

            with dve.Fori(0, HEADS // 2) as cb:
                for rr in range(2):
                    h1 = cb * 2 + (rr + 1)
                    for v in range(2 * UPB):
                        loc = 24 * rr + v + v // 2
                        low(cb * 32 + (W_C + 16 * rr + v), loc % RING, v % 2)
                        if v % 2:
                            first = rr == 0 and v == 1
                            rl = R0 + W_C + loc + 1
                            ada_unit(None, rl % RING, cb * (48 * 4) + 16 * (rl // RING + 1), gacc,
                                     2 * (8 * rr + v // 2), first, False)
                        if v == 5:
                            dve.wait_ge(s_pe, h1)
                            dve.wait_ge(ba_in, h1 * 32 + 16)
                            for qb in range(2):
                                V.tensor_tensor(sc[:, qb, :, :], bank[6 + qb][:, :].rearrange("p (m k) -> p m k", m=2),
                                                bias_in[:, qb:qb + 1, :].to_broadcast([P, 2, TOK]), ALU.add)
                            dve.drain()
                            V.tensor_reduce(small[:, 16:20], sc.rearrange("p q m k -> p (q m) k"), AX.X, ALU.max)
                            dve.drain()
                            V.tensor_scalar(small[:, 16:20], small[:, 16:20], -1.0, None, ALU.mult).then_inc(s_max, 1)
                        if v == 7:
                            dve.wait_ge(p_exp, h1)
                            V.reciprocal(small[:, 24:28], small[:, 20:24])
                            dve.drain()
                            for qb in range(2):
                                k = 25 + 2 * qb
                                V.tensor_tensor(small[:, k:k + 1], small[:, k:k + 1], small[:, 6:7], ALU.mult)
                            dve.drain()
                            for qb in range(2):
                                V.tensor_scalar(sc[:, qb, 0, :], sc[:, qb, 0, :], small[:, 24 + 2 * qb:25 + 2 * qb],
                                                None, ALU.mult)
                            dve.drain()
                            for qb in range(2):
                                last = V.scalar_tensor_tensor(at[:, qb, :], sc[:, qb, 1, :],
                                                              small[:, 25 + 2 * qb:26 + 2 * qb], sc[:, qb, 0, :],
                                                              ALU.mult, ALU.add)
                            last.then_inc(at_sb, 1)
                        if v == 13:
                            dve.wait_ge(o_ssq, h1)
                            V.reciprocal(small[:, 36:38], small[:, 30:32])
                            V.tensor_tensor(szA, szA, za_in, ALU.mult)
                            dve.drain()
                            V.tensor_scalar(small[:, 36:38], small[:, 36:38], 1.0 - LAM_INIT, None, ALU.mult)
                            V.tensor_tensor(szA, szA, subg.unsqueeze(1).to_broadcast([P, 2, TOK]), ALU.mult)
                            dve.drain()
                            for qb in range(2):
                                last = V.scalar_tensor_tensor(ya[:, qb, :], bank[6 + qb][:, 0:TOK],
                                                              small[:, 36 + qb:37 + qb], szA[:, qb, :],
                                                              ALU.mult, ALU.mult)
                            last.then_inc(ya_sb, 1)
                dve.drain().then_inc(gacc_ready, 1)
                dve.wait_ge(gate_pe, cb + 1)
                dve.wait_ge(bg_in, cb * 16 + 16)
                for k in range(2):
                    g_row = grow[0:1, CB * k:CB * (k + 1)]
                    last = V.tensor_tensor(g_row, g_row, bank[(4, 7)[k]][0:1, :], ALU.add)
                last.then_inc(gate_row, 1)

            def ys_prev(j):
                dve.wait_ge(sig_done, j + 1)
                dve.wait_ge(gt_pe, j + 1)
                if j:
                    dve.wait_ge(ys_pe, j)
                else:
                    dve.wait_ge(gate_st, 16 * 4)
                V.tensor_tensor(ys, zs, sz, ALU.mult)
                for hh in range(NH):
                    V.tensor_tensor(sig[:, hh, :], bank[4 + hh][:, :], sig[:, hh, :], ALU.mult)
                dve.drain()
                V.tensor_tensor(ys, ys, sig, ALU.mult).then_inc(ys_sb, 1)

            for j in range(4):
                for u in range(UT):
                    w = W_D + UT * j + u
                    if j == 0:
                        split(feat[:, UT * u:UT * (u + 1), :], UT * u, W_D - UPB + u + 1)
                    low(w, w % RING, w % 2)
                    if u == 1 and j:
                        ys_prev(j - 1)

            def merge_prev(j):
                dve.wait_ge(pe_used, W_E + UPB * (j + 1))
                dve.wait_ge(gs_sig, j + 1)
                if j:
                    dve.wait_ge(m_pe, j)
                for hh in range(NH):
                    last = V.tensor_tensor(mrg[:, hh, :], bank[2 + hh][:, :], gs[:, hh, :], ALU.mult)
                last.then_inc(acc_free_v, 1)
                dve.drain()
                V.tensor_tensor(mrg, mrg, part, ALU.add).then_inc(m_sb, 1)
                dve.drain()

            for j in range(8):
                for u in range(UPB):
                    w = W_E + UPB * j + u
                    if j == 0 and u < UT:
                        split(feat[:, 16 + UT * u:16 + UT * (u + 1), :], UT * u, W_E - UT + u + 1)
                    elif j == 0:
                        k = u - UT
                        dve.wait_ge(feat_sb, k + 1)
                        split(ysT[:, UT * k:UT * (k + 1), :], 16 + UT * k, 0)
                    low(w, w % RING, w % 2)
                    if u == 1:
                        if j == 0:
                            ys_prev(3)
                        else:
                            merge_prev(j - 1)
                    if u == 5:
                        dve.wait_ge(pe_used, W_E + UPB * j + UT)
                        dve.wait_ge(ga_sig, j + 1)
                        for hh in range(NH):
                            last = V.tensor_tensor(part[:, hh, :], bank[hh][:, :], ga[:, hh, :], ALU.mult)
                        last.then_inc(acc_free_v, 1)
                        dve.drain().then_inc(ga_used, 1)

            def out_prev(j):
                dve.wait_ge(pe_used, W_F + UPB * (j + 1))
                dve.wait_ge(xg_in[j % 2], 32 * (j // 2 + 1))
                o = [obuf[:, hh, CB * j:CB * (j + 1)] for hh in range(NH)]
                for hh in range(NH):
                    last = V.tensor_tensor(o[hh], bank[2 * (j % 2) + hh][:, :], gate_b[:, j % 2, :], ALU.mult)
                last.then_inc(acc_free_v, 1)
                dve.drain()
                for hh in range(NH):
                    last = V.tensor_tensor(o[hh], o[hh], xb[:, j % 2, hh, :], ALU.add)
                last.then_inc(o_sb, 1)

            for j in range(8):
                for u in range(UPB):
                    w = W_F + UPB * j + u
                    if j == 0:
                        dve.wait_ge(feat_sb, 4 + u + 1)
                        split(feat[:, UT * u:UT * (u + 1), :], UT * u, W_F - UPB + u + 1)
                    low(w, w % RING, w % 2)
                    if u == 1:
                        if j == 0:
                            merge_prev(7)
                        else:
                            out_prev(j - 1)
            out_prev(7)
            dve.wait_ge(o_sq, 8)
            V.tensor_reduce(small[:, 32:34], small[:, 40:56].rearrange("p (h j) -> p h j", h=2), AX.X,
                            ALU.add).then_inc(f_rms, 1)
            dve.wait_ge(f_rstd, 1)
            V.reciprocal(small[:, 36:38], small[:, 34:36])
            dve.drain()
            dve.wait_ge(fg_in, 16)
            for j in range(8):
                for hh in range(NH):
                    o = obuf[:, hh, CB * j:CB * (j + 1)]
                    last = V.scalar_tensor_tensor(o, o, small[:, 36 + hh:37 + hh], fg[:, CB * j:CB * (j + 1)],
                                                  ALU.mult, ALU.mult)
                last.then_inc(f_out, 1)

        @block.tensor
        def _(pe):
            T = nc.tensor

            pe.wait_ge(cons_in, 16 * 5)
            pe.wait_ge(dve_misc, 4)
            ph = coef_l[:, 1, 0:6, :].rearrange("p (a b) s -> p a (b s)", a=3)
            for k in range(3):
                T.transpose(bank[1][:, G * k:G * (k + 1)], ph[:, k, :], ident[:, :])
            pe.wait_ge(misc_in, 16 * 11)
            T.matmul(bank[2][0:HEADS, 0:TOK], hf[0:32, 1, 0, 0:HEADS],
                     hf[0:32, 0, 0, :], start=True, stop=True).then_inc(pe_misc, 1)
            for cb in range(NADA):
                pe.wait_ge(acc_ready, cb + 1)
                for k in range(ADA_CB // P):
                    col = (ADA_CB // P) * cb + k
                    last = T.matmul(bank[0][:, col:col + 1], adacc[:, cb % 2, P * k:P * (k + 1)], ones[:, 0:1],
                                    start=True, stop=True)
                last.then_inc(ada_mm, 1)

            def unit(w, ring, hb, k0, pair, first, last, stat):
                pe.wait_ge(raw_used, ring + 1)
                if stat:
                    pe.wait_ge(stat_ready, stat)
                for t in range(UT):
                    for hh in range(NH):
                        acc = bank[2 * pair + hh][:, :]
                        cols = slice(P * hh, P * (hh + 1))
                        s_hi, s_lo = a_hi[:, k0 + t, cols], a_lo[:, k0 + t, cols]
                        T.matmul(acc, s_hi, w_hi[:, hb, t, :], start=first and t == 0, stop=False)
                        T.matmul(acc, s_hi, w_lo[:, hb, t, :], start=False, stop=False)
                        ins = T.matmul(acc, s_lo, w_hi[:, hb, t, :], start=False, stop=last and t == UT - 1)
                ins.then_inc(pe_used, 1)

            def acc_wait(a):
                if not (isinstance(a, int) and a < 2):
                    pe.wait_ge(acc_free_a, a - 1)

            def xt(u):
                if u >= 2:
                    pe.wait_ge(hf_ready, u - 1)
                for t in range(UT):
                    kt = UT * u + t
                    pb = bank[4 + 2 * (u % 2) + t // 2]
                    for h in range(NH):
                        o = TOK * (t % 2) + P * h
                        last = T.transpose(pb[:, o:o + P], xs[:, h, P * kt:P * (kt + 1)], ident[:, :])
                last.then_inc(xt_pe, 1)

            def ut(b):
                pe.wait_ge(acc_free_a, b + 1)
                if b:
                    pe.wait_ge(ut_done, b)
                for t in range(UT):
                    for h in range(NH):
                        o = TOK * (t % 2) + P * h
                        last = T.transpose(bank[6 + t // 2][:, o:o + P], stage[:, b % 2, h, P * t:P * (t + 1)], ident[:, :])
                last.then_inc(ut_pe, 1)

            pe.wait_ge(dve_misc, 7)
            xt(0)
            xt(1)
            for b in range(BLK_A):
                acc_wait(b)
                for u in range(UPB):
                    w = UPB * b + u
                    unit(w, R0 + w, u % 2, UT * u, b % 2, u == 0, u == UPB - 1, u + 1 if b == 0 else 0)
                    if b == 0 and u + 2 < UPB:
                        xt(u + 2)
                    if b and u == 2:
                        ut(b - 1)

            def x_mm(s, sup, j, first):
                buf = j % 2
                pe.wait_ge(bd_ready, s + 1)
                if not (first and j == 0):
                    pe.wait_ge(x_used, s)
                for k in range(2):
                    for g in range(2):
                        u_t = (feat[:, bass.ds(sup, 1), :] if not isinstance(sup, int)
                               else feat[:, sup:sup + 1, :]).rearrange("p k t -> p (k t)")
                        last = T.matmul(bank[4 + k][:, TOK * g:TOK * (g + 1)],
                                        bd[:, buf, g, k:k + 2, :].rearrange("p a s -> p (a s)"), u_t,
                                        start=True, stop=True)
                last.then_inc(x_pe, 1)

            def y_mm(s, q, buf, sup_wait):
                pe.wait_ge(hcs_ready, s + 1)
                pe.wait_ge(cst_ready, s + 1)
                if sup_wait is not None:
                    pe.wait_ge(y_used, sup_wait)
                k = 0
                for g in range(2):
                    for m, hb in enumerate((hcb, hsb)):
                        last = T.matmul(bank[6][32 * q:32 * q + 32, 0:TOK], cst[:, q, g, m, :], hb[:, buf, g, :],
                                        start=k == 0, stop=k == 3)
                        k += 1
                last.then_inc(y_pe, 1)

            def pe_b(i, first):
                for v in range(2 * UPB):
                    bl, u = v // UPB, v % UPB
                    if u == 0:
                        acc_wait(i * 2 + (BLK_A + bl))
                    w = i * 16 + (UPB * BLK_A + v)
                    unit(w, w + R0, v % 2, UT * u, bl, u == 0, u == UPB - 1, 0)
                    j = v // 2
                    if first and v == 2:
                        ut(3)
                    if v % 2 == 0:
                        if first and j == 4:
                            pe.wait_ge(ut_done, 4)
                        x_mm(i * 8 + j, i * 2 + j // 4, j, first)
                    elif not (first and j == 0):
                        if first and j == 1:
                            pe.wait_ge(ut_done, 4)
                        wait = None
                        if j == 5:
                            wait = i * 2 + 1
                        if j == 1 and not first:
                            wait = i * 2
                        y_mm(i * 8 + (j - 1), (j - 1) % 4, (j - 1) % 2, wait)

            pe_b(0, True)
            with pe.Fori(1, 8) as i:
                pe_b(i, False)
            for bl in range(4):
                acc_wait(20 + bl)
                for u in range(UPB):
                    w = UPB * (20 + bl) + u
                    unit(w, w + R0, u % 2, UT * u, bl % 2, u == 0, u == UPB - 1, 0)
                    if bl == 0 and u == 1:
                        y_mm(63, 3, 1, None)

            with pe.Fori(0, HEADS // 2) as cb:
                for rr in range(2):
                    h1 = cb * 2 + (rr + 1)
                    for v in range(2 * UPB):
                        bl, u = v // UPB, v % UPB
                        loc = 24 * rr + v + v // 2
                        if u == 0:
                            acc_wait(cb * 4 + (24 + 2 * rr + bl))
                        unit(None, cb * 48 + (R0 + W_C + loc), v % 2, UT * u, bl, u == 0, u == UPB - 1, 0)
                        if v == 0:
                            pe.wait_ge(qk_in, h1 * 32)
                            for src, pb in ((q_in, bank[4]), (k_in, bank[5])):
                                for m in range(2):
                                    for h in range(NH):
                                        last = T.transpose(pb[:, TOK * m + P * h:TOK * m + P * (h + 1)],
                                                           src[:, h, P * m:P * (m + 1)], ident[:, :])
                            last.then_inc(qk_pe, 1)
                        if v == 3:
                            pe.wait_ge(qk_sb, h1)
                            for qb in range(2):
                                for m in range(2):
                                    last = T.matmul(bank[6 + qb][:, TOK * m:TOK * (m + 1)],
                                                    qT[:, m, P * qb:P * (qb + 1)], kT[:, m, :], start=True, stop=True)
                            last.then_inc(s_pe, 1)
                        if v == 8:
                            pe.wait_ge(at_sb, h1)
                            for kk in range(2):
                                for qb in range(2):
                                    last = T.transpose(bank[4][:, TOK * kk + P * qb:TOK * kk + P * (qb + 1)],
                                                       at[:, qb, P * kk:P * (kk + 1)], ident[:, :])
                            last.then_inc(at_pe, 1)
                        if v == 10:
                            pe.wait_ge(at_t, h1)
                            pe.wait_ge(va_in, h1 * 16)
                            for qb in range(2):
                                for kk in range(2):
                                    last = T.matmul(bank[6 + qb][:, 0:TOK], aT[:, kk, P * qb:P * (qb + 1)],
                                                    v_in[:, kk, :], start=kk == 0, stop=kk == 1)
                            last.then_inc(o_pe, 1)
                        if v == 13:
                            pe.wait_ge(ya_sb, h1)
                            for ct in range(2):
                                for h in range(NH):
                                    last = T.transpose(bank[5][:, TOK * ct + P * h:TOK * ct + P * (h + 1)],
                                                       ya[:, h, P * ct:P * (ct + 1)], ident[:, :])
                            last.then_inc(ya_pe, 1)
                pe.wait_ge(gacc_ready, cb + 1)
                for k in range(2):
                    last = T.matmul(bank[(4, 7)[k]][0:1, :], ones[:, 0:1], gacc[:, CB * k:CB * (k + 1)],
                                    start=True, stop=True)
                last.then_inc(gate_pe, 1)

            def ysT_t(j):
                pe.wait_ge(ys_sb, j + 1)
                if j:
                    pe.wait_ge(feat_sb, j)
                for t in range(UT):
                    for h in range(NH):
                        o = TOK * (t % 2) + P * h
                        last = T.transpose(bank[6 + t // 2][:, o:o + P], ys[:, h, P * t:P * (t + 1)], ident[:, :])
                last.then_inc(ys_pe, 1)

            for j in range(4):
                acc_wait(40 + j)
                for u in range(UT):
                    w = W_D + UT * j + u
                    unit(w, ring_of(w), u % 2, UT * u, j % 2, u == 0, u == UT - 1, 8 + u + 1 if j == 0 else 0)
                    if u == 2 and j:
                        ysT_t(j - 1)
                    if u == 3:
                        if j == 0:
                            pe.wait_ge(yaT_sb, HEADS)
                            pe.wait_ge(gate_row, 4)
                        else:
                            pe.wait_ge(ys_sb, j)
                        for h in range(NH):
                            for t in range(UT):
                                last = T.transpose(bank[4 + h][:, P * t:P * (t + 1)],
                                                   feat[:, 4 * j + t, P * h:P * (h + 1)], ident[:, :])
                        last.then_inc(gt_pe, 1)

            def mT_t(j):
                pe.wait_ge(m_sb, j + 1)
                pe.wait_ge(feat_sb, j + 4)
                for t in range(UT):
                    for h in range(NH):
                        o = TOK * (t % 2) + P * h
                        last = T.transpose(bank[4 + t // 2][:, o:o + P], mrg[:, h, P * t:P * (t + 1)], ident[:, :])
                last.then_inc(m_pe, 1)

            def pe_e(j):
                for u in range(UPB):
                    if u % UT == 0:
                        if isinstance(j, int):
                            acc_wait(44 + u // UT)
                        else:
                            pe.wait_ge(acc_free_v, j * 2 + (u // UT - 1))
                    unit(None, j * UPB + (ring_of(W_E) + u), u % 2, UT * u, u // UT, u % UT == 0, u % UT == UT - 1,
                         12 + u + 1 if isinstance(j, int) else 0)
                    if u == 2:
                        if isinstance(j, int):
                            ysT_t(3)
                        else:
                            mT_t(j - 1)

            pe_e(0)
            with pe.Fori(1, 8) as j:
                pe_e(j)

            def pe_f(j, par, first):
                pe.wait_ge(acc_free_v, j + 15)
                for u in range(UPB):
                    unit(None, j * UPB + (ring_of(W_F) + u), u % 2, UT * u, par, u == 0, u == UPB - 1,
                         20 + u + 1 if first else 0)
                    if u == 2 and first:
                        mT_t(7)

            pe_f(0, 0, True)
            pe_f(1, 1, False)
            with pe.Fori(1, 4) as i:
                for par in range(2):
                    pe_f(i * 2 + par, par, False)


def kernel(**inputs):
    import numpy as np
    import concourse.bacc as bacc
    from concourse.bass_utils import run_bass_kernel_spmd

    f = {k: np.asarray(v) for k, v in inputs.items()}
    nc = bacc.Bacc("TRN2", target_bir_lowering=False, num_devices=1)
    arrays = {}

    def give(name, a):
        name = "in_" + name
        a = np.ascontiguousarray(a)
        arrays[name] = a
        return nc.dram_tensor(name, a.shape, mybir.dt.from_np(a.dtype), kind="ExternalInput").ap()

    cr = f["ssm_c_re"][0].transpose(2, 0, 1)
    ci = f["ssm_c_im"][0].transpose(2, 0, 1)
    cm = np.zeros((G // 2, 2 * ST, 2, 2, 2 * GC), cr.dtype)
    for gg in range(2):
        ch = slice(GC * gg, GC * (gg + 1))
        cm[:, :ST, gg, 0, ch] = cr[:, gg::2].transpose(1, 0, 2)
        cm[:, ST:, gg, 0, ch] = ci[:, gg::2].transpose(1, 0, 2)
        cm[:, :ST, gg, 1, ch] = ci[:, gg::2].transpose(1, 0, 2)
        cm[:, ST:, gg, 1, ch] = cr[:, gg::2].transpose(1, 0, 2)
    dist = np.arange(TOK)
    nf = np.maximum(dist, 1).astype(np.float32)
    large = 16 + (np.log(nf / np.float32(16)) / np.float32(math.log(8)) * np.float32(16)).astype(np.int32)
    bucket = np.where(dist < 16, dist, np.minimum(large, 31))[::-1]
    onehot = (np.arange(32)[:, None] == bucket[None, :]).astype(np.float32)
    gmask = (np.arange(P)[:, None] // GC == np.arange(8)[None, :]).astype(np.float32)

    def b_layout(b):
        return b.reshape(16, 8, ST, GC).transpose(1, 3, 0, 2).reshape(P, 16, ST)

    args = [
        give("x", f["x"][0]), give("c_col", f["c"].reshape(KT, P).T), give("g_col", f["norm_g"].reshape(KT, P).T),
        give("w_ada", f["w_ada"][0]), give("bada_col", f["b_ada"].reshape(3 * KT, P).T),
        give("bada_gate", f["b_ada"][:, 2 * D:]), give("w_in", f["w_in"][0]),
        give("lam_re", f["ssm_lambda_re"][0]), give("lam_im", f["ssm_lambda_im"][0]),
        give("log_dt", f["ssm_log_dt"].reshape(G, 1)),
        give("b_re", b_layout(f["ssm_b_re"][0])), give("b_im", b_layout(f["ssm_b_im"][0])),
        give("c_map", cm.reshape(G // 2, P, 2 * 2 * 2 * GC)), give("d_col", f["ssm_d"].reshape(16, P).T),
        give("w_glu", f["w_glu"][0]),
        give("lambdas", np.concatenate([f[k] for k in ("lambda_q1", "lambda_k1", "lambda_q2", "lambda_k2")], 1)),
        give("subln_g", f["subln_g"]), give("w_oss", f["w_out_ssm"][0]), give("w_oat", f["w_out_attn"][0]),
        give("w_o", f["w_o"][0]), give("rel_bias", f["rel_bias"]), give("final_g", f["final_g"].reshape(1, D)),
        give("onehot", onehot), give("ident", np.eye(P, dtype=np.float32)),
        give("tvals", np.arange(TOK, dtype=np.float32).reshape(1, TOK)), give("gmask", gmask),
    ]
    out = nc.dram_tensor("out", (TOK, D), F32, kind="ExternalOutput").ap()
    build(nc, *args, out)
    r = run_bass_kernel_spmd(nc, [arrays], core_ids=[0])
    return r.results[0]["out"].reshape(1, TOK, D)
```

```python
from contextlib import ExitStack
import math

import concourse.bass as bass
from concourse import mybir

F32 = mybir.dt.float32
F32R = mybir.dt.float32r
ALU = mybir.AluOpType
ACT = mybir.ActivationFunctionType
AX = mybir.AxisListType

P = 128
TOK = 256
NH = TOK // P
D = 4096
KT = D // P
CB = 512
UT = 4
UPB = KT // UT
RING = 4
NIN = 20480
G, ST, GC = 128, 64, 16
HEADS, HD = 8, 128
BLK_A, BLK_B, BLK_C = 4, 20, 16
SHIFT_SCALE = 2 * D
ADA_CB = 1024
ADA_UNITS = D // (2 * P)
NADA = SHIFT_SCALE // ADA_CB
R0 = NADA * ADA_UNITS
NC0 = D // ADA_CB
BLK_0 = 3
CH_W = 2 * BLK_0
CH_R = 2 * ADA_UNITS + CH_W
W_AT = [4 + 2 * v for v in range(CH_W)]
W_C = UPB * (BLK_A + BLK_B)
W_D = W_C + UPB * BLK_C
W_E = W_D + 4 * UT
W_F = W_E + 8 * UPB
ADA_C = (D // ADA_CB) * ADA_UNITS
ROUND = 1.5 * 2.0 ** 23
ROUND16 = 192.0
PI = math.pi
CW1 = 6.28125
CW2 = 0.0019340515136718750
CW3 = 2 * PI - CW1 - CW2
BELOW_PI = 3.1415925
NEG = -1e30
EPS = 1e-6
LAM_INIT = 0.8 - 0.6 * math.exp(-0.3 * 0)


def build(nc, x, c_col, g_col, w_ada, bada_col, bada_gate, w_in, lam_re, lam_im, log_dt,
          b_re, b_im, c_map, d_col, w_glu, lambdas, subln_g, w_oss, w_oat, w_o, rel_bias,
          final_g, onehot, ident_in, tvals, gmask_in, out):
    ctx = ExitStack()
    with ctx:
        def sb(name, shape, dt=F32):
            return ctx.enter_context(nc.sbuf_tensor(name, shape, dt))

        def sem(name):
            return ctx.enter_context(nc.semaphore(name))

        raw = sb("raw", [P, RING, UT, CB])
        w_hi = sb("w_hi", [P, 2, UT, CB], F32R)
        w_lo = sb("w_lo", [P, 2, UT, CB], F32R)
        a_hi = sb("a_hi", [P, KT, TOK], F32R)
        a_lo = sb("a_lo", [P, KT, TOK], F32R)
        feat = sb("feat", [P, KT, TOK])
        stage = sb("stage", [P, 2, NH, CB])
        work = sb("work", [P, 9216])
        ident = sb("ident", [P, P])
        tv = sb("tv", [P, TOK])
        gmask = sb("gmask", [P, 8])
        rot = sb("rot", [P, 3, G])
        dcol = sb("dcol", [P, 16])
        g_sb = sb("g_sb", [P, KT])
        ba_sb = sb("ba_sb", [P, 2, KT])
        cact = sb("cact", [P, KT])
        small = sb("small", [P, 64])
        ones = small[:, 56:60]
        sgn = small[:, 61:63]
        sc8, sh8 = small[:, 8:16], small[:, 24:32]
        bank = [ctx.enter_context(nc.psum_tensor(f"bank{i}", [P, CB], F32)) for i in range(8)]

        def carve(base, off, shape):
            n = 1
            for s in shape:
                n *= s
            ap = base[:, off:off + n]
            if len(shape) == 1:
                return ap
            names = "abcd"[:len(shape)]
            return ap.rearrange(f"p ({' '.join(names)}) -> p {' '.join(names)}",
                                **{k: v for k, v in zip(names, shape)})

        def wk(off, *shape):
            return carve(work, off, shape)

        featf = feat[:, :, :].rearrange("p k t -> p (k t)")
        xs = carve(featf, 0, (NH, D))
        bb = wk(0, 2, 16, ST)
        adacc = wk(2048, 2, ADA_CB)
        hf = wk(4096, 2, UT, TOK)
        coef_l = wk(6144, 2, 16, ST)
        b_ld = carve(stage[:, :, :, :].rearrange("p b h c -> p (b h c)"), 0, (2, 16, ST))
        npar = wk(8192, 1024)
        PH, LO = wk(2048, 2, 2, TOK), wk(3072, 2, 2, TOK)
        FR = wk(4096, 2, 2, TOK)
        FA = wk(5120, 2, TOK)
        T1, T2, HH = wk(5632, 2, TOK), wk(6144, 2, TOK), wk(6656, 2, TOK)
        bd = wk(7168, 2, 2, 3, ST)
        cst = wk(7936, 4, 2, 2, 32)
        gl = wk(8448, 3, TOK)
        cosb = carve(featf, 4096, (2, 2, TOK))
        sinb = carve(featf, 5120, (2, 2, TOK))
        hcb = carve(featf, 6144, (2, 2, TOK))
        hsb = carve(featf, 7168, (2, 2, TOK))
        gacc = wk(0, ADA_CB)
        q_in, k_in, v_in, za_in, bias_in = (wk(1024 + 512 * i, NH, TOK) for i in range(5))
        qT, kT = wk(3584, 2, TOK), wk(4096, 2, TOK)
        sc = wk(4608, 2, 2, TOK)
        at = wk(5632, 2, TOK)
        aT = wk(6144, 2, TOK)
        ya = wk(6656, 2, TOK)
        szA = wk(7168, 2, TOK)
        subg = wk(7680, TOK)
        grow = wk(7936, ADA_CB)
        ysT = wk(0, 16, TOK)
        zs, sz, sig, ys = (wk(4096 + 1024 * i, NH, CB) for i in range(4))
        ga, gs, part, mrg = (wk(4096 + 1024 * i, NH, CB) for i in range(4))
        obuf = carve(featf, 0, (NH, D))
        xb = wk(0, 2, NH, CB)
        gate_b = wk(2048, 2, CB)
        fg = wk(3072, D)
        junk = wk(7168, NH, CB)

        proj_d = nc.dram_tensor("proj_scratch", (TOK, NIN), F32, kind="Internal").ap()
        coef_d = nc.dram_tensor("coef_scratch", (2, G, ST), F32, kind="Internal").ap()
        dist_d = nc.dram_tensor("dist_scratch", (HEADS, 512), F32, kind="Internal").ap()
        skew_d = nc.dram_tensor("skew_scratch", (HEADS, P * 513), F32, kind="Internal").ap()
        gate_d = nc.dram_tensor("gate_scratch", (1, D), F32, kind="Internal").ap()

        raw_full = [sem(f"raw_full{i}") for i in range(RING)]
        raw_used = sem("raw_used")
        h_done = sem("h_done")
        pe_used = sem("pe_used")
        stat_ready = sem("stat_ready")
        acc_free_a = sem("acc_free_a")
        acc_free_v = sem("acc_free_v")
        x_scaled = sem("x_scaled")
        mod_ready = sem("mod_ready")
        cons_in, x_in, misc_in = sem("cons_in"), sem("x_in"), sem("misc_in")
        act_misc = sem("act_misc")
        dve_misc = sem("dve_misc")
        pe_misc = sem("pe_misc")
        coef_io, dist_io, bias_io = sem("coef_io"), sem("dist_io"), sem("bias_io")
        bb_ready = sem("bb_ready")
        acc_ready = sem("acc_ready")
        ada_mm = sem("ada_mm")
        xt_pe = sem("xt_pe")
        hf_ready = sem("hf_ready")
        staged = sem("staged")
        stored = sem("stored")
        ut_pe, ut_done = sem("ut_pe"), sem("ut_done")
        frac_ready = sem("frac_ready")
        trig_ready = sem("trig_ready")
        prod_ready = sem("prod_ready")
        bd_ready = sem("bd_ready")
        c_in = sem("c_in")
        cst_ready = sem("cst_ready")
        x_pe = sem("x_pe")
        x_used = sem("x_used")
        hcs_ready = sem("hcs_ready")
        y_pe = sem("y_pe")
        y_used = sem("y_used")
        tanh_in, tanh_out = sem("tanh_in"), sem("tanh_out")
        gelu_done = sem("gelu_done")
        qk_in, va_in, ba_in, za_in_s = sem("qk_in"), sem("va_in"), sem("ba_in"), sem("za_in_s")
        qk_pe, qk_sb, s_pe, s_max, p_exp = (sem(n) for n in ("qk_pe", "qk_sb", "s_pe", "s_max", "p_exp"))
        at_sb, at_pe, at_t, o_pe, o_ssq, ya_sb, ya_pe, yaT_sb = (
            sem(n) for n in ("at_sb", "at_pe", "at_t", "o_pe", "o_ssq", "ya_sb", "ya_pe", "yaT_sb"))
        gacc_ready, gate_pe, gate_row, gate_st = (
            sem(n) for n in ("gacc_ready", "gate_pe", "gate_row", "gate_st"))
        bg_in = sem("bg_in")
        zs_in, gt_pe, sig_done, ys_sb, ys_pe, feat_sb = (
            sem(n) for n in ("zs_in", "gt_pe", "sig_done", "ys_sb", "ys_pe", "feat_sb"))
        ga_in, gs_in, ga_sig, gs_sig, ga_used, m_sb, m_pe = (
            sem(n) for n in ("ga_in", "gs_in", "ga_sig", "gs_sig", "ga_used", "m_sb", "m_pe"))
        xg_in = [sem("xg_in0"), sem("xg_in1")]
        fg_in, o_sb, o_sq, f_rms, f_rstd, f_out, out_st = (
            sem(n) for n in ("fg_in", "o_sb", "o_sq", "f_rms", "f_rstd", "f_out", "out_st"))

        w_in_v = w_in.rearrange("(u t p) (b c) -> b u p t c", t=UT, p=P, c=CB)
        w_glu_v = w_glu.rearrange("(u t p) (b c) -> b u p t c", t=UT, p=P, c=CB)
        w_oss_v = w_oss.rearrange("(u t p) (b c) -> b u p t c", t=UT, p=P, c=CB)
        w_oat_v = w_oat.rearrange("(u t p) (b c) -> b u p t c", t=UT, p=P, c=CB)
        w_o_v = w_o.rearrange("(u t p) (b c) -> b u p t c", t=UT, p=P, c=CB)
        ada_v = w_ada.rearrange("(u t p) (b c) -> b u p t c", t=2, p=P, c=ADA_CB)
        proj_v = proj_d.rearrange("(h p) (b c) -> b p h c", p=P, c=CB)
        proj_h = proj_d.rearrange("(h p) (b c) -> b p h c", p=P, c=TOK)
        x_v = x.rearrange("(h p) (b c) -> b p h c", p=P, c=CB)
        out_v = out.rearrange("(h p) (b c) -> b p h c", p=P, c=CB)

        def rows(v, n):
            return bass.AP(v.tensor, 0, [[0, P], [1, n]])

        def at_block(v, b):
            if isinstance(b, int):
                return v[b]
            return v[bass.ds(b, 1)].rearrange("o p h c -> (o p) h c")

        def at_unit(v, b, u):
            if isinstance(b, int) and isinstance(u, int):
                return v[b, u]
            if isinstance(b, int):
                return v[b, bass.ds(u, 1)].rearrange("o p t c -> (o p) t c")
            if isinstance(u, int):
                return v[bass.ds(b, 1), u].rearrange("o p t c -> (o p) t c")
            return v[bass.ds(b, 1), bass.ds(u, 1)].rearrange("o q p t c -> (o q p) t c")

        raw_ada = raw[:, :, :, :].rearrange("p r t c -> p r (t c)").rearrange("p r (t c) -> p r t c", c=ADA_CB)

        def ring_ada(c, a):
            if c == 0:
                return a
            return 2 * ADA_UNITS + CH_R * (c - 1) + a + sum(at < a for at in W_AT)

        def ring_of(w):
            if w < BLK_0 * UPB:
                c, v = w // CH_W, w % CH_W
                return ring_ada(c + 1, W_AT[v]) + 1 if c < NC0 - 1 else 2 * ADA_UNITS + CH_R * c + v
            return R0 + w if w < W_C else (R0 + w + ADA_C if w >= W_D else None)

        block = ctx.enter_context(nc.Block())

        @block.sync
        def _(sp):
            sp.dma_start(ident[:, :], ident_in).then_inc(cons_in, 16)
            sp.dma_start(cact[:, :], c_col).then_inc(cons_in, 16)
            sp.dma_start(npar[:, 0:64], lam_re).then_inc(cons_in, 16)
            sp.dma_start(npar[:, 64:128], lam_im).then_inc(cons_in, 16)
            sp.dma_start(small[:, 0:1], log_dt).then_inc(cons_in, 16)

            def load(r, slot, dst, src):
                sp.wait_ge(raw_used, r + 1)
                sp.dma_start(dst, src).then_inc(raw_full[slot], 16)

            def load_unit(r, slot, src):
                load(r, slot, raw[:, slot, :, :], src)

            def load_ada(r, slot, src):
                load(r, slot, raw_ada[:, slot, :, :], src)

            def chunk_weight(c, v):
                r = ring_of(CH_W * c + v)
                load_unit(r, r % RING, w_in_v[v % BLK_0, c * 2 + v // BLK_0])

            for c in range(NC0):
                for a in range(2 * ADA_UNITS):
                    r = ring_ada(c, a)
                    load_ada(r, r % RING, ada_v[c + NC0 * (a // ADA_UNITS), a % ADA_UNITS])
                    if c and a in W_AT:
                        chunk_weight(c - 1, W_AT.index(a))
            for v in range(CH_W):
                chunk_weight(NC0 - 1, v)
            with sp.Fori(BLK_0, BLK_A + BLK_B) as b:
                for u in range(UPB):
                    load_unit(b * UPB + (R0 + u), u % RING, at_unit(w_in_v, b, u))
            with sp.Fori(0, HEADS // 2) as cb:
                for rr in range(2):
                    for v in range(2 * UPB):
                        loc = 24 * rr + v + (v + 1) // 2
                        load_unit(cb * 48 + (R0 + W_C + loc), loc % RING,
                                  at_unit(w_in_v, cb * 4 + (BLK_A + BLK_B + 2 * rr + v // UPB), v % UPB))
                        if v % 2 == 0:
                            load_ada(cb * 48 + (R0 + W_C + loc + 1), (loc + 1) % RING,
                                     at_unit(ada_v, cb + NADA, 8 * rr + v // 2))
            for w in range(W_D, W_E):
                r = ring_of(w)
                load_unit(r, r % RING, w_glu_v[(w - W_D) // UT, (w - W_D) % UT])
            with sp.Fori(0, 8) as j:
                for u in range(UPB):
                    v = w_oat_v if u < UT else w_oss_v
                    load_unit(j * UPB + (ring_of(W_E) + u), u % RING, at_unit(v, j, u % UT))
            with sp.Fori(0, 8) as j:
                for u in range(UPB):
                    load_unit(j * UPB + (ring_of(W_F) + u), u % RING, at_unit(w_o_v, j, u))
            sp.wait_ge(out_st, 16 * 8)

        @block.gpsimd
        def _(pool):
            pool.dma_start(tv[:, :], rows(tvals, TOK)).then_inc(misc_in, 16)
            pool.dma_start(gmask[:, :], gmask_in).then_inc(misc_in, 16)
            pool.dma_start(dcol[:, :], d_col).then_inc(misc_in, 16)
            pool.dma_start(g_sb[:, :], g_col).then_inc(misc_in, 16)
            pool.dma_start(ba_sb[:, :, :].rearrange("p a k -> p (a k)"), bada_col[:, 0:2 * KT]).then_inc(misc_in, 16)
            pool.dma_start(npar[:, 512:1024].rearrange("p (a d) -> p a d", a=4),
                           rows(lambdas, 4 * HD).rearrange("p (a d) -> p a d", a=4)).then_inc(misc_in, 16)
            for k, src in enumerate((b_re, b_im)):
                pool.dma_start(b_ld[:, k, :, :], src).then_inc(misc_in, 16)
            pool.dma_start(hf[0:32, 0, 0:1, :].rearrange("p a t -> p (a t)"), onehot).then_inc(misc_in, 16)
            pool.dma_start(hf[0:32, 1, 0, 0:HEADS], rel_bias).then_inc(misc_in, 16)

            nc.gpsimd.memset(small[:, 44:46], -0.5)
            pool.wait_ge(act_misc, 5)
            nc.gpsimd.tensor_scalar(small[:, 42:44], small[:, 40:42], 1.0 / D, EPS, ALU.mult, ALU.add)
            pool.drain()
            nc.gpsimd.tensor_tensor(small[:, 42:44], small[:, 42:44], small[:, 44:46], ALU.pow)
            pool.drain()
            for h in range(NH):
                ins = nc.gpsimd.tensor_scalar(xs[:, h, :], xs[:, h, :], small[:, 42 + h:43 + h], 1.0,
                                              ALU.mult, ALU.mult)
            ins.then_inc(x_scaled, 1)
            pool.wait_ge(dve_misc, 4)
            for k in range(2):
                pool.dma_start(coef_d[k], coef_l[:, 0, 6 + k, :]).then_inc(coef_io, 16)
            pool.wait_ge(coef_io, 32)
            pool.wait_ge(pe_misc, 1)
            for k in range(2):
                for e in range(8):
                    pool.dma_start(coef_l[e * GC:(e + 1) * GC, k, :, :],
                                   bass.AP(coef_d.tensor, k * G * ST + e * ST, [[0, GC], [8 * ST, 16], [1, ST]])
                                   ).then_inc(coef_io, 16)
            pool.wait_ge(dve_misc, 5)
            pool.dma_start(dist_d, hf[0:HEADS, 0, 1:3, :].rearrange("p a t -> p (a t)")).then_inc(dist_io, 16)
            pool.wait_ge(dist_io, 16)
            for h in range(HEADS):
                pool.dma_start(bass.AP(skew_d.tensor, h * P * 513, [[513, P], [1, 512]]),
                               bass.AP(dist_d.tensor, h * 512, [[0, P], [1, 512]])).then_inc(bias_io, 16)
            pool.wait_ge(coef_io, 32 + 16 * 16)
            pool.wait_ge(misc_in, 16 * 10)
            cre, cim = coef_l[:, 0, :, :], coef_l[:, 1, :, :]
            bre, bim = b_ld[:, 0, :, :], b_ld[:, 1, :, :]
            nc.gpsimd.tensor_tensor(bb[:, 0, :, :], cre, bre, ALU.mult)
            nc.gpsimd.tensor_tensor(bb[:, 1, :, :], cre, bim, ALU.mult)
            pool.drain()
            nc.gpsimd.tensor_tensor(bre, cim, bre, ALU.mult)
            nc.gpsimd.tensor_tensor(bim, cim, bim, ALU.mult)
            pool.drain()
            nc.gpsimd.tensor_tensor(bb[:, 0, :, :], bb[:, 0, :, :], bim, ALU.subtract)
            nc.gpsimd.tensor_tensor(bb[:, 1, :, :], bb[:, 1, :, :], bre, ALU.add).then_inc(bb_ready, 1)
            pool.drain()
            pool.wait_ge(hf_ready, UPB)
            pool.wait_ge(stat_ready, UPB)

            def map_load(s, buf):
                pool.dma_start(cst[:, buf, :, :, :].rearrange("p a b c -> p (a b c)"),
                               c_map[bass.ds(s, 1)].rearrange("o p n -> (o p) n")).then_inc(c_in, 16)

            def tables(i, j, first, last):
                s = i * 8 + j
                buf = j % 2
                late = not (first and j < 2)
                pool.wait_ge(prod_ready, s + 1)
                if late:
                    pool.wait_ge(trig_ready, s - 1)
                SU = FR[:, buf, :, :]
                nc.gpsimd.tensor_tensor(SU, PH[:, buf, :, :], LO[:, buf, :, :], ALU.add)
                pool.drain()
                nc.gpsimd.tensor_scalar(SU, SU, 1.0, ROUND, ALU.mult, ALU.add)
                pool.drain()
                nc.gpsimd.tensor_scalar(SU, SU, 1.0, -ROUND, ALU.mult, ALU.add)
                pool.drain()
                nc.gpsimd.tensor_tensor(SU, PH[:, buf, :, :], SU, ALU.subtract)
                pool.drain()
                nc.gpsimd.tensor_tensor(SU, SU, LO[:, buf, :, :], ALU.add)
                pool.drain()
                nc.gpsimd.tensor_scalar(SU, SU, BELOW_PI / (2 * PI), -BELOW_PI / (2 * PI),
                                        ALU.min, ALU.max).then_inc(frac_ready, 1)
                pool.wait_ge(c_in, (s + 1) * 16)
                for k in range(2):
                    m_k = cst[:, j % 4, :, k, :]
                    ins = nc.gpsimd.tensor_tensor(m_k, m_k, sgn[:, k:k + 1].unsqueeze(2).to_broadcast([P, 2, 32]),
                                                  ALU.mult)
                ins.then_inc(cst_ready, 1)
                if late:
                    pool.wait_ge(x_pe, s - 1)
                    pool.wait_ge(y_pe, s - 1)
                if not (last and j >= 6):
                    map_load(s + 2, (j + 2) % 4)
                q = j % 4
                sup = i * 2 + j // 4
                m = gmask[:, 2 * q:2 * q + 2].unsqueeze(2).to_broadcast([P, 2, ST])
                for k in range(2):
                    src = bb[:, k, bass.ds(sup, 1), :].to_broadcast([P, 2, ST])
                    nc.gpsimd.tensor_tensor(bd[:, buf, :, k, :], src, m, ALU.mult)
                pool.drain()
                nc.gpsimd.tensor_scalar(bd[:, buf, :, 2, :], bd[:, buf, :, 0, :], -1.0, 0.0,
                                        ALU.mult, ALU.add).then_inc(bd_ready, 1)

            map_load(0, 0)
            map_load(1, 1)
            for j in range(8):
                tables(0, j, True, False)
            with pool.Fori(1, 7) as i:
                for j in range(8):
                    tables(i, j, False, False)
            for j in range(8):
                tables(7, j, False, True)

            pool.wait_ge(gelu_done, 16)
            pool.wait_ge(bias_io, 16 * HEADS)
            skew_v = skew_d[:, 0:P * 512].rearrange("h (p j) -> h p j", j=512)
            pool.dma_start(subg, rows(subln_g, TOK)).then_inc(ba_in, 16)

            def head_loads(h, first):
                if not first:
                    pool.wait_ge(qk_pe, h)
                pool.wait_ge(stored, h * 16 + 16 * 19)
                qk = [(q_in, 16), (k_in, 24)]
                for dst, b0 in qk:
                    pool.dma_start(dst, at_block(proj_h, h + b0)).then_inc(qk_in, 16)
                if not first:
                    pool.wait_ge(s_max, h)
                sk = skew_v[h] if first else skew_v[bass.ds(h, 1)].rearrange("o p j -> (o p) j")
                for qb in range(NH):
                    start = TOK - 1 - P * qb
                    pool.dma_start(bias_in[:, qb, :], sk[:, start:start + TOK]).then_inc(ba_in, 16)
                if not first:
                    pool.wait_ge(o_pe, h)
                pool.dma_start(v_in, at_block(proj_h, h + 32)).then_inc(va_in, 16)
                if not first:
                    pool.wait_ge(ya_sb, h)
                pool.dma_start(za_in, at_block(proj_h, h + 40)).then_inc(za_in_s, 16)

            bg_v = bada_gate.rearrange("o (b c) -> b o c", c=ADA_CB)
            gate_v = gate_d.rearrange("o (b c) -> b o c", c=ADA_CB)

            def block_row(v, b):
                return v[b] if isinstance(b, int) else v[bass.ds(b, 1)].rearrange("q o c -> (q o) c")

            def gate_out(cb):
                pool.wait_ge(gate_row, cb + 1)
                pool.dma_start(block_row(gate_v, cb), grow[0:1, :]).then_inc(gate_st, 16)
                pool.wait_ge(gate_st, cb * 16 + 16)

            pool.dma_start(grow[0:1, :], bg_v[0]).then_inc(bg_in, 16)
            head_loads(0, True)
            with pool.Fori(0, HEADS // 2 - 1) as cb:
                head_loads(cb * 2 + 1, False)
                head_loads(cb * 2 + 2, False)
                gate_out(cb)
                pool.dma_start(grow[0:1, :], block_row(bg_v, cb + 1)).then_inc(bg_in, 16)
            head_loads(HEADS - 1, False)
            gate_out(HEADS // 2 - 1)

            pool.wait_ge(yaT_sb, HEADS)
            for j in range(4):
                if j:
                    pool.wait_ge(ys_sb, j)
                pool.dma_start(zs, at_block(proj_v, 4 + j)).then_inc(zs_in, 16)
            pool.wait_ge(ys_sb, 4)
            pool.wait_ge(stored, 16 * 36)
            for j in range(8):
                if j:
                    pool.wait_ge(ga_used, j)
                pool.dma_start(ga, at_block(proj_v, 32 + j)).then_inc(ga_in, 16)
                if j:
                    pool.wait_ge(m_sb, j)
                pool.dma_start(gs, at_block(proj_v, 24 + j)).then_inc(gs_in, 16)
            pool.wait_ge(m_pe, 8)
            for j in range(8):
                if j >= 2:
                    pool.wait_ge(o_sb, j - 1)
                pool.dma_start(xb[:, j % 2, :, :], x_v[j]).then_inc(xg_in[j % 2], 16)
                pool.dma_start(gate_b[:, j % 2, :], bass.AP(gate_d.tensor, j * CB, [[0, P], [1, CB]])
                               ).then_inc(xg_in[j % 2], 16)
                if j == 1:
                    pool.dma_start(fg, rows(final_g, D)).then_inc(fg_in, 16)

        @block.scalar
        def _(act):
            for h in range(NH):
                act.dma_start(xs[:, h, :], x[h * P:(h + 1) * P, :]).then_inc(x_in, 16)
            act.wait_ge(cons_in, 16 * 5)
            nc.scalar.activation(small[:, 1:2], small[:, 0:1], ACT.Exp)
            act.drain()
            nc.scalar.activation(npar[:, 128:192], npar[:, 0:64], ACT.Exp,
                                 scale=small[:, 1:2]).then_inc(act_misc, 1)
            nc.scalar.activation(coef_l[:, 0, 0, 0:KT], cact[:, :], ACT.Sigmoid).then_inc(act_misc, 1)
            act.wait_ge(dve_misc, 2)
            nc.scalar.activation(npar[:, 256:320], npar[:, 192:256], ACT.Sin)
            nc.scalar.activation(npar[:, 320:384], npar[:, 192:256], ACT.Abs)
            act.drain()
            nc.scalar.activation(npar[:, 384:448], npar[:, 320:384], ACT.Sin,
                                 scale=-1.0, bias=small[:, 2:3]).then_inc(act_misc, 1)
            act.wait_ge(dve_misc, 3)
            nc.scalar.activation(small[:, 5:7], small[:, 3:5], ACT.Exp).then_inc(act_misc, 1)
            act.wait_ge(x_in, 32)
            for h in range(NH):
                nc.scalar.activation(a_hi[:, 16 * h:16 * h + 16, :].rearrange("p k t -> p (k t)"), xs[:, h, :], ACT.Square,
                                     accum_out=small[:, 40 + h:41 + h])
            act.drain().then_inc(act_misc, 1)

            def high(w, slot, hb, full):
                act.wait_ge(raw_full[slot], full)
                if not (isinstance(w, int) and w < 2):
                    act.wait_ge(pe_used, w - 1)
                nc.scalar.activation(w_hi[:, hb, :, :], raw[:, slot, :, :], ACT.Copy).then_inc(h_done, 1)

            def turns(r):
                return (r // RING + 1) * 16

            def evac(b, par, pe_count, pair=None):
                act.wait_ge(pe_used, pe_count)
                pair = par if pair is None else pair
                for hh in range(NH):
                    last = nc.scalar.activation(stage[:, par, hh, :], bank[2 * pair + hh][:, :], ACT.Copy)
                last.then_inc(acc_free_a, 1)

            def store(b, par, n):
                act.wait_ge(acc_free_a, b + 1)
                if not (isinstance(n, int) and n == 0):
                    act.wait_ge(stored, n * 16)
                act.dma_start(at_block(proj_v, b), stage[:, par, :, :]).then_inc(stored, 16)

            def products(s, buf):
                for g in range(2):
                    col = s * 2 + g
                    for k, dst in enumerate((PH, LO)):
                        ph = rot[:, k, bass.ds(col, 1)] if not isinstance(col, int) else rot[:, k, col:col + 1]
                        ins = nc.scalar.activation(dst[:, buf, g, :], tv[:, :], ACT.Copy, scale=ph)
                ins.then_inc(prod_ready, 1)

            act.wait_ge(dist_io, 16)
            for c in range(NC0):
                act.wait_ge(mod_ready, c + 1)
                for gi in range(2):
                    g = c * 2 + gi
                    act.wait_ge(xt_pe, g + 1)
                    if g >= 2:
                        act.wait_ge(stat_ready, g - 1)
                    for t in range(UT):
                        k = UT * gi + t
                        last = nc.scalar.activation(hf[:, gi, t, :],
                                                    bank[6 + t // 2][:, TOK * (t % 2):TOK * (t % 2 + 1)],
                                                    ACT.Identity, scale=sc8[:, k:k + 1], bias=sh8[:, k:k + 1])
                    last.then_inc(hf_ready, 1)
                    for v in range(BLK_0 * gi, BLK_0 * (gi + 1)):
                        w = CH_W * c + v
                        high(w, ring_of(w) % RING, v % 2, turns(ring_of(w)))
            act.wait_ge(bb_ready, 1)
            for u in range(UPB):
                w = UPB * BLK_0 + u
                high(w, w % RING, w % 2, turns(R0 + w))
                if u == 0:
                    evac(0, 0, w - 2, 0)
                    evac(1, 1, w - 1, 1)
                if u == 4:
                    act.wait_ge(ut_pe, 1)
                    evac(2, 0, UPB * BLK_0, 2)
                if u in (5, 6):
                    products(u - 5, u - 5)

            def trig(i, j, first):
                s = i * 8 + j
                buf = j % 2
                act.wait_ge(frac_ready, s + 1)
                if not (first and j < 2):
                    act.wait_ge(hcs_ready, s - 1)
                nc.scalar.activation(FA, FR[:, buf, :, :], ACT.Abs)
                nc.scalar.activation(sinb[:, buf, :, :], FR[:, buf, :, :], ACT.Sin, scale=2 * PI)
                act.drain()
                nc.scalar.activation(cosb[:, buf, :, :], FA, ACT.Sin, scale=-2 * PI,
                                     bias=small[:, 2:3]).then_inc(trig_ready, 1)
                act.drain()

            def tanh(n):
                act.wait_ge(tanh_in, n)
                nc.scalar.activation(gl[:, 1, :], gl[:, 0, :], ACT.Tanh,
                                     scale=math.sqrt(2 / PI)).then_inc(tanh_out, 1)

            def act_b(i, first):
                for bl in range(2):
                    for u in range(UPB):
                        v = UPB * bl + u
                        w = i * 16 + (UPB * BLK_A + v)
                        high(w, v % RING, v % 2, i * 64 + turns(R0 + UPB * BLK_A + v))
                        if u == 1:
                            b = i * 2 + (BLK_A + bl - 1)
                            par = (bl + 1) % 2
                            if first and bl == 0:
                                act.wait_ge(ut_pe, 2)
                                evac(b, par, UPB * BLK_A)
                            else:
                                act.wait_ge(ut_pe, 3 if first else 4)
                                evac(b, par, i * 16 + UPB * (BLK_A + bl))
                                store(b, par, i * 2 + (bl - 1))
                        if v % 2:
                            act_pair(i, v // 2, first)

            def act_pair(i, j, first):
                trig(i, j, first)
                if not (isinstance(i, int) and i == 7 and j >= 6):
                    products(i * 8 + (j + 2), j % 2)
                if j == 2 and not first:
                    tanh(i * 2)
                if j == 6:
                    tanh(i * 2 + 1)

            act_b(0, True)
            with act.Fori(1, 7) as i:
                act_b(i, False)
            act_b(7, False)

            def plain_evac(b, par, nstored):
                evac(b, par, (b + 1) * UPB)
                store(b, par, nstored)

            for bl in range(4):
                for u in range(UPB):
                    w = UPB * (20 + bl) + u
                    high(w, u % RING, u % 2, turns(R0 + w))
                    if u == 1:
                        plain_evac(19 + bl, (19 + bl) % 2, 15 + bl)
                    if bl == 0 and u == 5:
                        tanh(16)

            def act_c(cb):
                for rr in range(2):
                    h1 = cb * 2 + (rr + 1)
                    for v in range(2 * UPB):
                        loc = 24 * rr + v + (v + 1) // 2
                        w = cb * 32 + (W_C + 16 * rr + v)
                        high(w, loc % RING, v % 2, cb * (48 * 4) + turns(R0 + W_C + loc))
                        if v % UPB == 1:
                            b = cb * 4 + (23 + 2 * rr + v // UPB)
                            plain_evac(b, (1 + v // UPB) % 2, cb * 4 + (19 + 2 * rr + v // UPB))
                        if v == 2:
                            act.wait_ge(qk_pe, h1)
                            nc.scalar.activation(qT.rearrange("p m t -> p (m t)"), bank[4][:, :], ACT.Copy,
                                                 scale=HD ** -0.5)
                            nc.scalar.activation(kT.rearrange("p m t -> p (m t)"), bank[5][:, :],
                                                 ACT.Copy).then_inc(qk_sb, 1)
                        if v == 6:
                            act.wait_ge(s_max, h1)
                            for qb in range(2):
                                for m in range(2):
                                    k = 2 * qb + m
                                    nc.scalar.activation(sc[:, qb, m, :], sc[:, qb, m, :], ACT.Exp,
                                                         bias=small[:, 16 + k:17 + k],
                                                         accum_out=small[:, 20 + k:21 + k])
                            act.wait_ge(za_in_s, h1 * 16)
                            nc.scalar.activation(szA, za_in, ACT.Sigmoid).then_inc(p_exp, 1)
                        if v == 10:
                            act.wait_ge(at_pe, h1)
                            nc.scalar.activation(aT.rearrange("p m t -> p (m t)"), bank[4][:, :],
                                                 ACT.Copy).then_inc(at_t, 1)
                        if v == 12:
                            act.wait_ge(o_pe, h1)
                            for qb in range(2):
                                nc.scalar.activation(aT[:, qb, :], bank[6 + qb][:, 0:TOK], ACT.Square,
                                                     accum_out=small[:, 28 + qb:29 + qb])
                            act.drain()
                            nc.scalar.activation(small[:, 30:32], small[:, 28:30], ACT.Sqrt, scale=1.0 / TOK,
                                                 bias=small[:, 60:61]).then_inc(o_ssq, 1)
                        if v == 15:
                            act.wait_ge(ya_pe, h1)
                            nc.scalar.activation(feat[:, bass.ds(cb * 4 + (16 + 2 * rr), 2), :].rearrange("p k t -> p (k t)"),
                                                 bank[5][:, :], ACT.Copy).then_inc(yaT_sb, 1)

            with act.Fori(0, HEADS // 2) as cb:
                act_c(cb)

            def sig_prev(j):
                act.wait_ge(pe_used, W_D + UT * (j + 1))
                if j:
                    act.wait_ge(ys_sb, j)
                for hh in range(NH):
                    last = nc.scalar.activation(sig[:, hh, :], bank[2 * (j % 2) + hh][:, :], ACT.Sigmoid)
                last.then_inc(acc_free_a, 1)
                act.wait_ge(zs_in, 16 * (j + 1))
                nc.scalar.activation(sz, zs, ACT.Sigmoid).then_inc(sig_done, 1)

            def ysT_copy(j):
                act.wait_ge(ys_pe, j + 1)
                for k in range(2):
                    last = nc.scalar.activation(ysT[:, 4 * j + 2 * k:4 * j + 2 * k + 2, :].rearrange("p k t -> p (k t)"),
                                                bank[6 + k][:, :], ACT.Copy)
                last.then_inc(feat_sb, 1)

            for j in range(4):
                for u in range(UT):
                    w = W_D + UT * j + u
                    high(w, w % RING, w % 2, turns(ring_of(w)))
                    if u == 1:
                        if j == 0:
                            plain_evac(39, 1, 35)
                        else:
                            sig_prev(j - 1)
                    if u == 3 and j:
                        ysT_copy(j - 1)

            def mT_copy(j):
                act.wait_ge(m_pe, j + 1)
                for k in range(2):
                    last = nc.scalar.activation(feat[:, 4 * j + 2 * k:4 * j + 2 * k + 2, :].rearrange("p k t -> p (k t)"),
                                                bank[4 + k][:, :], ACT.Copy)
                last.then_inc(feat_sb, 1)

            def gs_sigmoid(j):
                act.wait_ge(gs_in, 16 * (j + 1))
                nc.scalar.activation(gs, gs, ACT.Sigmoid).then_inc(gs_sig, 1)

            for j in range(8):
                for u in range(UPB):
                    w = W_E + UPB * j + u
                    high(w, w % RING, w % 2, turns(ring_of(w)))
                    if u == 1:
                        if j == 0:
                            sig_prev(3)
                        else:
                            gs_sigmoid(j - 1)
                    if u == 3:
                        if j == 0:
                            ysT_copy(3)
                        act.wait_ge(ga_in, 16 * (j + 1))
                        nc.scalar.activation(ga, ga, ACT.Sigmoid).then_inc(ga_sig, 1)
                    if u == 4 and j:
                        mT_copy(j - 1)

            def squares(j):
                act.wait_ge(o_sb, j + 1)
                for hh in range(NH):
                    last = nc.scalar.activation(junk[:, hh, :], obuf[:, hh, CB * j:CB * (j + 1)], ACT.Square,
                                                accum_out=small[:, 40 + 8 * hh + j:41 + 8 * hh + j])
                last.then_inc(o_sq, 1)
                act.drain()

            for j in range(8):
                for u in range(UPB):
                    w = W_F + UPB * j + u
                    high(w, w % RING, w % 2, turns(ring_of(w)))
                    if u == 1 and j == 0:
                        gs_sigmoid(7)
                    if u == 4:
                        if j == 0:
                            mT_copy(7)
                        else:
                            squares(j - 1)
            squares(7)
            act.wait_ge(f_rms, 1)
            nc.scalar.activation(small[:, 34:36], small[:, 32:34], ACT.Sqrt, scale=1.0 / D,
                                 bias=small[:, 7:8]).then_inc(f_rstd, 1)
            for j in range(8):
                act.wait_ge(f_out, j + 1)
                act.dma_start(out_v[j], obuf[:, :, CB * j:CB * (j + 1)]).then_inc(out_st, 16)

        @block.vector
        def _(dve):
            V = nc.vector

            def ada_unit(slot, full, acc, kt, first):
                dve.wait_ge(raw_full[slot], full)
                for t in range(2):
                    src, col = raw_ada[:, slot, t, :], kt + t
                    cc = cact[:, col:col + 1] if isinstance(col, int) else cact[:, bass.ds(col, 1)]
                    if first and t == 0:
                        ins = V.tensor_scalar(acc, src, cc, None, ALU.mult)
                    else:
                        ins = V.scalar_tensor_tensor(acc, src, cc, acc, ALU.mult, ALU.add)
                    if t:
                        ins.then_inc(raw_used, 1)
                    dve.drain()

            def ada(c, a0, a1):
                for a in range(a0, a1):
                    k, u = a // ADA_UNITS, a % ADA_UNITS
                    n, r = 2 * c + k, ring_ada(c, a)
                    if u == 0 and n >= 2:
                        dve.wait_ge(ada_mm, n - 1)
                    ada_unit(r % RING, 16 * (r // RING + 1), adacc[:, k, :], 2 * u, u == 0)
                    if u == ADA_UNITS - 1:
                        dve.drain().then_inc(acc_ready, 1)

            for _k in range(RING):
                V.memset(ones[:, _k:_k + 1], 1.0).then_inc(raw_used, 1)
            V.memset(sgn[:, :], -1.0)
            dve.drain()
            V.memset(sgn[0:ST, 0:1], 1.0)
            V.memset(small[:, 2:3], PI / 2)
            V.memset(small[:, 7:8], 1e-6)
            V.memset(small[:, 60:61], 1e-5).then_inc(dve_misc, 1)
            dve.wait_ge(act_misc, 2)
            n = lambda k: npar[:, 64 * k:64 * (k + 1)]
            lr, li, mag, red, sn, ab, cs = n(0), n(1), n(2), n(3), n(4), n(5), n(6)
            V.tensor_tensor(cact[:, :], cact[:, :], coef_l[:, 0, 0, 0:KT], ALU.mult)
            V.tensor_scalar(red, li, small[:, 1:2], None, ALU.mult)
            dve.drain()
            V.tensor_scalar(ab, red, 1 / (2 * PI), ROUND, ALU.mult, ALU.add)
            dve.drain()
            V.tensor_scalar(ab, ab, ROUND, None, ALU.subtract)
            dve.drain()
            for cw in (CW1, CW2, CW3):
                V.scalar_tensor_tensor(red, ab, -cw, red, ALU.mult, ALU.add)
                dve.drain()
            V.tensor_scalar(red, red, BELOW_PI, -BELOW_PI, ALU.min, ALU.max).then_inc(dve_misc, 1)
            ada(0, 0, 4)
            dve.wait_ge(misc_in, 16 * 10)
            lam = npar[:, 512:1024].rearrange("p (a d) -> p a d", a=4)
            for k in range(2):
                V.tensor_tensor(lam[:, 2 * k, :], lam[:, 2 * k, :], lam[:, 2 * k + 1, :], ALU.mult)
            dve.drain()
            V.tensor_reduce(small[:, 3:5], lam[:, 0::2, :], AX.X, ALU.add).then_inc(dve_misc, 1)
            dve.wait_ge(act_misc, 3)
            abre, abim, den, num, t0, t1 = cs, sn, coef_l[:, 0, 2, :], coef_l[:, 0, 3, :], coef_l[:, 0, 4, :], coef_l[:, 0, 5, :]
            cre, cim, ph = coef_l[:, 0, 6, :], coef_l[:, 0, 7, :], coef_l[:, 1, 0:6, :].rearrange("p (a b) s -> p a (b s)", a=3)
            V.tensor_tensor(abre, mag, cs, ALU.mult)
            V.tensor_tensor(abim, mag, sn, ALU.mult)
            V.tensor_tensor(den, lr, lr, ALU.mult)
            V.tensor_tensor(t0, li, li, ALU.mult)
            dve.drain()
            V.tensor_tensor(den, den, t0, ALU.add)
            V.tensor_scalar(num, abre, 1.0, None, ALU.subtract)
            dve.drain()
            V.reciprocal(den, den)
            V.tensor_tensor(cre, num, lr, ALU.mult)
            V.tensor_tensor(t0, abim, li, ALU.mult)
            V.tensor_tensor(cim, abim, lr, ALU.mult)
            V.tensor_tensor(t1, num, li, ALU.mult)
            dve.drain()
            V.tensor_tensor(cre, cre, t0, ALU.add)
            V.tensor_tensor(cim, cim, t1, ALU.subtract)
            dve.drain()
            V.tensor_tensor(cre, cre, den, ALU.mult)
            V.tensor_tensor(cim, cim, den, ALU.mult)
            V.tensor_scalar(red, red, 1 / (2 * PI), None, ALU.mult)
            dve.drain()
            V.tensor_scalar(ab, red, ROUND16, None, ALU.add)
            dve.drain()
            for half in range(2):
                V.tensor_scalar(ph[:, 0, ST * half:ST * (half + 1)], ab, ROUND16, None, ALU.subtract)
                V.tensor_copy(ph[:, 2, ST * half:ST * (half + 1)], mag)
            dve.drain()
            for half in range(2):
                last = V.tensor_tensor(ph[:, 1, ST * half:ST * (half + 1)], red, ph[:, 0, 0:ST], ALU.subtract)
            last.then_inc(dve_misc, 1)
            ada(0, 4, 8)
            dve.wait_ge(pe_misc, 1)
            V.tensor_copy(rot[:, :, :].rearrange("p a g -> p (a g)"), bank[1][:, 0:3 * G])
            V.tensor_copy(hf[0:HEADS, 0, 1, :], bank[2][0:HEADS, 0:TOK])
            V.memset(hf[0:HEADS, 0, 2, :], NEG)
            dve.wait_ge(act_misc, 4)
            dve.drain()
            V.tensor_tensor(small[:, 5:6], small[:, 6:7], small[:, 5:6], ALU.subtract)
            dve.drain()
            V.tensor_scalar(small[:, 6:7], small[:, 5:6], LAM_INIT, None, ALU.subtract).then_inc(dve_misc, 1)

            def low(w, slot, hb):
                dve.wait_ge(h_done, w + 1)
                V.tensor_tensor(w_lo[:, hb, :, :], raw[:, slot, :, :], w_hi[:, hb, :, :].bitcast(F32),
                                ALU.subtract).then_inc(raw_used, 1)

            def split(src, k0, pe_count):
                if pe_count:
                    dve.wait_ge(pe_used, pe_count)
                V.tensor_copy(a_hi[:, k0:k0 + UT, :], src)
                dve.drain()
                V.tensor_tensor(a_lo[:, k0:k0 + UT, :], src, a_hi[:, k0:k0 + UT, :].bitcast(F32),
                                ALU.subtract).then_inc(stat_ready, 1)

            def ut_copy(b):
                dve.wait_ge(ut_pe, b + 1)
                for k in range(2):
                    last = V.tensor_copy(feat[:, 4 * b + 2 * k:4 * b + 2 * k + 2, :].rearrange("p k t -> p (k t)"),
                                         bank[6 + k][:, :])
                last.then_inc(ut_done, 1)

            def columns(c):
                dve.wait_ge(ada_mm, 2 * c + 2)
                if c:
                    dve.wait_ge(hf_ready, 2 * c)
                at8 = slice(8 * c, 8 * c + 8)
                V.tensor_tensor(sh8[:, :], bank[7][:, 0:8], ba_sb[:, 0, at8], ALU.add)
                V.tensor_tensor(sc8[:, :], bank[7][:, 8:16], ba_sb[:, 1, at8], ALU.add)
                dve.drain()
                V.scalar_tensor_tensor(sc8[:, :], sc8[:, :], 1.0, g_sb[:, at8], ALU.add,
                                       ALU.mult).then_inc(mod_ready, 1)

            def group(g):
                dve.wait_ge(hf_ready, g + 1)
                split(hf[:, g % 2, :, :], UT * g, 0)

            def chunk_low(c, v):
                w = CH_W * c + v
                low(w, ring_of(w) % RING, v % 2)

            ada(0, 8, 2 * ADA_UNITS)
            for c in range(1, NC0):
                ada(c, 0, 1)
                columns(c - 1)
                ada(c, 1, 3)
                group(2 * c - 2)
                done = 3
                for v in range(CH_W):
                    ada(c, done, W_AT[v] + 1)
                    chunk_low(c - 1, v)
                    done = W_AT[v] + 1
                    if v == BLK_0 - 1:
                        group(2 * c - 1)
                ada(c, done, 2 * ADA_UNITS)
            columns(NC0 - 1)
            for gi in range(2):
                group(2 * NC0 - 2 + gi)
                for v in range(BLK_0 * gi, BLK_0 * (gi + 1)):
                    chunk_low(NC0 - 1, v)

            for u in range(UPB):
                low(UPB * BLK_0 + u, u % RING, u % 2)
                if u in (3, 5, 7):
                    ut_copy((u - 3) // 2)

            def scan_pair(s, buf, first):
                dve.wait_ge(trig_ready, s + 1)
                dve.wait_ge(x_pe, s + 1)
                bx = [bank[4 + k][:, :].rearrange("p (a t) -> p a t", a=2) for k in range(2)]
                V.tensor_tensor(T1, bx[0], cosb[:, buf, :, :], ALU.mult)
                V.tensor_tensor(T2, bx[1], sinb[:, buf, :, :], ALU.mult).then_inc(x_used, 1)
                dve.drain()
                V.tensor_tensor(T1, T1, T2, ALU.add)
                dve.drain()
                for g in range(2):
                    col = s * 2 + g
                    r = rot[:, 2, bass.ds(col, 1)] if not isinstance(col, int) else rot[:, 2, col:col + 1]
                    V.tensor_tensor_scan(HH[:, g, :], r.to_broadcast([P, TOK]), T1[:, g, :], 0.0,
                                         ALU.mult, ALU.add)
                dve.drain()
                if not first:
                    dve.wait_ge(y_pe, s - 1)
                V.tensor_tensor(hcb[:, buf, :, :], HH, cosb[:, buf, :, :], ALU.mult)
                V.tensor_tensor(hsb[:, buf, :, :], HH, sinb[:, buf, :, :], ALU.mult).then_inc(hcs_ready, 1)

            def y_evac(sup):
                dve.wait_ge(y_pe, sup * 4 + 4)
                if isinstance(sup, int):
                    f, dd = feat[:, sup:sup + 1, :].rearrange("p k t -> p (k t)"), dcol[:, sup:sup + 1]
                else:
                    f, dd = feat[:, bass.ds(sup, 1), :].rearrange("p k t -> p (k t)"), dcol[:, bass.ds(sup, 1)]
                V.scalar_tensor_tensor(gl[:, 2, :], f, dd, bank[6][:, 0:TOK], ALU.mult, ALU.add).then_inc(y_used, 1)
                dve.drain()
                V.tensor_tensor(gl[:, 0, :], gl[:, 2, :], gl[:, 2, :], ALU.mult)
                dve.drain()
                V.tensor_scalar(gl[:, 0, :], gl[:, 0, :], 0.044715, 1.0, ALU.mult, ALU.add)
                dve.drain()
                V.tensor_tensor(gl[:, 0, :], gl[:, 0, :], gl[:, 2, :], ALU.mult).then_inc(tanh_in, 1)

            def y_gelu(sup):
                dve.wait_ge(tanh_out, sup + 1)
                f = (feat[:, sup:sup + 1, :] if isinstance(sup, int) else feat[:, bass.ds(sup, 1), :]
                     ).rearrange("p k t -> p (k t)")
                V.scalar_tensor_tensor(gl[:, 0, :], gl[:, 1, :], 1.0, gl[:, 2, :], ALU.add, ALU.mult)
                dve.drain()
                V.tensor_scalar(f, gl[:, 0, :], 0.5, None, ALU.mult).then_inc(gelu_done, 1)
                dve.drain()

            def dve_b(i, first):
                for v in range(2 * UPB):
                    low(i * 16 + (UPB * BLK_A + v), v % RING, v % 2)
                    if first and v == 3:
                        ut_copy(3)
                    if v % 2:
                        j = v // 2
                        if not (first and j == 0):
                            scan_pair(i * 8 + (j - 1), (j - 1) % 2, first and j <= 2)
                        if j == 5:
                            y_evac(i * 2)
                        if j == 6:
                            y_gelu(i * 2)
                        if j == 1 and not first:
                            y_evac(i * 2 - 1)
                        if j == 2 and not first:
                            y_gelu(i * 2 - 1)

            dve_b(0, True)
            with dve.Fori(1, 8) as i:
                dve_b(i, False)
            for bl in range(4):
                for u in range(UPB):
                    w = UPB * (20 + bl) + u
                    low(w, u % RING, u % 2)
                    if bl == 0:
                        if u == 1:
                            scan_pair(63, 1, False)
                        if u == 3:
                            y_evac(15)
                        if u == 6:
                            y_gelu(15)

            with dve.Fori(0, HEADS // 2) as cb:
                for rr in range(2):
                    h1 = cb * 2 + (rr + 1)
                    for v in range(2 * UPB):
                        loc = 24 * rr + v + (v + 1) // 2
                        low(cb * 32 + (W_C + 16 * rr + v), loc % RING, v % 2)
                        if v % 2 == 0:
                            first = rr == 0 and v == 0
                            rl = R0 + W_C + loc + 1
                            ada_unit(rl % RING, cb * (48 * 4) + 16 * (rl // RING + 1), gacc,
                                     2 * (8 * rr + v // 2), first)
                            if rr == 1 and v == 14:
                                dve.drain().then_inc(gacc_ready, 1)
                        if v == 5:
                            dve.wait_ge(s_pe, h1)
                            dve.wait_ge(ba_in, h1 * 32 + 16)
                            for qb in range(2):
                                V.tensor_tensor(sc[:, qb, :, :], bank[6 + qb][:, :].rearrange("p (m k) -> p m k", m=2),
                                                bias_in[:, qb:qb + 1, :].to_broadcast([P, 2, TOK]), ALU.add)
                            dve.drain()
                            V.tensor_reduce(small[:, 16:20], sc.rearrange("p q m k -> p (q m) k"), AX.X, ALU.max)
                            dve.drain()
                            V.tensor_scalar(small[:, 16:20], small[:, 16:20], -1.0, None, ALU.mult).then_inc(s_max, 1)
                        if v == 7:
                            dve.wait_ge(p_exp, h1)
                            V.reciprocal(small[:, 24:28], small[:, 20:24])
                            dve.drain()
                            for qb in range(2):
                                k = 25 + 2 * qb
                                V.tensor_tensor(small[:, k:k + 1], small[:, k:k + 1], small[:, 6:7], ALU.mult)
                            dve.drain()
                            for qb in range(2):
                                V.tensor_scalar(sc[:, qb, 0, :], sc[:, qb, 0, :], small[:, 24 + 2 * qb:25 + 2 * qb],
                                                None, ALU.mult)
                            dve.drain()
                            for qb in range(2):
                                last = V.scalar_tensor_tensor(at[:, qb, :], sc[:, qb, 1, :],
                                                              small[:, 25 + 2 * qb:26 + 2 * qb], sc[:, qb, 0, :],
                                                              ALU.mult, ALU.add)
                            last.then_inc(at_sb, 1)
                        if v == 13:
                            dve.wait_ge(o_ssq, h1)
                            V.reciprocal(small[:, 36:38], small[:, 30:32])
                            V.tensor_tensor(szA, szA, za_in, ALU.mult)
                            dve.drain()
                            V.tensor_scalar(small[:, 36:38], small[:, 36:38], 1.0 - LAM_INIT, None, ALU.mult)
                            V.tensor_tensor(szA, szA, subg.unsqueeze(1).to_broadcast([P, 2, TOK]), ALU.mult)
                            dve.drain()
                            for qb in range(2):
                                last = V.scalar_tensor_tensor(ya[:, qb, :], bank[6 + qb][:, 0:TOK],
                                                              small[:, 36 + qb:37 + qb], szA[:, qb, :],
                                                              ALU.mult, ALU.mult)
                            last.then_inc(ya_sb, 1)
                dve.wait_ge(gate_pe, cb + 1)
                dve.wait_ge(bg_in, cb * 16 + 16)
                for k in range(2):
                    g_row = grow[0:1, CB * k:CB * (k + 1)]
                    last = V.tensor_tensor(g_row, g_row, bank[(4, 7)[k]][0:1, :], ALU.add)
                last.then_inc(gate_row, 1)

            def ys_prev(j):
                dve.wait_ge(sig_done, j + 1)
                dve.wait_ge(gt_pe, j + 1)
                if j:
                    dve.wait_ge(ys_pe, j)
                else:
                    dve.wait_ge(gate_st, 16 * 4)
                V.tensor_tensor(ys, zs, sz, ALU.mult)
                for hh in range(NH):
                    V.tensor_tensor(sig[:, hh, :], bank[4 + hh][:, :], sig[:, hh, :], ALU.mult)
                dve.drain()
                V.tensor_tensor(ys, ys, sig, ALU.mult).then_inc(ys_sb, 1)

            for j in range(4):
                for u in range(UT):
                    w = W_D + UT * j + u
                    if j == 0:
                        split(feat[:, UT * u:UT * (u + 1), :], UT * u, W_D - UPB + u + 1)
                    low(w, w % RING, w % 2)
                    if u == 1 and j:
                        ys_prev(j - 1)

            def merge_prev(j):
                dve.wait_ge(pe_used, W_E + UPB * (j + 1))
                dve.wait_ge(gs_sig, j + 1)
                if j:
                    dve.wait_ge(m_pe, j)
                for hh in range(NH):
                    last = V.tensor_tensor(mrg[:, hh, :], bank[2 + hh][:, :], gs[:, hh, :], ALU.mult)
                last.then_inc(acc_free_v, 1)
                dve.drain()
                V.tensor_tensor(mrg, mrg, part, ALU.add).then_inc(m_sb, 1)
                dve.drain()

            for j in range(8):
                for u in range(UPB):
                    w = W_E + UPB * j + u
                    if j == 0 and u < UT:
                        split(feat[:, 16 + UT * u:16 + UT * (u + 1), :], UT * u, W_E - UT + u + 1)
                    elif j == 0:
                        k = u - UT
                        dve.wait_ge(feat_sb, k + 1)
                        split(ysT[:, UT * k:UT * (k + 1), :], 16 + UT * k, 0)
                    low(w, w % RING, w % 2)
                    if u == 1:
                        if j == 0:
                            ys_prev(3)
                        else:
                            merge_prev(j - 1)
                    if u == 5:
                        dve.wait_ge(pe_used, W_E + UPB * j + UT)
                        dve.wait_ge(ga_sig, j + 1)
                        for hh in range(NH):
                            last = V.tensor_tensor(part[:, hh, :], bank[hh][:, :], ga[:, hh, :], ALU.mult)
                        last.then_inc(acc_free_v, 1)
                        dve.drain().then_inc(ga_used, 1)

            def out_prev(j):
                dve.wait_ge(pe_used, W_F + UPB * (j + 1))
                dve.wait_ge(xg_in[j % 2], 32 * (j // 2 + 1))
                o = [obuf[:, hh, CB * j:CB * (j + 1)] for hh in range(NH)]
                for hh in range(NH):
                    last = V.tensor_tensor(o[hh], bank[2 * (j % 2) + hh][:, :], gate_b[:, j % 2, :], ALU.mult)
                last.then_inc(acc_free_v, 1)
                dve.drain()
                for hh in range(NH):
                    last = V.tensor_tensor(o[hh], o[hh], xb[:, j % 2, hh, :], ALU.add)
                last.then_inc(o_sb, 1)

            for j in range(8):
                for u in range(UPB):
                    w = W_F + UPB * j + u
                    if j == 0:
                        dve.wait_ge(feat_sb, 4 + u + 1)
                        split(feat[:, UT * u:UT * (u + 1), :], UT * u, W_F - UPB + u + 1)
                    low(w, w % RING, w % 2)
                    if u == 1:
                        if j == 0:
                            merge_prev(7)
                        else:
                            out_prev(j - 1)
            out_prev(7)
            dve.wait_ge(o_sq, 8)
            V.tensor_reduce(small[:, 32:34], small[:, 40:56].rearrange("p (h j) -> p h j", h=2), AX.X,
                            ALU.add).then_inc(f_rms, 1)
            dve.wait_ge(f_rstd, 1)
            V.reciprocal(small[:, 36:38], small[:, 34:36])
            dve.drain()
            dve.wait_ge(fg_in, 16)
            for j in range(8):
                for hh in range(NH):
                    o = obuf[:, hh, CB * j:CB * (j + 1)]
                    last = V.scalar_tensor_tensor(o, o, small[:, 36 + hh:37 + hh], fg[:, CB * j:CB * (j + 1)],
                                                  ALU.mult, ALU.mult)
                last.then_inc(f_out, 1)

        @block.tensor
        def _(pe):
            T = nc.tensor

            pe.wait_ge(cons_in, 16 * 5)
            pe.wait_ge(dve_misc, 4)
            ph = coef_l[:, 1, 0:6, :].rearrange("p (a b) s -> p a (b s)", a=3)
            for k in range(3):
                T.transpose(bank[1][:, G * k:G * (k + 1)], ph[:, k, :], ident[:, :])
            pe.wait_ge(misc_in, 16 * 10)
            T.matmul(bank[2][0:HEADS, 0:TOK], hf[0:32, 1, 0, 0:HEADS],
                     hf[0:32, 0, 0, :], start=True, stop=True).then_inc(pe_misc, 1)
            def unit(w, ring, hb, k0, pair, first, last, stat):
                pe.wait_ge(raw_used, ring + (RING + 1))
                if stat:
                    pe.wait_ge(stat_ready, stat)
                for t in range(UT):
                    for hh in range(NH):
                        acc = bank[2 * pair + hh][:, :]
                        cols = slice(P * hh, P * (hh + 1))
                        s_hi, s_lo = a_hi[:, k0 + t, cols], a_lo[:, k0 + t, cols]
                        T.matmul(acc, s_hi, w_hi[:, hb, t, :], start=first and t == 0, stop=False)
                        T.matmul(acc, s_hi, w_lo[:, hb, t, :], start=False, stop=False)
                        ins = T.matmul(acc, s_lo, w_hi[:, hb, t, :], start=False, stop=last and t == UT - 1)
                ins.then_inc(pe_used, 1)

            def acc_wait(a):
                if not (isinstance(a, int) and a < 2):
                    pe.wait_ge(acc_free_a, a - 1)

            def xt(g):
                if g:
                    pe.wait_ge(hf_ready, g)
                for t in range(UT):
                    kt = UT * g + t
                    for h in range(NH):
                        o = TOK * (t % 2) + P * h
                        last = T.transpose(bank[6 + t // 2][:, o:o + P], xs[:, h, P * kt:P * (kt + 1)], ident[:, :])
                last.then_inc(xt_pe, 1)

            def ut(b):
                pe.wait_ge(acc_free_a, b + 1)
                if b:
                    pe.wait_ge(ut_done, b)
                for t in range(UT):
                    for h in range(NH):
                        o = TOK * (t % 2) + P * h
                        last = T.transpose(bank[6 + t // 2][:, o:o + P], stage[:, b % 2, h, P * t:P * (t + 1)], ident[:, :])
                last.then_inc(ut_pe, 1)

            for c in range(NC0):
                if c:
                    pe.wait_ge(hf_ready, 2 * c)
                for n in range(2):
                    pe.wait_ge(acc_ready, 2 * c + n + 1)
                    for k in range(ADA_CB // P):
                        last = T.matmul(bank[7][:, 8 * n + k:8 * n + k + 1], adacc[:, n, P * k:P * (k + 1)],
                                        ones[:, 0:1], start=True, stop=True)
                    last.then_inc(ada_mm, 1)
                pe.wait_ge(x_scaled, 1)
                pe.wait_ge(mod_ready, c + 1)
                for v in range(CH_W):
                    g, w = 2 * c + v // BLK_0, CH_W * c + v
                    if v == 0:
                        xt(g)
                    if v == 1:
                        xt(g + 1)
                    unit(w, ring_of(w), w % 2, UT * g, v % BLK_0, g == 0, g == UPB - 1, g + 1)

            acc_wait(BLK_0)
            for u in range(UPB):
                w = UPB * BLK_0 + u
                unit(w, ring_of(w), w % 2, UT * u, BLK_0 % 2, u == 0, u == UPB - 1, 0)
                if u in (1, 3, 5):
                    ut((u - 1) // 2)

            def x_mm(s, sup, j, first):
                buf = j % 2
                pe.wait_ge(bd_ready, s + 1)
                if not (first and j == 0):
                    pe.wait_ge(x_used, s)
                for k in range(2):
                    for g in range(2):
                        u_t = (feat[:, bass.ds(sup, 1), :] if not isinstance(sup, int)
                               else feat[:, sup:sup + 1, :]).rearrange("p k t -> p (k t)")
                        last = T.matmul(bank[4 + k][:, TOK * g:TOK * (g + 1)],
                                        bd[:, buf, g, k:k + 2, :].rearrange("p a s -> p (a s)"), u_t,
                                        start=True, stop=True)
                last.then_inc(x_pe, 1)

            def y_mm(s, q, buf, sup_wait):
                pe.wait_ge(hcs_ready, s + 1)
                pe.wait_ge(cst_ready, s + 1)
                if sup_wait is not None:
                    pe.wait_ge(y_used, sup_wait)
                k = 0
                for g in range(2):
                    for m, hb in enumerate((hcb, hsb)):
                        last = T.matmul(bank[6][32 * q:32 * q + 32, 0:TOK], cst[:, q, g, m, :], hb[:, buf, g, :],
                                        start=k == 0, stop=k == 3)
                        k += 1
                last.then_inc(y_pe, 1)

            def pe_b(i, first):
                for v in range(2 * UPB):
                    bl, u = v // UPB, v % UPB
                    if u == 0:
                        acc_wait(i * 2 + (BLK_A + bl))
                    w = i * 16 + (UPB * BLK_A + v)
                    unit(w, w + R0, v % 2, UT * u, bl, u == 0, u == UPB - 1, 0)
                    j = v // 2
                    if first and v == 2:
                        ut(3)
                    if v % 2 == 0:
                        if first and j == 4:
                            pe.wait_ge(ut_done, 4)
                        x_mm(i * 8 + j, i * 2 + j // 4, j, first)
                    elif not (first and j == 0):
                        if first and j == 1:
                            pe.wait_ge(ut_done, 4)
                        wait = None
                        if j == 5:
                            wait = i * 2 + 1
                        if j == 1 and not first:
                            wait = i * 2
                        y_mm(i * 8 + (j - 1), (j - 1) % 4, (j - 1) % 2, wait)

            pe_b(0, True)
            with pe.Fori(1, 8) as i:
                pe_b(i, False)
            for bl in range(4):
                acc_wait(20 + bl)
                for u in range(UPB):
                    w = UPB * (20 + bl) + u
                    unit(w, w + R0, u % 2, UT * u, bl % 2, u == 0, u == UPB - 1, 0)
                    if bl == 0 and u == 1:
                        y_mm(63, 3, 1, None)

            with pe.Fori(0, HEADS // 2) as cb:
                for rr in range(2):
                    h1 = cb * 2 + (rr + 1)
                    for v in range(2 * UPB):
                        bl, u = v // UPB, v % UPB
                        loc = 24 * rr + v + (v + 1) // 2
                        if u == 0:
                            acc_wait(cb * 4 + (24 + 2 * rr + bl))
                        unit(None, cb * 48 + (R0 + W_C + loc), v % 2, UT * u, bl, u == 0, u == UPB - 1, 0)
                        if v == 0:
                            pe.wait_ge(qk_in, h1 * 32)
                            for src, pb in ((q_in, bank[4]), (k_in, bank[5])):
                                for m in range(2):
                                    for h in range(NH):
                                        last = T.transpose(pb[:, TOK * m + P * h:TOK * m + P * (h + 1)],
                                                           src[:, h, P * m:P * (m + 1)], ident[:, :])
                            last.then_inc(qk_pe, 1)
                        if v == 3:
                            pe.wait_ge(qk_sb, h1)
                            for qb in range(2):
                                for m in range(2):
                                    last = T.matmul(bank[6 + qb][:, TOK * m:TOK * (m + 1)],
                                                    qT[:, m, P * qb:P * (qb + 1)], kT[:, m, :], start=True, stop=True)
                            last.then_inc(s_pe, 1)
                        if v == 8:
                            pe.wait_ge(at_sb, h1)
                            for kk in range(2):
                                for qb in range(2):
                                    last = T.transpose(bank[4][:, TOK * kk + P * qb:TOK * kk + P * (qb + 1)],
                                                       at[:, qb, P * kk:P * (kk + 1)], ident[:, :])
                            last.then_inc(at_pe, 1)
                        if v == 10:
                            pe.wait_ge(at_t, h1)
                            pe.wait_ge(va_in, h1 * 16)
                            for qb in range(2):
                                for kk in range(2):
                                    last = T.matmul(bank[6 + qb][:, 0:TOK], aT[:, kk, P * qb:P * (qb + 1)],
                                                    v_in[:, kk, :], start=kk == 0, stop=kk == 1)
                            last.then_inc(o_pe, 1)
                        if v == 13:
                            pe.wait_ge(ya_sb, h1)
                            for ct in range(2):
                                for h in range(NH):
                                    last = T.transpose(bank[5][:, TOK * ct + P * h:TOK * ct + P * (h + 1)],
                                                       ya[:, h, P * ct:P * (ct + 1)], ident[:, :])
                            last.then_inc(ya_pe, 1)
                        if rr == 1 and v == 14:
                            pe.wait_ge(gacc_ready, cb + 1)
                            for k in range(2):
                                last = T.matmul(bank[(4, 7)[k]][0:1, :], ones[:, 0:1], gacc[:, CB * k:CB * (k + 1)],
                                                start=True, stop=True)
                            last.then_inc(gate_pe, 1)

            def ysT_t(j):
                pe.wait_ge(ys_sb, j + 1)
                if j:
                    pe.wait_ge(feat_sb, j)
                for t in range(UT):
                    for h in range(NH):
                        o = TOK * (t % 2) + P * h
                        last = T.transpose(bank[6 + t // 2][:, o:o + P], ys[:, h, P * t:P * (t + 1)], ident[:, :])
                last.then_inc(ys_pe, 1)

            for j in range(4):
                acc_wait(40 + j)
                for u in range(UT):
                    w = W_D + UT * j + u
                    unit(w, ring_of(w), u % 2, UT * u, j % 2, u == 0, u == UT - 1, 8 + u + 1 if j == 0 else 0)
                    if u == 2 and j:
                        ysT_t(j - 1)
                    if u == 3:
                        if j == 0:
                            pe.wait_ge(yaT_sb, HEADS)
                            pe.wait_ge(gate_row, 4)
                        else:
                            pe.wait_ge(ys_sb, j)
                        for h in range(NH):
                            for t in range(UT):
                                last = T.transpose(bank[4 + h][:, P * t:P * (t + 1)],
                                                   feat[:, 4 * j + t, P * h:P * (h + 1)], ident[:, :])
                        last.then_inc(gt_pe, 1)

            def mT_t(j):
                pe.wait_ge(m_sb, j + 1)
                pe.wait_ge(feat_sb, j + 4)
                for t in range(UT):
                    for h in range(NH):
                        o = TOK * (t % 2) + P * h
                        last = T.transpose(bank[4 + t // 2][:, o:o + P], mrg[:, h, P * t:P * (t + 1)], ident[:, :])
                last.then_inc(m_pe, 1)

            def pe_e(j):
                for u in range(UPB):
                    if u % UT == 0:
                        if isinstance(j, int):
                            acc_wait(44 + u // UT)
                        else:
                            pe.wait_ge(acc_free_v, j * 2 + (u // UT - 1))
                    unit(None, j * UPB + (ring_of(W_E) + u), u % 2, UT * u, u // UT, u % UT == 0, u % UT == UT - 1,
                         12 + u + 1 if isinstance(j, int) else 0)
                    if u == 2:
                        if isinstance(j, int):
                            ysT_t(3)
                        else:
                            mT_t(j - 1)

            pe_e(0)
            with pe.Fori(1, 8) as j:
                pe_e(j)

            def pe_f(j, par, first):
                pe.wait_ge(acc_free_v, j + 15)
                for u in range(UPB):
                    unit(None, j * UPB + (ring_of(W_F) + u), u % 2, UT * u, par, u == 0, u == UPB - 1,
                         20 + u + 1 if first else 0)
                    if u == 2 and first:
                        mT_t(7)

            pe_f(0, 0, True)
            pe_f(1, 1, False)
            with pe.Fori(1, 4) as i:
                for par in range(2):
                    pe_f(i * 2 + par, par, False)


def kernel(**inputs):
    import numpy as np
    import concourse.bacc as bacc
    from concourse.bass_utils import run_bass_kernel_spmd

    f = {k: np.asarray(v) for k, v in inputs.items()}
    nc = bacc.Bacc("TRN2", target_bir_lowering=False, num_devices=1)
    arrays = {}

    def give(name, a):
        name = "in_" + name
        a = np.ascontiguousarray(a)
        arrays[name] = a
        return nc.dram_tensor(name, a.shape, mybir.dt.from_np(a.dtype), kind="ExternalInput").ap()

    cr = f["ssm_c_re"][0].transpose(2, 0, 1)
    ci = f["ssm_c_im"][0].transpose(2, 0, 1)
    cm = np.zeros((G // 2, 2 * ST, 2, 2, 2 * GC), cr.dtype)
    for gg in range(2):
        ch = slice(GC * gg, GC * (gg + 1))
        cm[:, :ST, gg, 0, ch] = cr[:, gg::2].transpose(1, 0, 2)
        cm[:, ST:, gg, 0, ch] = ci[:, gg::2].transpose(1, 0, 2)
        cm[:, :ST, gg, 1, ch] = ci[:, gg::2].transpose(1, 0, 2)
        cm[:, ST:, gg, 1, ch] = cr[:, gg::2].transpose(1, 0, 2)
    dist = np.arange(TOK)
    nf = np.maximum(dist, 1).astype(np.float32)
    large = 16 + (np.log(nf / np.float32(16)) / np.float32(math.log(8)) * np.float32(16)).astype(np.int32)
    bucket = np.where(dist < 16, dist, np.minimum(large, 31))[::-1]
    onehot = (np.arange(32)[:, None] == bucket[None, :]).astype(np.float32)
    gmask = (np.arange(P)[:, None] // GC == np.arange(8)[None, :]).astype(np.float32)

    def b_layout(b):
        return b.reshape(16, 8, ST, GC).transpose(1, 3, 0, 2).reshape(P, 16, ST)

    args = [
        give("x", f["x"][0]), give("c_col", f["c"].reshape(KT, P).T), give("g_col", f["norm_g"].reshape(KT, P).T),
        give("w_ada", f["w_ada"][0]), give("bada_col", f["b_ada"].reshape(3 * KT, P).T),
        give("bada_gate", f["b_ada"][:, 2 * D:]), give("w_in", f["w_in"][0]),
        give("lam_re", f["ssm_lambda_re"][0]), give("lam_im", f["ssm_lambda_im"][0]),
        give("log_dt", f["ssm_log_dt"].reshape(G, 1)),
        give("b_re", b_layout(f["ssm_b_re"][0])), give("b_im", b_layout(f["ssm_b_im"][0])),
        give("c_map", cm.reshape(G // 2, P, 2 * 2 * 2 * GC)), give("d_col", f["ssm_d"].reshape(16, P).T),
        give("w_glu", f["w_glu"][0]),
        give("lambdas", np.concatenate([f[k] for k in ("lambda_q1", "lambda_k1", "lambda_q2", "lambda_k2")], 1)),
        give("subln_g", f["subln_g"]), give("w_oss", f["w_out_ssm"][0]), give("w_oat", f["w_out_attn"][0]),
        give("w_o", f["w_o"][0]), give("rel_bias", f["rel_bias"]), give("final_g", f["final_g"].reshape(1, D)),
        give("onehot", onehot), give("ident", np.eye(P, dtype=np.float32)),
        give("tvals", np.arange(TOK, dtype=np.float32).reshape(1, TOK)), give("gmask", gmask),
    ]
    out = nc.dram_tensor("out", (TOK, D), F32, kind="ExternalOutput").ap()
    build(nc, *args, out)
    r = run_bass_kernel_spmd(nc, [arrays], core_ids=[0])
    return r.results[0]["out"].reshape(1, TOK, D)
```

```python
from contextlib import ExitStack
import math

import concourse.bass as bass
from concourse import mybir

F32 = mybir.dt.float32
F32R = mybir.dt.float32r
ALU = mybir.AluOpType
ACT = mybir.ActivationFunctionType
AX = mybir.AxisListType

P = 128
TOK = 256
NH = TOK // P
D = 4096
KT = D // P
CB = 512
UT = 4
UPB = KT // UT
RING = 4
NIN = 20480
G, ST, GC = 128, 64, 16
HEADS, HD = 8, 128
BLK_A, BLK_B, BLK_C = 4, 20, 16
SHIFT_SCALE = 2 * D
ADA_CB = 1024
ADA_UNITS = D // (2 * P)
NADA = SHIFT_SCALE // ADA_CB
R0 = NADA * ADA_UNITS
NC0 = D // ADA_CB
BLK_0 = 3
CH_W = 2 * BLK_0
EARLY = {1: (20, 21), 2: (22, 23)}
K_EARLY = {c: 2 * (c + 1) for c in EARLY}
EARLY_OF = {b: K_EARLY[c] for c in EARLY for b in EARLY[c]}
N_EARLY = sum(EARLY_OF.values())

TURN = [[(v % BLK_0, 2 * c + v // BLK_0) for v in range(CH_W)]
        + [(b, k) for b in EARLY.get(c, ()) for k in range(K_EARLY.get(c, 0))] for c in range(NC0)]
TURN_AT = [[3 + 2 * v for v in range(CH_W)]
           + [14 + 16 * e // (len(t) - CH_W) for e in range(len(t) - CH_W)] for t in TURN]
TURN_W = [sum(len(t) for t in TURN[:c]) for c in range(NC0)]
W_A3 = UPB * BLK_0 + N_EARLY
W_B = W_A3 + UPB
W_B2 = W_B + UPB * 16
W_C = UPB * (BLK_A + BLK_B)
W_D = W_C + UPB * BLK_C
W_E = W_D + 4 * UT
W_F = W_E + 8 * UPB
ADA_C = (D // ADA_CB) * ADA_UNITS
ROUND = 1.5 * 2.0 ** 23
ROUND16 = 192.0
PI = math.pi
CW1 = 6.28125
CW2 = 0.0019340515136718750
CW3 = 2 * PI - CW1 - CW2
BELOW_PI = 3.1415925
NEG = -1e30
EPS = 1e-6
LAM_INIT = 0.8 - 0.6 * math.exp(-0.3 * 0)


def build(nc, x, c_col, g_col, w_ada, bada_col, bada_gate, w_in, lam_re, lam_im, log_dt,
          b_re, b_im, c_map, d_col, w_glu, lambdas, subln_g, w_oss, w_oat, w_o, rel_bias,
          final_g, onehot, ident_in, tvals, gmask_in, out):
    ctx = ExitStack()
    with ctx:
        def sb(name, shape, dt=F32):
            return ctx.enter_context(nc.sbuf_tensor(name, shape, dt))

        def sem(name):
            return ctx.enter_context(nc.semaphore(name))

        raw = sb("raw", [P, RING, UT, CB])
        w_hi = sb("w_hi", [P, 2, UT, CB], F32R)
        w_lo = sb("w_lo", [P, 2, UT, CB], F32R)
        a_hi = sb("a_hi", [P, KT, TOK], F32R)
        a_lo = sb("a_lo", [P, KT, TOK], F32R)
        feat = sb("feat", [P, KT, TOK])
        stage = sb("stage", [P, 2, NH, CB])
        work = sb("work", [P, 9216])
        ident = sb("ident", [P, P])
        tv = sb("tv", [P, TOK])
        gmask = sb("gmask", [P, 8])
        rot = sb("rot", [P, 3, G // 2])
        dcol = sb("dcol", [P, 16])
        g_sb = sb("g_sb", [P, KT])
        ba_sb = sb("ba_sb", [P, 2, KT])
        cact = sb("cact", [P, KT])
        small = sb("small", [P, 64])
        ones, minus = small[:, 56:60], small[:, 61:62]
        sc8, sh8 = small[:, 8:16], small[:, 24:32]
        bank = [ctx.enter_context(nc.psum_tensor(f"bank{i}", [P, CB], F32)) for i in range(8)]

        def carve(base, off, shape):
            n = 1
            for s in shape:
                n *= s
            ap = base[:, off:off + n]
            if len(shape) == 1:
                return ap
            names = "abcd"[:len(shape)]
            return ap.rearrange(f"p ({' '.join(names)}) -> p {' '.join(names)}",
                                **{k: v for k, v in zip(names, shape)})

        def wk(off, *shape):
            return carve(work, off, shape)

        featf = feat[:, :, :].rearrange("p k t -> p (k t)")
        xs = carve(featf, 0, (NH, D))
        bb = wk(0, 2, 16, ST)
        adacc = wk(2048, 2, ADA_CB)
        hf = wk(4096, 2, UT, TOK)
        coef_l = wk(6144, 2, 16, ST)
        b_ld = carve(stage[:, :, :, :].rearrange("p b h c -> p (b h c)"), 0, (2, 16, ST))
        npar = wk(8192, 1024)
        PH, LO, FR = wk(2048, 2, TOK), wk(2560, 2, TOK), wk(3072, 2, TOK)
        FA = wk(3584, TOK)
        T1, T2, HH = wk(5632, 2, TOK), wk(6144, 2, TOK), wk(6656, 2, TOK)
        bd = wk(7168, 2, 2, 2, ST)
        cst = wk(7936, 4, 4, 32)
        gl = wk(8448, 3, TOK)
        cosb = carve(featf, 4096, (2, TOK))
        sinb = carve(featf, 4608, (2, TOK))
        early = [carve(featf, 5120, (NH, CB)), wk(4096, NH, CB)]
        hcb = carve(featf, 6144, (2, 2, TOK))
        hsb = carve(featf, 7168, (2, 2, TOK))
        gacc = wk(0, ADA_CB)
        q_in, k_in, v_in, za_in, bias_in = (wk(1024 + 512 * i, NH, TOK) for i in range(5))
        qT, kT = wk(3584, 2, TOK), wk(4096, 2, TOK)
        sc = wk(4608, 2, 2, TOK)
        at = wk(5632, 2, TOK)
        aT = wk(6144, 2, TOK)
        ya = wk(6656, 2, TOK)
        szA = wk(7168, 2, TOK)
        subg = wk(7680, TOK)
        grow = wk(7936, ADA_CB)
        ysT = wk(0, 16, TOK)
        zs, sz, sig, ys = (wk(4096 + 1024 * i, NH, CB) for i in range(4))
        ga, gs, part, mrg = (wk(4096 + 1024 * i, NH, CB) for i in range(4))
        obuf = carve(featf, 0, (NH, D))
        xb = wk(0, 2, NH, CB)
        gate_b = wk(2048, 2, CB)
        fg = wk(3072, D)
        junk = wk(7168, NH, CB)

        proj_d = nc.dram_tensor("proj_scratch", (TOK, NIN), F32, kind="Internal").ap()
        coef_d = nc.dram_tensor("coef_scratch", (2, G, ST), F32, kind="Internal").ap()
        dist_d = nc.dram_tensor("dist_scratch", (HEADS, 512), F32, kind="Internal").ap()
        skew_d = nc.dram_tensor("skew_scratch", (HEADS, P * 513), F32, kind="Internal").ap()
        gate_d = nc.dram_tensor("gate_scratch", (1, D), F32, kind="Internal").ap()

        raw_full = [sem(f"raw_full{i}") for i in range(RING)]
        raw_used = sem("raw_used")
        h_done = sem("h_done")
        pe_used = sem("pe_used")
        stat_ready = sem("stat_ready")
        acc_free_a = sem("acc_free_a")
        acc_free_v = sem("acc_free_v")
        x_scaled = sem("x_scaled")
        mod_ready = sem("mod_ready")
        cons_in, x_in, misc_in = sem("cons_in"), sem("x_in"), sem("misc_in")
        act_misc = sem("act_misc")
        dve_misc = sem("dve_misc")
        pe_misc = sem("pe_misc")
        coef_io, dist_io, bias_io = sem("coef_io"), sem("dist_io"), sem("bias_io")
        bb_ready = sem("bb_ready")
        acc_ready = sem("acc_ready")
        ada_mm = sem("ada_mm")
        xt_pe = sem("xt_pe")
        hf_ready = sem("hf_ready")
        staged = sem("staged")
        early_free = sem("early_free")
        early_st = sem("early_st")
        early_in = [sem("early_in0"), sem("early_in1")]
        stored = sem("stored")
        ut_pe, ut_done = sem("ut_pe"), sem("ut_done")
        frac_ready = sem("frac_ready")
        trig_ready = sem("trig_ready")
        prod_ready = sem("prod_ready")
        bd_ready = sem("bd_ready")
        c_in = sem("c_in")
        cst_ready = sem("cst_ready")
        x_pe = sem("x_pe")
        x_used = sem("x_used")
        hcs_ready = sem("hcs_ready")
        y_pe = sem("y_pe")
        y_used = sem("y_used")
        tanh_in, tanh_out = sem("tanh_in"), sem("tanh_out")
        gelu_done = sem("gelu_done")
        qk_in, va_in, ba_in, za_in_s = sem("qk_in"), sem("va_in"), sem("ba_in"), sem("za_in_s")
        qk_pe, qk_sb, s_pe, s_max, p_exp = (sem(n) for n in ("qk_pe", "qk_sb", "s_pe", "s_max", "p_exp"))
        at_sb, at_pe, at_t, o_pe, o_ssq, ya_sb, ya_pe, yaT_sb = (
            sem(n) for n in ("at_sb", "at_pe", "at_t", "o_pe", "o_ssq", "ya_sb", "ya_pe", "yaT_sb"))
        gacc_ready, gate_pe, gate_row, gate_st = (
            sem(n) for n in ("gacc_ready", "gate_pe", "gate_row", "gate_st"))
        bg_in = sem("bg_in")
        zs_in, gt_pe, sig_done, ys_sb, ys_pe, feat_sb = (
            sem(n) for n in ("zs_in", "gt_pe", "sig_done", "ys_sb", "ys_pe", "feat_sb"))
        ga_in, gs_in, ga_sig, gs_sig, ga_used, m_sb, m_pe = (
            sem(n) for n in ("ga_in", "gs_in", "ga_sig", "gs_sig", "ga_used", "m_sb", "m_pe"))
        xg_in = [sem("xg_in0"), sem("xg_in1")]
        fg_in, o_sb, o_sq, f_rms, f_rstd, f_out, out_st = (
            sem(n) for n in ("fg_in", "o_sb", "o_sq", "f_rms", "f_rstd", "f_out", "out_st"))

        w_in_v = w_in.rearrange("(u t p) (b c) -> b u p t c", t=UT, p=P, c=CB)
        w_glu_v = w_glu.rearrange("(u t p) (b c) -> b u p t c", t=UT, p=P, c=CB)
        w_oss_v = w_oss.rearrange("(u t p) (b c) -> b u p t c", t=UT, p=P, c=CB)
        w_oat_v = w_oat.rearrange("(u t p) (b c) -> b u p t c", t=UT, p=P, c=CB)
        w_o_v = w_o.rearrange("(u t p) (b c) -> b u p t c", t=UT, p=P, c=CB)
        ada_v = w_ada.rearrange("(u t p) (b c) -> b u p t c", t=2, p=P, c=ADA_CB)
        proj_v = proj_d.rearrange("(h p) (b c) -> b p h c", p=P, c=CB)
        proj_h = proj_d.rearrange("(h p) (b c) -> b p h c", p=P, c=TOK)
        x_v = x.rearrange("(h p) (b c) -> b p h c", p=P, c=CB)
        out_v = out.rearrange("(h p) (b c) -> b p h c", p=P, c=CB)

        def rows(v, n):
            return bass.AP(v.tensor, 0, [[0, P], [1, n]])

        def at_block(v, b):
            if isinstance(b, int):
                return v[b]
            return v[bass.ds(b, 1)].rearrange("o p h c -> (o p) h c")

        def at_unit(v, b, u):
            if isinstance(b, int) and isinstance(u, int):
                return v[b, u]
            if isinstance(b, int):
                return v[b, bass.ds(u, 1)].rearrange("o p t c -> (o p) t c")
            if isinstance(u, int):
                return v[bass.ds(b, 1), u].rearrange("o p t c -> (o p) t c")
            return v[bass.ds(b, 1), bass.ds(u, 1)].rearrange("o q p t c -> (o q p) t c")

        raw_ada = raw[:, :, :, :].rearrange("p r t c -> p r (t c)").rearrange("p r (t c) -> p r t c", c=ADA_CB)

        def ring_ada(c, a):
            if c == 0:
                return a
            return 2 * ADA_UNITS * c + TURN_W[c - 1] + a + sum(at < a for at in TURN_AT[c - 1])

        def ring_of(w):
            if w < W_A3:
                c = max(c for c in range(NC0) if TURN_W[c] <= w)
                v = w - TURN_W[c]
                return ring_ada(c + 1, TURN_AT[c][v]) + 1 + TURN_AT[c][:v].count(TURN_AT[c][v]) if c < NC0 - 1 else R0 + w
            return R0 + w if w < W_C else (R0 + w + ADA_C if w >= W_D else None)

        LATE = [(b, u) for b in range(20, 24) for u in range(EARLY_OF[b], UPB)]

        LATE_AT = [LATE.index((b, EARLY_OF[b])) for b in range(20, 24)]

        block = ctx.enter_context(nc.Block())

        @block.sync
        def _(sp):
            sp.dma_start(ident[:, :], ident_in).then_inc(cons_in, 16)
            sp.dma_start(cact[:, :], c_col).then_inc(cons_in, 16)
            sp.dma_start(npar[:, 0:64], lam_re).then_inc(cons_in, 16)
            sp.dma_start(npar[:, 64:128], lam_im).then_inc(cons_in, 16)
            sp.dma_start(small[:, 0:1], log_dt).then_inc(cons_in, 16)

            def load(r, slot, dst, src):
                sp.wait_ge(raw_used, r + 1)
                sp.dma_start(dst, src).then_inc(raw_full[slot], 16)

            def load_unit(r, slot, src):
                load(r, slot, raw[:, slot, :, :], src)

            def load_ada(r, slot, src):
                load(r, slot, raw_ada[:, slot, :, :], src)

            def turn_unit(c, v):
                r = ring_of(TURN_W[c] + v)
                load_unit(r, r % RING, w_in_v[TURN[c][v]])

            for c in range(NC0):
                for a in range(2 * ADA_UNITS):
                    r = ring_ada(c, a)
                    load_ada(r, r % RING, ada_v[c + NC0 * (a // ADA_UNITS), a % ADA_UNITS])
                    if c:
                        for v in range(len(TURN[c - 1])):
                            if TURN_AT[c - 1][v] == a:
                                turn_unit(c - 1, v)
            for v in range(CH_W):
                turn_unit(NC0 - 1, v)
            with sp.Fori(BLK_0, BLK_A + 16) as b:
                for u in range(UPB):
                    load_unit(b * UPB + (R0 + N_EARLY + u), u % RING, at_unit(w_in_v, b, u))
            for n, (b, u) in enumerate(LATE):
                load_unit(R0 + W_B2 + n, n % RING, w_in_v[b, u])
            with sp.Fori(0, HEADS // 2) as cb:
                for rr in range(2):
                    for v in range(2 * UPB):
                        loc = 24 * rr + v + (v + 1) // 2
                        load_unit(cb * 48 + (R0 + W_C + loc), loc % RING,
                                  at_unit(w_in_v, cb * 4 + (BLK_A + BLK_B + 2 * rr + v // UPB), v % UPB))
                        if v % 2 == 0:
                            load_ada(cb * 48 + (R0 + W_C + loc + 1), (loc + 1) % RING,
                                     at_unit(ada_v, cb + NADA, 8 * rr + v // 2))
            for w in range(W_D, W_E):
                r = ring_of(w)
                load_unit(r, r % RING, w_glu_v[(w - W_D) // UT, (w - W_D) % UT])
            with sp.Fori(0, 8) as j:
                for u in range(UPB):
                    v = w_oat_v if u < UT else w_oss_v
                    load_unit(j * UPB + (ring_of(W_E) + u), u % RING, at_unit(v, j, u % UT))
            with sp.Fori(0, 8) as j:
                for u in range(UPB):
                    load_unit(j * UPB + (ring_of(W_F) + u), u % RING, at_unit(w_o_v, j, u))
            sp.wait_ge(out_st, 16 * 8)

        @block.gpsimd
        def _(pool):
            pool.dma_start(tv[:, :], rows(tvals, TOK)).then_inc(misc_in, 16)
            pool.dma_start(gmask[:, :], gmask_in).then_inc(misc_in, 16)
            pool.dma_start(dcol[:, :], d_col).then_inc(misc_in, 16)
            pool.dma_start(g_sb[:, :], g_col).then_inc(misc_in, 16)
            pool.dma_start(ba_sb[:, :, :].rearrange("p a k -> p (a k)"), bada_col[:, 0:2 * KT]).then_inc(misc_in, 16)
            pool.dma_start(npar[:, 512:1024].rearrange("p (a d) -> p a d", a=4),
                           rows(lambdas, 4 * HD).rearrange("p (a d) -> p a d", a=4)).then_inc(misc_in, 16)
            for k, src in enumerate((b_re, b_im)):
                pool.dma_start(b_ld[:, k, :, :], src).then_inc(misc_in, 16)
            pool.dma_start(hf[0:32, 0, 0:1, :].rearrange("p a t -> p (a t)"), onehot).then_inc(misc_in, 16)
            pool.dma_start(hf[0:32, 1, 0, 0:HEADS], rel_bias).then_inc(misc_in, 16)

            nc.gpsimd.memset(small[:, 44:46], -0.5)
            pool.wait_ge(act_misc, 5)
            nc.gpsimd.tensor_scalar(small[:, 42:44], small[:, 40:42], 1.0 / D, EPS, ALU.mult, ALU.add)
            pool.drain()
            nc.gpsimd.tensor_tensor(small[:, 42:44], small[:, 42:44], small[:, 44:46], ALU.pow)
            pool.drain()
            for h in range(NH):
                ins = nc.gpsimd.tensor_scalar(xs[:, h, :], xs[:, h, :], small[:, 42 + h:43 + h], 1.0,
                                              ALU.mult, ALU.mult)
            ins.then_inc(x_scaled, 1)
            pool.wait_ge(dve_misc, 4)
            for k in range(2):
                pool.dma_start(coef_d[k], coef_l[:, 0, 6 + k, :]).then_inc(coef_io, 16)
            pool.wait_ge(coef_io, 32)
            pool.wait_ge(pe_misc, 1)
            for k in range(2):
                for e in range(8):
                    pool.dma_start(coef_l[e * GC:(e + 1) * GC, k, :, :],
                                   bass.AP(coef_d.tensor, k * G * ST + e * ST, [[0, GC], [8 * ST, 16], [1, ST]])
                                   ).then_inc(coef_io, 16)
            pool.wait_ge(dve_misc, 5)
            pool.dma_start(dist_d, hf[0:HEADS, 0, 1:3, :].rearrange("p a t -> p (a t)")).then_inc(dist_io, 16)
            pool.wait_ge(dist_io, 16)
            pool.wait_ge(coef_io, 32 + 16 * 16)
            pool.wait_ge(misc_in, 16 * 10)
            cre, cim = coef_l[:, 0, :, :], coef_l[:, 1, :, :]
            bre, bim = b_ld[:, 0, :, :], b_ld[:, 1, :, :]
            nc.gpsimd.tensor_tensor(bb[:, 0, :, :], cre, bre, ALU.mult)
            nc.gpsimd.tensor_tensor(bb[:, 1, :, :], cre, bim, ALU.mult)
            pool.drain()
            nc.gpsimd.tensor_tensor(bre, cim, bre, ALU.mult)
            nc.gpsimd.tensor_tensor(bim, cim, bim, ALU.mult)
            pool.drain()
            nc.gpsimd.tensor_tensor(bb[:, 0, :, :], bb[:, 0, :, :], bim, ALU.subtract)
            nc.gpsimd.tensor_tensor(bb[:, 1, :, :], bb[:, 1, :, :], bre, ALU.add).then_inc(bb_ready, 1)
            pool.drain()
            pool.wait_ge(hf_ready, UPB)
            pool.wait_ge(stat_ready, UPB)

            def map_load(s, buf):
                pool.dma_start(cst[:, buf, 0:2, :].rearrange("p a b -> p (a b)"),
                               c_map[bass.ds(s, 1)].rearrange("o p n -> (o p) n")).then_inc(c_in, 16)

            def tables(i, j, first, last):
                s = i * 8 + j
                buf = j % 2
                late = not (first and j < 2)
                pool.wait_ge(prod_ready, s + 1)
                if late:
                    pool.wait_ge(trig_ready, s - 1)
                SU = FR[:, buf, :]
                nc.gpsimd.tensor_tensor(SU, PH[:, buf, :], LO[:, buf, :], ALU.add)
                pool.drain()
                nc.gpsimd.tensor_scalar(SU, SU, 1.0, ROUND, ALU.mult, ALU.add)
                pool.drain()
                nc.gpsimd.tensor_scalar(SU, SU, 1.0, -ROUND, ALU.mult, ALU.add)
                pool.drain()
                nc.gpsimd.tensor_tensor(SU, PH[:, buf, :], SU, ALU.subtract)
                pool.drain()
                nc.gpsimd.tensor_tensor(SU, SU, LO[:, buf, :], ALU.add)
                pool.drain()
                nc.gpsimd.tensor_scalar(SU, SU, BELOW_PI / (2 * PI), -BELOW_PI / (2 * PI),
                                        ALU.min, ALU.max).then_inc(frac_ready, 1)
                pool.wait_ge(c_in, (s + 1) * 16)
                nc.gpsimd.tensor_tensor(cst[:, j % 4, 2:4, :], cst[:, j % 4, 0:2, :],
                                        minus.unsqueeze(2).to_broadcast([P, 2, 32]), ALU.mult).then_inc(cst_ready, 1)
                if late:
                    pool.wait_ge(x_pe, s - 1)
                    pool.wait_ge(y_pe, s - 1)
                if not (last and j >= 6):
                    map_load(s + 2, (j + 2) % 4)
                q = j % 4
                sup = i * 2 + j // 4
                m = gmask[:, 2 * q:2 * q + 2].unsqueeze(2).to_broadcast([P, 2, ST])
                for k in range(2):
                    src = bb[:, k, bass.ds(sup, 1), :].to_broadcast([P, 2, ST])
                    ins = nc.gpsimd.tensor_tensor(bd[:, buf, k, :, :], src, m, ALU.mult)
                ins.then_inc(bd_ready, 1)

            map_load(0, 0)
            map_load(1, 1)
            for j in range(8):
                tables(0, j, True, False)
            for h in range(HEADS):
                pool.dma_start(bass.AP(skew_d.tensor, h * P * 513, [[513, P], [1, 512]]),
                               bass.AP(dist_d.tensor, h * 512, [[0, P], [1, 512]])).then_inc(bias_io, 16)
            with pool.Fori(1, 7) as i:
                for j in range(8):
                    tables(i, j, False, False)
            for j in range(8):
                tables(7, j, False, True)

            pool.wait_ge(early_st, 16 * 4)
            for n in range(4):
                if n >= 2:
                    pool.wait_ge(pe_used, W_B2 + LATE_AT[n - 2] + 1)
                pool.dma_start(early[n % 2], proj_v[20 + n]).then_inc(early_in[n % 2], 16)

            pool.wait_ge(gelu_done, 16)
            pool.wait_ge(bias_io, 16 * HEADS)
            skew_v = skew_d[:, 0:P * 512].rearrange("h (p j) -> h p j", j=512)
            pool.dma_start(subg, rows(subln_g, TOK)).then_inc(ba_in, 16)

            def head_loads(h, first):
                if not first:
                    pool.wait_ge(qk_pe, h)
                pool.wait_ge(stored, h * 16 + 16 * 19)
                qk = [(q_in, 16), (k_in, 24)]
                for dst, b0 in qk:
                    pool.dma_start(dst, at_block(proj_h, h + b0)).then_inc(qk_in, 16)
                if not first:
                    pool.wait_ge(s_max, h)
                sk = skew_v[h] if first else skew_v[bass.ds(h, 1)].rearrange("o p j -> (o p) j")
                for qb in range(NH):
                    start = TOK - 1 - P * qb
                    pool.dma_start(bias_in[:, qb, :], sk[:, start:start + TOK]).then_inc(ba_in, 16)
                if not first:
                    pool.wait_ge(o_pe, h)
                pool.dma_start(v_in, at_block(proj_h, h + 32)).then_inc(va_in, 16)
                if not first:
                    pool.wait_ge(ya_sb, h)
                pool.dma_start(za_in, at_block(proj_h, h + 40)).then_inc(za_in_s, 16)

            bg_v = bada_gate.rearrange("o (b c) -> b o c", c=ADA_CB)
            gate_v = gate_d.rearrange("o (b c) -> b o c", c=ADA_CB)

            def block_row(v, b):
                return v[b] if isinstance(b, int) else v[bass.ds(b, 1)].rearrange("q o c -> (q o) c")

            def gate_out(cb):
                pool.wait_ge(gate_row, cb + 1)
                pool.dma_start(block_row(gate_v, cb), grow[0:1, :]).then_inc(gate_st, 16)
                pool.wait_ge(gate_st, cb * 16 + 16)

            pool.dma_start(grow[0:1, :], bg_v[0]).then_inc(bg_in, 16)
            head_loads(0, True)
            with pool.Fori(0, HEADS // 2 - 1) as cb:
                head_loads(cb * 2 + 1, False)
                head_loads(cb * 2 + 2, False)
                gate_out(cb)
                pool.dma_start(grow[0:1, :], block_row(bg_v, cb + 1)).then_inc(bg_in, 16)
            head_loads(HEADS - 1, False)
            gate_out(HEADS // 2 - 1)

            pool.wait_ge(yaT_sb, HEADS)
            for j in range(4):
                if j:
                    pool.wait_ge(ys_sb, j)
                pool.dma_start(zs, at_block(proj_v, 4 + j)).then_inc(zs_in, 16)
            pool.wait_ge(ys_sb, 4)
            pool.wait_ge(stored, 16 * 36)
            for j in range(8):
                if j:
                    pool.wait_ge(ga_used, j)
                pool.dma_start(ga, at_block(proj_v, 32 + j)).then_inc(ga_in, 16)
                if j:
                    pool.wait_ge(m_sb, j)
                pool.dma_start(gs, at_block(proj_v, 24 + j)).then_inc(gs_in, 16)
            pool.wait_ge(m_pe, 8)
            for j in range(8):
                if j >= 2:
                    pool.wait_ge(o_sb, j - 1)
                pool.dma_start(xb[:, j % 2, :, :], x_v[j]).then_inc(xg_in[j % 2], 16)
                pool.dma_start(gate_b[:, j % 2, :], bass.AP(gate_d.tensor, j * CB, [[0, P], [1, CB]])
                               ).then_inc(xg_in[j % 2], 16)
                if j == 1:
                    pool.dma_start(fg, rows(final_g, D)).then_inc(fg_in, 16)

        @block.scalar
        def _(act):
            for h in range(NH):
                act.dma_start(xs[:, h, :], x[h * P:(h + 1) * P, :]).then_inc(x_in, 16)
            act.wait_ge(cons_in, 16 * 5)
            nc.scalar.activation(small[:, 1:2], small[:, 0:1], ACT.Exp)
            act.drain()
            nc.scalar.activation(npar[:, 128:192], npar[:, 0:64], ACT.Exp,
                                 scale=small[:, 1:2]).then_inc(act_misc, 1)
            nc.scalar.activation(coef_l[:, 0, 0, 0:KT], cact[:, :], ACT.Sigmoid).then_inc(act_misc, 1)
            act.wait_ge(dve_misc, 2)
            nc.scalar.activation(npar[:, 256:320], npar[:, 192:256], ACT.Sin)
            nc.scalar.activation(npar[:, 320:384], npar[:, 192:256], ACT.Abs)
            act.drain()
            nc.scalar.activation(npar[:, 384:448], npar[:, 320:384], ACT.Sin,
                                 scale=-1.0, bias=small[:, 2:3]).then_inc(act_misc, 1)
            act.wait_ge(dve_misc, 3)
            nc.scalar.activation(small[:, 5:7], small[:, 3:5], ACT.Exp).then_inc(act_misc, 1)
            act.wait_ge(x_in, 32)
            for h in range(NH):
                nc.scalar.activation(a_hi[:, 16 * h:16 * h + 16, :].rearrange("p k t -> p (k t)"), xs[:, h, :], ACT.Square,
                                     accum_out=small[:, 40 + h:41 + h])
            act.drain().then_inc(act_misc, 1)

            def high(w, slot, hb, full):
                act.wait_ge(raw_full[slot], full)
                if not (isinstance(w, int) and w < 2):
                    act.wait_ge(pe_used, w - 1)
                nc.scalar.activation(w_hi[:, hb, :, :], raw[:, slot, :, :], ACT.Copy).then_inc(h_done, 1)

            def turns(r):
                return (r // RING + 1) * 16

            def evac(b, par, pe_count, pair=None):
                act.wait_ge(pe_used, pe_count)
                pair = par if pair is None else pair
                for hh in range(NH):
                    last = nc.scalar.activation(stage[:, par, hh, :], bank[2 * pair + hh][:, :], ACT.Copy)
                last.then_inc(acc_free_a, 1)

            def store(b, par, n):
                act.wait_ge(acc_free_a, b + 1)
                if not (isinstance(n, int) and n == 0):
                    act.wait_ge(stored, n * 16)
                act.dma_start(at_block(proj_v, b), stage[:, par, :, :]).then_inc(stored, 16)

            def products(s, buf):
                for k, dst in enumerate((PH, LO)):
                    ph = rot[:, k, bass.ds(s, 1)] if not isinstance(s, int) else rot[:, k, s:s + 1]
                    ins = nc.scalar.activation(dst[:, buf, :], tv[:, :], ACT.Copy, scale=ph)
                ins.then_inc(prod_ready, 1)

            def early_out(b, w):
                n = b - 20
                act.wait_ge(pe_used, w + 1)
                if n >= 2:
                    act.wait_ge(early_st, 16 * (n - 1))
                for hh in range(NH):
                    nc.scalar.activation(stage[:, n % 2, hh, :], bank[6 + hh][:, :], ACT.Copy)
                act.drain().then_inc(early_free, 1)
                if n:
                    act.wait_ge(early_st, 16 * n)
                act.dma_start(proj_v[b], stage[:, n % 2, :, :]).then_inc(early_st, 16)

            act.wait_ge(dist_io, 16)
            for c in range(NC0):
                act.wait_ge(mod_ready, c + 1)
                for gi in range(2):
                    g = c * 2 + gi
                    act.wait_ge(xt_pe, g + 1)
                    if g >= 2:
                        act.wait_ge(stat_ready, g - 1)
                    for t in range(UT):
                        k = UT * gi + t
                        last = nc.scalar.activation(hf[:, gi, t, :],
                                                    bank[6 + t // 2][:, TOK * (t % 2):TOK * (t % 2 + 1)],
                                                    ACT.Identity, scale=sc8[:, k:k + 1], bias=sh8[:, k:k + 1])
                    last.then_inc(hf_ready, 1)
                    for v in range(BLK_0 * gi, BLK_0 * (gi + 1)):
                        w = TURN_W[c] + v
                        high(w, ring_of(w) % RING, v % 2, turns(ring_of(w)))
                if c == 1:
                    act.wait_ge(bb_ready, 1)
                for v in range(CH_W, len(TURN[c])):
                    w, (b, k) = TURN_W[c] + v, TURN[c][v]
                    high(w, ring_of(w) % RING, w % 2, turns(ring_of(w)))
                    if k == EARLY_OF[b] - 1:
                        early_out(b, w)
            for u in range(UPB):
                w = W_A3 + u
                high(w, w % RING, w % 2, turns(R0 + w))
                if u == 0:
                    act.wait_ge(early_st, 16 * 4)
                    evac(0, 0, w - 2, 0)
                    evac(1, 1, w - 1, 1)
                if u == 4:
                    act.wait_ge(ut_pe, 1)
                    evac(2, 0, W_A3, 2)
                if u in (5, 6):
                    products(u - 5, u - 5)

            def trig(i, j, first):
                s = i * 8 + j
                buf = j % 2
                act.wait_ge(frac_ready, s + 1)
                if not (first and j < 2):
                    act.wait_ge(hcs_ready, s - 1)
                nc.scalar.activation(FA, FR[:, buf, :], ACT.Abs)
                nc.scalar.activation(sinb[:, buf, :], FR[:, buf, :], ACT.Sin, scale=2 * PI)
                act.drain()
                nc.scalar.activation(cosb[:, buf, :], FA, ACT.Sin, scale=-2 * PI,
                                     bias=small[:, 2:3]).then_inc(trig_ready, 1)
                act.drain()

            def tanh(n):
                act.wait_ge(tanh_in, n)
                nc.scalar.activation(gl[:, 1, :], gl[:, 0, :], ACT.Tanh,
                                     scale=math.sqrt(2 / PI)).then_inc(tanh_out, 1)

            def act_b(i, first):
                for bl in range(2):
                    for u in range(UPB):
                        v = UPB * bl + u
                        w = i * 16 + (W_B + v)
                        high(w, v % RING, v % 2, i * 64 + turns(R0 + W_B + v))
                        if u == 1:
                            b = i * 2 + (BLK_A + bl - 1)
                            par = (bl + 1) % 2
                            if first and bl == 0:
                                act.wait_ge(ut_pe, 2)
                                evac(b, par, W_B)
                            else:
                                act.wait_ge(ut_pe, 3 if first else 4)
                                evac(b, par, i * 16 + (W_B + UPB * bl))
                                store(b, par, i * 2 + (bl - 1))
                        if v % 2:
                            act_pair(i, v // 2, first)

            def act_pair(i, j, first):
                trig(i, j, first)
                if not (isinstance(i, int) and i == 7 and j >= 6):
                    products(i * 8 + (j + 2), j % 2)
                if j == 2 and not first:
                    tanh(i * 2)
                if j == 6:
                    tanh(i * 2 + 1)

            act_b(0, True)
            with act.Fori(1, 7) as i:
                act_b(i, False)
            act_b(7, False)

            def plain_evac(b, par, pe_count, nstored):
                evac(b, par, pe_count)
                store(b, par, nstored)

            for n, (b, u) in enumerate(LATE):
                w = W_B2 + n
                high(w, n % RING, w % 2, turns(R0 + w))
                if u == EARLY_OF[b] + 1:
                    plain_evac(b - 1, (b - 1) % 2, w - 1, b - 5)
                if n == 5:
                    tanh(16)

            def act_c(cb):
                for rr in range(2):
                    h1 = cb * 2 + (rr + 1)
                    for v in range(2 * UPB):
                        loc = 24 * rr + v + (v + 1) // 2
                        w = cb * 32 + (W_C + 16 * rr + v)
                        high(w, loc % RING, v % 2, cb * (48 * 4) + turns(R0 + W_C + loc))
                        if v % UPB == 1:
                            b = cb * 4 + (23 + 2 * rr + v // UPB)
                            plain_evac(b, (1 + v // UPB) % 2, (b + 1) * UPB, cb * 4 + (19 + 2 * rr + v // UPB))
                        if v == 2:
                            act.wait_ge(qk_pe, h1)
                            nc.scalar.activation(qT.rearrange("p m t -> p (m t)"), bank[4][:, :], ACT.Copy,
                                                 scale=HD ** -0.5)
                            nc.scalar.activation(kT.rearrange("p m t -> p (m t)"), bank[5][:, :],
                                                 ACT.Copy).then_inc(qk_sb, 1)
                        if v == 6:
                            act.wait_ge(s_max, h1)
                            for qb in range(2):
                                for m in range(2):
                                    k = 2 * qb + m
                                    nc.scalar.activation(sc[:, qb, m, :], sc[:, qb, m, :], ACT.Exp,
                                                         bias=small[:, 16 + k:17 + k],
                                                         accum_out=small[:, 20 + k:21 + k])
                            act.wait_ge(za_in_s, h1 * 16)
                            nc.scalar.activation(szA, za_in, ACT.Sigmoid).then_inc(p_exp, 1)
                        if v == 10:
                            act.wait_ge(at_pe, h1)
                            nc.scalar.activation(aT.rearrange("p m t -> p (m t)"), bank[4][:, :],
                                                 ACT.Copy).then_inc(at_t, 1)
                        if v == 12:
                            act.wait_ge(o_pe, h1)
                            for qb in range(2):
                                nc.scalar.activation(aT[:, qb, :], bank[6 + qb][:, 0:TOK], ACT.Square,
                                                     accum_out=small[:, 28 + qb:29 + qb])
                            act.drain()
                            nc.scalar.activation(small[:, 30:32], small[:, 28:30], ACT.Sqrt, scale=1.0 / TOK,
                                                 bias=small[:, 60:61]).then_inc(o_ssq, 1)
                        if v == 15:
                            act.wait_ge(ya_pe, h1)
                            nc.scalar.activation(feat[:, bass.ds(cb * 4 + (16 + 2 * rr), 2), :].rearrange("p k t -> p (k t)"),
                                                 bank[5][:, :], ACT.Copy).then_inc(yaT_sb, 1)

            with act.Fori(0, HEADS // 2) as cb:
                act_c(cb)

            def sig_prev(j):
                act.wait_ge(pe_used, W_D + UT * (j + 1))
                if j:
                    act.wait_ge(ys_sb, j)
                for hh in range(NH):
                    last = nc.scalar.activation(sig[:, hh, :], bank[2 * (j % 2) + hh][:, :], ACT.Sigmoid)
                last.then_inc(acc_free_a, 1)
                act.wait_ge(zs_in, 16 * (j + 1))
                nc.scalar.activation(sz, zs, ACT.Sigmoid).then_inc(sig_done, 1)

            def ysT_copy(j):
                act.wait_ge(ys_pe, j + 1)
                for k in range(2):
                    last = nc.scalar.activation(ysT[:, 4 * j + 2 * k:4 * j + 2 * k + 2, :].rearrange("p k t -> p (k t)"),
                                                bank[6 + k][:, :], ACT.Copy)
                last.then_inc(feat_sb, 1)

            for j in range(4):
                for u in range(UT):
                    w = W_D + UT * j + u
                    high(w, w % RING, w % 2, turns(ring_of(w)))
                    if u == 1:
                        if j == 0:
                            plain_evac(39, 1, W_D, 35)
                        else:
                            sig_prev(j - 1)
                    if u == 3 and j:
                        ysT_copy(j - 1)

            def mT_copy(j):
                act.wait_ge(m_pe, j + 1)
                for k in range(2):
                    last = nc.scalar.activation(feat[:, 4 * j + 2 * k:4 * j + 2 * k + 2, :].rearrange("p k t -> p (k t)"),
                                                bank[4 + k][:, :], ACT.Copy)
                last.then_inc(feat_sb, 1)

            def gs_sigmoid(j):
                act.wait_ge(gs_in, 16 * (j + 1))
                nc.scalar.activation(gs, gs, ACT.Sigmoid).then_inc(gs_sig, 1)

            for j in range(8):
                for u in range(UPB):
                    w = W_E + UPB * j + u
                    high(w, w % RING, w % 2, turns(ring_of(w)))
                    if u == 1:
                        if j == 0:
                            sig_prev(3)
                        else:
                            gs_sigmoid(j - 1)
                    if u == 3:
                        if j == 0:
                            ysT_copy(3)
                        act.wait_ge(ga_in, 16 * (j + 1))
                        nc.scalar.activation(ga, ga, ACT.Sigmoid).then_inc(ga_sig, 1)
                    if u == 4 and j:
                        mT_copy(j - 1)

            def squares(j):
                act.wait_ge(o_sb, j + 1)
                for hh in range(NH):
                    last = nc.scalar.activation(junk[:, hh, :], obuf[:, hh, CB * j:CB * (j + 1)], ACT.Square,
                                                accum_out=small[:, 40 + 8 * hh + j:41 + 8 * hh + j])
                last.then_inc(o_sq, 1)
                act.drain()

            for j in range(8):
                for u in range(UPB):
                    w = W_F + UPB * j + u
                    high(w, w % RING, w % 2, turns(ring_of(w)))
                    if u == 1 and j == 0:
                        gs_sigmoid(7)
                    if u == 4:
                        if j == 0:
                            mT_copy(7)
                        else:
                            squares(j - 1)
            squares(7)
            act.wait_ge(f_rms, 1)
            nc.scalar.activation(small[:, 34:36], small[:, 32:34], ACT.Sqrt, scale=1.0 / D,
                                 bias=small[:, 7:8]).then_inc(f_rstd, 1)
            for j in range(8):
                act.wait_ge(f_out, j + 1)
                act.dma_start(out_v[j], obuf[:, :, CB * j:CB * (j + 1)]).then_inc(out_st, 16)

        @block.vector
        def _(dve):
            V = nc.vector

            def ada_unit(slot, full, acc, kt, first):
                dve.wait_ge(raw_full[slot], full)
                for t in range(2):
                    src, col = raw_ada[:, slot, t, :], kt + t
                    cc = cact[:, col:col + 1] if isinstance(col, int) else cact[:, bass.ds(col, 1)]
                    if first and t == 0:
                        ins = V.tensor_scalar(acc, src, cc, None, ALU.mult)
                    else:
                        ins = V.scalar_tensor_tensor(acc, src, cc, acc, ALU.mult, ALU.add)
                    if t:
                        ins.then_inc(raw_used, 1)
                    dve.drain()

            def ada(c, a0, a1):
                for a in range(a0, a1):
                    k, u = a // ADA_UNITS, a % ADA_UNITS
                    n, r = 2 * c + k, ring_ada(c, a)
                    if u == 0 and n >= 2:
                        dve.wait_ge(ada_mm, n - 1)
                    ada_unit(r % RING, 16 * (r // RING + 1), adacc[:, k, :], 2 * u, u == 0)
                    if u == ADA_UNITS - 1:
                        dve.drain().then_inc(acc_ready, 1)

            for _k in range(RING):
                V.memset(ones[:, _k:_k + 1], 1.0).then_inc(raw_used, 1)
            V.memset(small[:, 2:3], PI / 2)
            V.memset(minus, -1.0)
            V.memset(small[:, 7:8], 1e-6)
            V.memset(small[:, 60:61], 1e-5).then_inc(dve_misc, 1)
            dve.wait_ge(act_misc, 2)
            n = lambda k: npar[:, 64 * k:64 * (k + 1)]
            lr, li, mag, red, sn, ab, cs = n(0), n(1), n(2), n(3), n(4), n(5), n(6)
            V.tensor_tensor(cact[:, :], cact[:, :], coef_l[:, 0, 0, 0:KT], ALU.mult)
            V.tensor_scalar(red, li, small[:, 1:2], None, ALU.mult)
            dve.drain()
            V.tensor_scalar(ab, red, 1 / (2 * PI), ROUND, ALU.mult, ALU.add)
            dve.drain()
            V.tensor_scalar(ab, ab, ROUND, None, ALU.subtract)
            dve.drain()
            for cw in (CW1, CW2, CW3):
                V.scalar_tensor_tensor(red, ab, -cw, red, ALU.mult, ALU.add)
                dve.drain()
            V.tensor_scalar(red, red, BELOW_PI, -BELOW_PI, ALU.min, ALU.max).then_inc(dve_misc, 1)
            ada(0, 0, 4)
            dve.wait_ge(misc_in, 16 * 10)
            lam = npar[:, 512:1024].rearrange("p (a d) -> p a d", a=4)
            for k in range(2):
                V.tensor_tensor(lam[:, 2 * k, :], lam[:, 2 * k, :], lam[:, 2 * k + 1, :], ALU.mult)
            dve.drain()
            V.tensor_reduce(small[:, 3:5], lam[:, 0::2, :], AX.X, ALU.add).then_inc(dve_misc, 1)
            dve.wait_ge(act_misc, 3)
            abre, abim, den, num, t0, t1 = cs, sn, coef_l[:, 0, 2, :], coef_l[:, 0, 3, :], coef_l[:, 0, 4, :], coef_l[:, 0, 5, :]
            cre, cim, ph = coef_l[:, 0, 6, :], coef_l[:, 0, 7, :], coef_l[:, 1, 0:6, :].rearrange("p (a b) s -> p a (b s)", a=3)
            V.tensor_tensor(abre, mag, cs, ALU.mult)
            V.tensor_tensor(abim, mag, sn, ALU.mult)
            V.tensor_tensor(den, lr, lr, ALU.mult)
            V.tensor_tensor(t0, li, li, ALU.mult)
            dve.drain()
            V.tensor_tensor(den, den, t0, ALU.add)
            V.tensor_scalar(num, abre, 1.0, None, ALU.subtract)
            dve.drain()
            V.reciprocal(den, den)
            V.tensor_tensor(cre, num, lr, ALU.mult)
            V.tensor_tensor(t0, abim, li, ALU.mult)
            V.tensor_tensor(cim, abim, lr, ALU.mult)
            V.tensor_tensor(t1, num, li, ALU.mult)
            dve.drain()
            V.tensor_tensor(cre, cre, t0, ALU.add)
            V.tensor_tensor(cim, cim, t1, ALU.subtract)
            dve.drain()
            V.tensor_tensor(cre, cre, den, ALU.mult)
            V.tensor_tensor(cim, cim, den, ALU.mult)
            V.tensor_scalar(red, red, 1 / (2 * PI), None, ALU.mult)
            dve.drain()
            V.tensor_scalar(ab, red, ROUND16, None, ALU.add)
            dve.drain()
            for half in range(2):
                V.tensor_scalar(ph[:, 0, ST * half:ST * (half + 1)], ab, ROUND16, None, ALU.subtract)
                V.tensor_copy(ph[:, 2, ST * half:ST * (half + 1)], mag)
            dve.drain()
            for half in range(2):
                last = V.tensor_tensor(ph[:, 1, ST * half:ST * (half + 1)], red, ph[:, 0, 0:ST], ALU.subtract)
            last.then_inc(dve_misc, 1)
            ada(0, 4, 8)
            dve.wait_ge(pe_misc, 1)
            by_pair = bank[1][:, 0:3 * G].rearrange("p (a g e) -> p a g e", a=3, e=2)
            for e in range(2):
                half = slice(ST * e, ST * (e + 1))
                V.tensor_copy(rot[half, :, :], by_pair[half, :, :, e])
            V.tensor_copy(hf[0:HEADS, 0, 1, :], bank[2][0:HEADS, 0:TOK])
            V.memset(hf[0:HEADS, 0, 2, :], NEG)
            dve.wait_ge(act_misc, 4)
            dve.drain()
            V.tensor_tensor(small[:, 5:6], small[:, 6:7], small[:, 5:6], ALU.subtract)
            dve.drain()
            V.tensor_scalar(small[:, 6:7], small[:, 5:6], LAM_INIT, None, ALU.subtract).then_inc(dve_misc, 1)

            def low(w, slot, hb):
                dve.wait_ge(h_done, w + 1)
                V.tensor_tensor(w_lo[:, hb, :, :], raw[:, slot, :, :], w_hi[:, hb, :, :].bitcast(F32),
                                ALU.subtract).then_inc(raw_used, 1)

            def split(src, k0, pe_count):
                if pe_count:
                    dve.wait_ge(pe_used, pe_count)
                V.tensor_copy(a_hi[:, k0:k0 + UT, :], src)
                dve.drain()
                V.tensor_tensor(a_lo[:, k0:k0 + UT, :], src, a_hi[:, k0:k0 + UT, :].bitcast(F32),
                                ALU.subtract).then_inc(stat_ready, 1)

            def ut_copy(b):
                dve.wait_ge(ut_pe, b + 1)
                for k in range(2):
                    last = V.tensor_copy(feat[:, 4 * b + 2 * k:4 * b + 2 * k + 2, :].rearrange("p k t -> p (k t)"),
                                         bank[6 + k][:, :])
                last.then_inc(ut_done, 1)

            def columns(c):
                dve.wait_ge(ada_mm, 2 * c + 2)
                if c:
                    dve.wait_ge(hf_ready, 2 * c)
                at8 = slice(8 * c, 8 * c + 8)
                V.tensor_tensor(sh8[:, :], bank[7][:, 0:8], ba_sb[:, 0, at8], ALU.add)
                V.tensor_tensor(sc8[:, :], bank[7][:, 8:16], ba_sb[:, 1, at8], ALU.add)
                dve.drain()
                V.scalar_tensor_tensor(sc8[:, :], sc8[:, :], 1.0, g_sb[:, at8], ALU.add,
                                       ALU.mult).then_inc(mod_ready, 1)

            def group(g):
                dve.wait_ge(hf_ready, g + 1)
                split(hf[:, g % 2, :, :], UT * g, 0)

            def turn_low(c, v):
                w = TURN_W[c] + v
                low(w, ring_of(w) % RING, w % 2)

            ada(0, 8, 2 * ADA_UNITS)
            for c in range(1, NC0):
                ada(c, 0, 1)
                columns(c - 1)
                ada(c, 1, 3)
                group(2 * c - 2)
                done = 3
                for v, a in enumerate(TURN_AT[c - 1]):
                    ada(c, done, a + 1)
                    turn_low(c - 1, v)
                    done = a + 1
                    if v == BLK_0 - 1:
                        group(2 * c - 1)
                ada(c, done, 2 * ADA_UNITS)
            columns(NC0 - 1)
            for gi in range(2):
                group(2 * NC0 - 2 + gi)
                for v in range(BLK_0 * gi, BLK_0 * (gi + 1)):
                    turn_low(NC0 - 1, v)

            for u in range(UPB):
                low(W_A3 + u, u % RING, u % 2)
                if u in (3, 5, 7):
                    ut_copy((u - 3) // 2)

            def scan_pair(s, buf, first):
                dve.wait_ge(trig_ready, s + 1)
                dve.wait_ge(x_pe, s + 1)
                bx = bank[4 + buf][:, :].rearrange("p (a t) -> p a t", a=2)
                cos2 = cosb[:, buf, :].unsqueeze(1).to_broadcast([P, 2, TOK])
                sin2 = sinb[:, buf, :].unsqueeze(1).to_broadcast([P, 2, TOK])
                V.tensor_tensor(T1, bx, cos2, ALU.mult)
                V.tensor_tensor(T2, bx, sin2, ALU.mult).then_inc(x_used, 1)
                dve.drain()
                V.tensor_tensor(T1[:, 0, :], T1[:, 0, :], T2[:, 1, :], ALU.add)
                V.tensor_tensor(T1[:, 1, :], T1[:, 1, :], T2[:, 0, :], ALU.subtract)
                dve.drain()
                r = rot[:, 2, bass.ds(s, 1)] if not isinstance(s, int) else rot[:, 2, s:s + 1]
                for a in range(2):
                    V.tensor_tensor_scan(HH[:, a, :], r.to_broadcast([P, TOK]), T1[:, a, :], 0.0,
                                         ALU.mult, ALU.add)
                dve.drain()
                if not first:
                    dve.wait_ge(y_pe, s - 1)
                V.tensor_tensor(hcb[:, buf, :, :], HH, cos2, ALU.mult)
                V.tensor_tensor(hsb[:, buf, :, :], HH, sin2, ALU.mult).then_inc(hcs_ready, 1)

            def y_evac(sup):
                dve.wait_ge(y_pe, sup * 4 + 4)
                if isinstance(sup, int):
                    f, dd = feat[:, sup:sup + 1, :].rearrange("p k t -> p (k t)"), dcol[:, sup:sup + 1]
                else:
                    f, dd = feat[:, bass.ds(sup, 1), :].rearrange("p k t -> p (k t)"), dcol[:, bass.ds(sup, 1)]
                V.scalar_tensor_tensor(gl[:, 2, :], f, dd, bank[6][:, 0:TOK], ALU.mult, ALU.add).then_inc(y_used, 1)
                dve.drain()
                V.tensor_tensor(gl[:, 0, :], gl[:, 2, :], gl[:, 2, :], ALU.mult)
                dve.drain()
                V.tensor_scalar(gl[:, 0, :], gl[:, 0, :], 0.044715, 1.0, ALU.mult, ALU.add)
                dve.drain()
                V.tensor_tensor(gl[:, 0, :], gl[:, 0, :], gl[:, 2, :], ALU.mult).then_inc(tanh_in, 1)

            def y_gelu(sup):
                dve.wait_ge(tanh_out, sup + 1)
                f = (feat[:, sup:sup + 1, :] if isinstance(sup, int) else feat[:, bass.ds(sup, 1), :]
                     ).rearrange("p k t -> p (k t)")
                V.scalar_tensor_tensor(gl[:, 0, :], gl[:, 1, :], 1.0, gl[:, 2, :], ALU.add, ALU.mult)
                dve.drain()
                V.tensor_scalar(f, gl[:, 0, :], 0.5, None, ALU.mult).then_inc(gelu_done, 1)
                dve.drain()

            def dve_b(i, first):
                for v in range(2 * UPB):
                    low(i * 16 + (W_B + v), v % RING, v % 2)
                    if first and v == 3:
                        ut_copy(3)
                    if v % 2:
                        j = v // 2
                        if not (first and j == 0):
                            scan_pair(i * 8 + (j - 1), (j - 1) % 2, first and j <= 2)
                        if j == 5:
                            y_evac(i * 2)
                        if j == 6:
                            y_gelu(i * 2)
                        if j == 1 and not first:
                            y_evac(i * 2 - 1)
                        if j == 2 and not first:
                            y_gelu(i * 2 - 1)

            dve_b(0, True)
            with dve.Fori(1, 8) as i:
                dve_b(i, False)
            for n in range(len(LATE)):
                low(W_B2 + n, n % RING, n % 2)
                if n == 1:
                    scan_pair(63, 1, False)
                if n == 3:
                    y_evac(15)
                if n == 6:
                    y_gelu(15)

            with dve.Fori(0, HEADS // 2) as cb:
                for rr in range(2):
                    h1 = cb * 2 + (rr + 1)
                    for v in range(2 * UPB):
                        loc = 24 * rr + v + (v + 1) // 2
                        low(cb * 32 + (W_C + 16 * rr + v), loc % RING, v % 2)
                        if v % 2 == 0:
                            first = rr == 0 and v == 0
                            rl = R0 + W_C + loc + 1
                            ada_unit(rl % RING, cb * (48 * 4) + 16 * (rl // RING + 1), gacc,
                                     2 * (8 * rr + v // 2), first)
                            if rr == 1 and v == 14:
                                dve.drain().then_inc(gacc_ready, 1)
                        if v == 5:
                            dve.wait_ge(s_pe, h1)
                            dve.wait_ge(ba_in, h1 * 32 + 16)
                            for qb in range(2):
                                V.tensor_tensor(sc[:, qb, :, :], bank[6 + qb][:, :].rearrange("p (m k) -> p m k", m=2),
                                                bias_in[:, qb:qb + 1, :].to_broadcast([P, 2, TOK]), ALU.add)
                            dve.drain()
                            V.tensor_reduce(small[:, 16:20], sc.rearrange("p q m k -> p (q m) k"), AX.X, ALU.max)
                            dve.drain()
                            V.tensor_scalar(small[:, 16:20], small[:, 16:20], -1.0, None, ALU.mult).then_inc(s_max, 1)
                        if v == 7:
                            dve.wait_ge(p_exp, h1)
                            V.reciprocal(small[:, 24:28], small[:, 20:24])
                            dve.drain()
                            for qb in range(2):
                                k = 25 + 2 * qb
                                V.tensor_tensor(small[:, k:k + 1], small[:, k:k + 1], small[:, 6:7], ALU.mult)
                            dve.drain()
                            for qb in range(2):
                                V.tensor_scalar(sc[:, qb, 0, :], sc[:, qb, 0, :], small[:, 24 + 2 * qb:25 + 2 * qb],
                                                None, ALU.mult)
                            dve.drain()
                            for qb in range(2):
                                last = V.scalar_tensor_tensor(at[:, qb, :], sc[:, qb, 1, :],
                                                              small[:, 25 + 2 * qb:26 + 2 * qb], sc[:, qb, 0, :],
                                                              ALU.mult, ALU.add)
                            last.then_inc(at_sb, 1)
                        if v == 13:
                            dve.wait_ge(o_ssq, h1)
                            V.reciprocal(small[:, 36:38], small[:, 30:32])
                            V.tensor_tensor(szA, szA, za_in, ALU.mult)
                            dve.drain()
                            V.tensor_scalar(small[:, 36:38], small[:, 36:38], 1.0 - LAM_INIT, None, ALU.mult)
                            V.tensor_tensor(szA, szA, subg.unsqueeze(1).to_broadcast([P, 2, TOK]), ALU.mult)
                            dve.drain()
                            for qb in range(2):
                                last = V.scalar_tensor_tensor(ya[:, qb, :], bank[6 + qb][:, 0:TOK],
                                                              small[:, 36 + qb:37 + qb], szA[:, qb, :],
                                                              ALU.mult, ALU.mult)
                            last.then_inc(ya_sb, 1)
                dve.wait_ge(gate_pe, cb + 1)
                dve.wait_ge(bg_in, cb * 16 + 16)
                for k in range(2):
                    g_row = grow[0:1, CB * k:CB * (k + 1)]
                    last = V.tensor_tensor(g_row, g_row, bank[(4, 7)[k]][0:1, :], ALU.add)
                last.then_inc(gate_row, 1)

            def ys_prev(j):
                dve.wait_ge(sig_done, j + 1)
                dve.wait_ge(gt_pe, j + 1)
                if j:
                    dve.wait_ge(ys_pe, j)
                else:
                    dve.wait_ge(gate_st, 16 * 4)
                V.tensor_tensor(ys, zs, sz, ALU.mult)
                for hh in range(NH):
                    V.tensor_tensor(sig[:, hh, :], bank[4 + hh][:, :], sig[:, hh, :], ALU.mult)
                dve.drain()
                V.tensor_tensor(ys, ys, sig, ALU.mult).then_inc(ys_sb, 1)

            for j in range(4):
                for u in range(UT):
                    w = W_D + UT * j + u
                    if j == 0:
                        split(feat[:, UT * u:UT * (u + 1), :], UT * u, W_D - UPB + u + 1)
                    low(w, w % RING, w % 2)
                    if u == 1 and j:
                        ys_prev(j - 1)

            def merge_prev(j):
                dve.wait_ge(pe_used, W_E + UPB * (j + 1))
                dve.wait_ge(gs_sig, j + 1)
                if j:
                    dve.wait_ge(m_pe, j)
                for hh in range(NH):
                    last = V.tensor_tensor(mrg[:, hh, :], bank[2 + hh][:, :], gs[:, hh, :], ALU.mult)
                last.then_inc(acc_free_v, 1)
                dve.drain()
                V.tensor_tensor(mrg, mrg, part, ALU.add).then_inc(m_sb, 1)
                dve.drain()

            for j in range(8):
                for u in range(UPB):
                    w = W_E + UPB * j + u
                    if j == 0 and u < UT:
                        split(feat[:, 16 + UT * u:16 + UT * (u + 1), :], UT * u, W_E - UT + u + 1)
                    elif j == 0:
                        k = u - UT
                        dve.wait_ge(feat_sb, k + 1)
                        split(ysT[:, UT * k:UT * (k + 1), :], 16 + UT * k, 0)
                    low(w, w % RING, w % 2)
                    if u == 1:
                        if j == 0:
                            ys_prev(3)
                        else:
                            merge_prev(j - 1)
                    if u == 5:
                        dve.wait_ge(pe_used, W_E + UPB * j + UT)
                        dve.wait_ge(ga_sig, j + 1)
                        for hh in range(NH):
                            last = V.tensor_tensor(part[:, hh, :], bank[hh][:, :], ga[:, hh, :], ALU.mult)
                        last.then_inc(acc_free_v, 1)
                        dve.drain().then_inc(ga_used, 1)

            def out_prev(j):
                dve.wait_ge(pe_used, W_F + UPB * (j + 1))
                dve.wait_ge(xg_in[j % 2], 32 * (j // 2 + 1))
                o = [obuf[:, hh, CB * j:CB * (j + 1)] for hh in range(NH)]
                for hh in range(NH):
                    last = V.tensor_tensor(o[hh], bank[2 * (j % 2) + hh][:, :], gate_b[:, j % 2, :], ALU.mult)
                last.then_inc(acc_free_v, 1)
                dve.drain()
                for hh in range(NH):
                    last = V.tensor_tensor(o[hh], o[hh], xb[:, j % 2, hh, :], ALU.add)
                last.then_inc(o_sb, 1)

            for j in range(8):
                for u in range(UPB):
                    w = W_F + UPB * j + u
                    if j == 0:
                        dve.wait_ge(feat_sb, 4 + u + 1)
                        split(feat[:, UT * u:UT * (u + 1), :], UT * u, W_F - UPB + u + 1)
                    low(w, w % RING, w % 2)
                    if u == 1:
                        if j == 0:
                            merge_prev(7)
                        else:
                            out_prev(j - 1)
            out_prev(7)
            dve.wait_ge(o_sq, 8)
            V.tensor_reduce(small[:, 32:34], small[:, 40:56].rearrange("p (h j) -> p h j", h=2), AX.X,
                            ALU.add).then_inc(f_rms, 1)
            dve.wait_ge(f_rstd, 1)
            V.reciprocal(small[:, 36:38], small[:, 34:36])
            dve.drain()
            dve.wait_ge(fg_in, 16)
            for j in range(8):
                for hh in range(NH):
                    o = obuf[:, hh, CB * j:CB * (j + 1)]
                    last = V.scalar_tensor_tensor(o, o, small[:, 36 + hh:37 + hh], fg[:, CB * j:CB * (j + 1)],
                                                  ALU.mult, ALU.mult)
                last.then_inc(f_out, 1)

        @block.tensor
        def _(pe):
            T = nc.tensor

            pe.wait_ge(cons_in, 16 * 5)
            pe.wait_ge(dve_misc, 4)
            ph = coef_l[:, 1, 0:6, :].rearrange("p (a b) s -> p a (b s)", a=3)
            for k in range(3):
                T.transpose(bank[1][:, G * k:G * (k + 1)], ph[:, k, :], ident[:, :])
            pe.wait_ge(misc_in, 16 * 10)
            T.matmul(bank[2][0:HEADS, 0:TOK], hf[0:32, 1, 0, 0:HEADS],
                     hf[0:32, 0, 0, :], start=True, stop=True).then_inc(pe_misc, 1)
            def unit(w, ring, hb, k0, pair, first, last, stat):
                pe.wait_ge(raw_used, ring + (RING + 1))
                if stat:
                    pe.wait_ge(stat_ready, stat)
                for t in range(UT):
                    for hh in range(NH):
                        acc = bank[2 * pair + hh][:, :]
                        cols = slice(P * hh, P * (hh + 1))
                        s_hi, s_lo = a_hi[:, k0 + t, cols], a_lo[:, k0 + t, cols]
                        T.matmul(acc, s_hi, w_hi[:, hb, t, :], start=first and t == 0, stop=False)
                        T.matmul(acc, s_hi, w_lo[:, hb, t, :], start=False, stop=False)
                        ins = T.matmul(acc, s_lo, w_hi[:, hb, t, :], start=False, stop=last and t == UT - 1)
                ins.then_inc(pe_used, 1)

            def acc_wait(a):
                if not (isinstance(a, int) and a < 2):
                    pe.wait_ge(acc_free_a, a - 1)

            def xt(g):
                if g:
                    pe.wait_ge(hf_ready, g)
                for t in range(UT):
                    kt = UT * g + t
                    for h in range(NH):
                        o = TOK * (t % 2) + P * h
                        last = T.transpose(bank[6 + t // 2][:, o:o + P], xs[:, h, P * kt:P * (kt + 1)], ident[:, :])
                last.then_inc(xt_pe, 1)

            def ut(b):
                pe.wait_ge(acc_free_a, b + 1)
                if b:
                    pe.wait_ge(ut_done, b)
                for t in range(UT):
                    for h in range(NH):
                        o = TOK * (t % 2) + P * h
                        last = T.transpose(bank[6 + t // 2][:, o:o + P], stage[:, b % 2, h, P * t:P * (t + 1)], ident[:, :])
                last.then_inc(ut_pe, 1)

            EARLY_END = {c + 1: EARLY[c][-1] - 19 for c in EARLY}
            for c in range(NC0):
                if c:
                    pe.wait_ge(hf_ready, 2 * c)
                if c in EARLY_END:
                    pe.wait_ge(early_free, EARLY_END[c])
                for n in range(2):
                    pe.wait_ge(acc_ready, 2 * c + n + 1)
                    for k in range(ADA_CB // P):
                        last = T.matmul(bank[7][:, 8 * n + k:8 * n + k + 1], adacc[:, n, P * k:P * (k + 1)],
                                        ones[:, 0:1], start=True, stop=True)
                    last.then_inc(ada_mm, 1)
                pe.wait_ge(x_scaled, 1)
                pe.wait_ge(mod_ready, c + 1)
                for v in range(CH_W):
                    g, w = 2 * c + v // BLK_0, TURN_W[c] + v
                    if v == 0:
                        xt(g)
                    if v == 1:
                        xt(g + 1)
                    unit(w, ring_of(w), w % 2, UT * g, v % BLK_0, g == 0, g == UPB - 1, g + 1)
                for v in range(CH_W, len(TURN[c])):
                    w, (b, k) = TURN_W[c] + v, TURN[c][v]
                    if k == 0 and b > EARLY[c][0]:
                        pe.wait_ge(early_free, b - 20)
                    elif k == 0:
                        pe.wait_ge(hf_ready, 2 * c + 2)
                    unit(w, ring_of(w), w % 2, UT * k, 3, k == 0, k == EARLY_OF[b] - 1, 0)

            acc_wait(BLK_0)
            for u in range(UPB):
                w = W_A3 + u
                unit(w, ring_of(w), w % 2, UT * u, BLK_0 % 2, u == 0, u == UPB - 1, 0)
                if u in (1, 3, 5):
                    ut((u - 1) // 2)

            def x_mm(s, sup, j, first):
                buf = j % 2
                pe.wait_ge(bd_ready, s + 1)
                if not (first and j < 2):
                    pe.wait_ge(x_used, s - 1)
                u_t = (feat[:, bass.ds(sup, 1), :] if not isinstance(sup, int)
                       else feat[:, sup:sup + 1, :]).rearrange("p k t -> p (k t)")
                for k in range(2):
                    last = T.matmul(bank[4 + buf][:, TOK * k:TOK * (k + 1)],
                                    bd[:, buf, k, :, :].rearrange("p a s -> p (a s)"), u_t,
                                    start=True, stop=True)
                last.then_inc(x_pe, 1)

            def y_mm(s, q, buf, sup_wait):
                pe.wait_ge(hcs_ready, s + 1)
                pe.wait_ge(cst_ready, s + 1)
                if sup_wait is not None:
                    pe.wait_ge(y_used, sup_wait)
                for k, (m, hb, a) in enumerate(((0, hcb, 0), (3, hcb, 1), (3, hsb, 0), (2, hsb, 1))):
                    last = T.matmul(bank[6][32 * q:32 * q + 32, 0:TOK], cst[:, q, m, :], hb[:, buf, a, :],
                                    start=k == 0, stop=k == 3)
                last.then_inc(y_pe, 1)

            def pe_b(i, first):
                for v in range(2 * UPB):
                    bl, u = v // UPB, v % UPB
                    if u == 0:
                        acc_wait(i * 2 + (BLK_A + bl))
                    w = i * 16 + (W_B + v)
                    unit(w, w + R0, v % 2, UT * u, bl, u == 0, u == UPB - 1, 0)
                    j = v // 2
                    if first and v == 2:
                        ut(3)
                    if v % 2 == 0:
                        if first and j == 4:
                            pe.wait_ge(ut_done, 4)
                        x_mm(i * 8 + j, i * 2 + j // 4, j, first)
                    elif not (first and j == 0):
                        if first and j == 1:
                            pe.wait_ge(ut_done, 4)
                        wait = None
                        if j == 5:
                            wait = i * 2 + 1
                        if j == 1 and not first:
                            wait = i * 2
                        y_mm(i * 8 + (j - 1), (j - 1) % 4, (j - 1) % 2, wait)

            pe_b(0, True)
            with pe.Fori(1, 8) as i:
                pe_b(i, False)
            for n, (b, u) in enumerate(LATE):
                w, k = W_B2 + n, b - 20
                if n == LATE_AT[k]:
                    acc_wait(b)
                    pe.wait_ge(early_in[k % 2], 16 * (k // 2 + 1))
                    for hh in range(NH):
                        T.matmul(bank[2 * (b % 2) + hh][:, :], ident[:, :], early[k % 2][:, hh, :],
                                 start=True, stop=False)
                unit(w, w + R0, n % 2, UT * u, b % 2, False, u == UPB - 1, 0)
                if n == 1:
                    y_mm(63, 3, 1, None)

            with pe.Fori(0, HEADS // 2) as cb:
                for rr in range(2):
                    h1 = cb * 2 + (rr + 1)
                    for v in range(2 * UPB):
                        bl, u = v // UPB, v % UPB
                        loc = 24 * rr + v + (v + 1) // 2
                        if u == 0:
                            acc_wait(cb * 4 + (24 + 2 * rr + bl))
                        unit(None, cb * 48 + (R0 + W_C + loc), v % 2, UT * u, bl, u == 0, u == UPB - 1, 0)
                        if v == 0:
                            pe.wait_ge(qk_in, h1 * 32)
                            for src, pb in ((q_in, bank[4]), (k_in, bank[5])):
                                for m in range(2):
                                    for h in range(NH):
                                        last = T.transpose(pb[:, TOK * m + P * h:TOK * m + P * (h + 1)],
                                                           src[:, h, P * m:P * (m + 1)], ident[:, :])
                            last.then_inc(qk_pe, 1)
                        if v == 3:
                            pe.wait_ge(qk_sb, h1)
                            for qb in range(2):
                                for m in range(2):
                                    last = T.matmul(bank[6 + qb][:, TOK * m:TOK * (m + 1)],
                                                    qT[:, m, P * qb:P * (qb + 1)], kT[:, m, :], start=True, stop=True)
                            last.then_inc(s_pe, 1)
                        if v == 8:
                            pe.wait_ge(at_sb, h1)
                            for kk in range(2):
                                for qb in range(2):
                                    last = T.transpose(bank[4][:, TOK * kk + P * qb:TOK * kk + P * (qb + 1)],
                                                       at[:, qb, P * kk:P * (kk + 1)], ident[:, :])
                            last.then_inc(at_pe, 1)
                        if v == 10:
                            pe.wait_ge(at_t, h1)
                            pe.wait_ge(va_in, h1 * 16)
                            for qb in range(2):
                                for kk in range(2):
                                    last = T.matmul(bank[6 + qb][:, 0:TOK], aT[:, kk, P * qb:P * (qb + 1)],
                                                    v_in[:, kk, :], start=kk == 0, stop=kk == 1)
                            last.then_inc(o_pe, 1)
                        if v == 13:
                            pe.wait_ge(ya_sb, h1)
                            for ct in range(2):
                                for h in range(NH):
                                    last = T.transpose(bank[5][:, TOK * ct + P * h:TOK * ct + P * (h + 1)],
                                                       ya[:, h, P * ct:P * (ct + 1)], ident[:, :])
                            last.then_inc(ya_pe, 1)
                        if rr == 1 and v == 14:
                            pe.wait_ge(gacc_ready, cb + 1)
                            for k in range(2):
                                last = T.matmul(bank[(4, 7)[k]][0:1, :], ones[:, 0:1], gacc[:, CB * k:CB * (k + 1)],
                                                start=True, stop=True)
                            last.then_inc(gate_pe, 1)

            def ysT_t(j):
                pe.wait_ge(ys_sb, j + 1)
                if j:
                    pe.wait_ge(feat_sb, j)
                for t in range(UT):
                    for h in range(NH):
                        o = TOK * (t % 2) + P * h
                        last = T.transpose(bank[6 + t // 2][:, o:o + P], ys[:, h, P * t:P * (t + 1)], ident[:, :])
                last.then_inc(ys_pe, 1)

            for j in range(4):
                acc_wait(40 + j)
                for u in range(UT):
                    w = W_D + UT * j + u
                    unit(w, ring_of(w), u % 2, UT * u, j % 2, u == 0, u == UT - 1, 8 + u + 1 if j == 0 else 0)
                    if u == 2 and j:
                        ysT_t(j - 1)
                    if u == 3:
                        if j == 0:
                            pe.wait_ge(yaT_sb, HEADS)
                            pe.wait_ge(gate_row, 4)
                        else:
                            pe.wait_ge(ys_sb, j)
                        for h in range(NH):
                            for t in range(UT):
                                last = T.transpose(bank[4 + h][:, P * t:P * (t + 1)],
                                                   feat[:, 4 * j + t, P * h:P * (h + 1)], ident[:, :])
                        last.then_inc(gt_pe, 1)

            def mT_t(j):
                pe.wait_ge(m_sb, j + 1)
                pe.wait_ge(feat_sb, j + 4)
                for t in range(UT):
                    for h in range(NH):
                        o = TOK * (t % 2) + P * h
                        last = T.transpose(bank[4 + t // 2][:, o:o + P], mrg[:, h, P * t:P * (t + 1)], ident[:, :])
                last.then_inc(m_pe, 1)

            def pe_e(j):
                for u in range(UPB):
                    if u % UT == 0:
                        if isinstance(j, int):
                            acc_wait(44 + u // UT)
                        else:
                            pe.wait_ge(acc_free_v, j * 2 + (u // UT - 1))
                    unit(None, j * UPB + (ring_of(W_E) + u), u % 2, UT * u, u // UT, u % UT == 0, u % UT == UT - 1,
                         12 + u + 1 if isinstance(j, int) else 0)
                    if u == 2:
                        if isinstance(j, int):
                            ysT_t(3)
                        else:
                            mT_t(j - 1)

            pe_e(0)
            with pe.Fori(1, 8) as j:
                pe_e(j)

            def pe_f(j, par, first):
                pe.wait_ge(acc_free_v, j + 15)
                for u in range(UPB):
                    unit(None, j * UPB + (ring_of(W_F) + u), u % 2, UT * u, par, u == 0, u == UPB - 1,
                         20 + u + 1 if first else 0)
                    if u == 2 and first:
                        mT_t(7)

            pe_f(0, 0, True)
            pe_f(1, 1, False)
            with pe.Fori(1, 4) as i:
                for par in range(2):
                    pe_f(i * 2 + par, par, False)


def kernel(**inputs):
    import numpy as np
    import concourse.bacc as bacc
    from concourse.bass_utils import run_bass_kernel_spmd

    f = {k: np.asarray(v) for k, v in inputs.items()}
    nc = bacc.Bacc("TRN2", target_bir_lowering=False, num_devices=1)
    arrays = {}

    def give(name, a):
        name = "in_" + name
        a = np.ascontiguousarray(a)
        arrays[name] = a
        return nc.dram_tensor(name, a.shape, mybir.dt.from_np(a.dtype), kind="ExternalInput").ap()

    cm = np.zeros((G // 2, 2, ST, 2, 2 * GC), f["ssm_c_re"].dtype)
    for gg in range(2):
        for k, cc in enumerate((f["ssm_c_re"][0], f["ssm_c_im"][0])):
            cm[:, gg, :, k, GC * gg:GC * (gg + 1)] = cc[gg::2].transpose(0, 2, 1)
    dist = np.arange(TOK)
    nf = np.maximum(dist, 1).astype(np.float32)
    large = 16 + (np.log(nf / np.float32(16)) / np.float32(math.log(8)) * np.float32(16)).astype(np.int32)
    bucket = np.where(dist < 16, dist, np.minimum(large, 31))[::-1]
    onehot = (np.arange(32)[:, None] == bucket[None, :]).astype(np.float32)
    gmask = (np.arange(P)[:, None] // GC == np.arange(8)[None, :]).astype(np.float32)

    def b_layout(b):
        return b.reshape(16, 8, ST, GC).transpose(1, 3, 0, 2).reshape(P, 16, ST)

    args = [
        give("x", f["x"][0]), give("c_col", f["c"].reshape(KT, P).T), give("g_col", f["norm_g"].reshape(KT, P).T),
        give("w_ada", f["w_ada"][0]), give("bada_col", f["b_ada"].reshape(3 * KT, P).T),
        give("bada_gate", f["b_ada"][:, 2 * D:]), give("w_in", f["w_in"][0]),
        give("lam_re", f["ssm_lambda_re"][0]), give("lam_im", f["ssm_lambda_im"][0]),
        give("log_dt", f["ssm_log_dt"].reshape(G, 1)),
        give("b_re", b_layout(f["ssm_b_re"][0])), give("b_im", b_layout(f["ssm_b_im"][0])),
        give("c_map", cm.reshape(G // 2, P, 2 * 2 * GC)), give("d_col", f["ssm_d"].reshape(16, P).T),
        give("w_glu", f["w_glu"][0]),
        give("lambdas", np.concatenate([f[k] for k in ("lambda_q1", "lambda_k1", "lambda_q2", "lambda_k2")], 1)),
        give("subln_g", f["subln_g"]), give("w_oss", f["w_out_ssm"][0]), give("w_oat", f["w_out_attn"][0]),
        give("w_o", f["w_o"][0]), give("rel_bias", f["rel_bias"]), give("final_g", f["final_g"].reshape(1, D)),
        give("onehot", onehot), give("ident", np.eye(P, dtype=np.float32)),
        give("tvals", np.arange(TOK, dtype=np.float32).reshape(1, TOK)), give("gmask", gmask),
    ]
    out = nc.dram_tensor("out", (TOK, D), F32, kind="ExternalOutput").ap()
    build(nc, *args, out)
    r = run_bass_kernel_spmd(nc, [arrays], core_ids=[0])
    return r.results[0]["out"].reshape(1, TOK, D)
```
